# Optimizing a Trainium2 kernel written in Bass

```python
import jax, jax.numpy as jnp
from jax import lax
import numpy as np

D_MODEL = 1024
BATCH = 1
SEQ = 2048
DEPTH = 2

N_MIXERS = 2
N_META = 16
BLOCK = 128
N_PAD = BLOCK - N_META
RMS_EPS = 1e-6

A_HEADS = 16
A_KV_HEADS = 2
A_HEAD_DIM = 64
A_GROUP = A_HEADS // A_KV_HEADS
A_WIDTH = A_HEADS * A_HEAD_DIM
A_KV_WIDTH = A_KV_HEADS * A_HEAD_DIM
A_IN = 2 * A_WIDTH + 2 * A_KV_WIDTH
WINDOW = 128
ROPE_THETA = 10000.0

B_HEADS = 8
B_QK_DIM = 64
B_V_DIM = 128
B_QK_WIDTH = B_HEADS * B_QK_DIM
B_WIDTH = B_HEADS * B_V_DIM
B_IN = 2 * B_QK_WIDTH + 3 * B_WIDTH + 2 * B_HEADS

N_LAYERS_A = (DEPTH + 1) // 2
N_LAYERS_B = DEPTH // 2

kernel_name = "hybrid_swa_sink_mlstm_interleaved"

def rmsnorm(x, g):
    xf = x.astype(jnp.float32)
    y = xf * lax.rsqrt(jnp.mean(xf * xf, axis=-1, keepdims=True) + RMS_EPS)
    return (y * g.astype(jnp.float32)).astype(x.dtype)

def rope(t, pos):
    half = t.shape[-1] // 2
    inv = ROPE_THETA ** (-jnp.arange(half, dtype=jnp.float32) / half)
    ang = pos.astype(jnp.float32)[:, None] * inv[None, :]
    cos = jnp.cos(ang)[None, :, None, :]
    sin = jnp.sin(ang)[None, :, None, :]
    t1 = t[..., :half].astype(jnp.float32)
    t2 = t[..., half:].astype(jnp.float32)
    out = jnp.concatenate([t1 * cos - t2 * sin, t2 * cos + t1 * sin], axis=-1)
    return out.astype(t.dtype)

def swa_sink_mixer(u, w_in, sinks, pos, valid):
    bsz, L, _ = u.shape
    nb = L // BLOCK
    proj = u @ w_in
    q, k, v, z = jnp.split(proj, [A_WIDTH, A_WIDTH + A_KV_WIDTH, A_WIDTH + 2 * A_KV_WIDTH], axis=-1)
    q = rope(q.reshape(bsz, L, A_HEADS, A_HEAD_DIM), pos)
    k = rope(k.reshape(bsz, L, A_KV_HEADS, A_HEAD_DIM), pos)
    v = v.reshape(bsz, L, A_KV_HEADS, A_HEAD_DIM)
    qb = q.reshape(bsz, nb, BLOCK, A_KV_HEADS, A_GROUP, A_HEAD_DIM)

    def with_prev(t):
        tb = t.reshape(bsz, nb, BLOCK, A_KV_HEADS, A_HEAD_DIM)
        prev = jnp.pad(tb[:, :-1], ((0, 0), (1, 0), (0, 0), (0, 0), (0, 0)))
        return jnp.concatenate([prev, tb], axis=2)

    kb, vb = with_prev(k), with_prev(v)
    s = jnp.einsum('bntkgd,bnskd->bnkgts', qb, kb,
                   preferred_element_type=jnp.float32) * (A_HEAD_DIM ** -0.5)

    dist = (jnp.arange(BLOCK)[:, None] + BLOCK) - jnp.arange(2 * BLOCK)[None, :]
    band = (dist >= 0) & (dist < WINDOW)
    vblk = valid.reshape(nb, BLOCK)
    vprev = jnp.concatenate([jnp.zeros((1, BLOCK), dtype=bool), vblk[:-1]], axis=0)
    key_valid = jnp.concatenate([vprev, vblk], axis=-1)
    mask = band[None] & key_valid[:, None, :]
    s = jnp.where(mask[None, :, None, None], s, -jnp.inf)

    sink = sinks.astype(jnp.float32).reshape(A_KV_HEADS, A_GROUP)[None, None, :, :, None, None]
    m = jnp.maximum(s.max(axis=-1, keepdims=True), sink)
    p = jnp.exp(s - m)
    p = p / (p.sum(axis=-1, keepdims=True) + jnp.exp(sink - m))
    o = jnp.einsum('bnkgts,bnskd->bntkgd', p.astype(vb.dtype), vb)
    o = o.reshape(bsz, L, A_WIDTH)
    return o * jax.nn.silu(z)

def mlstm_mixer(u, w_in, b_gates, valid):
    f32 = jnp.float32
    bsz, L, _ = u.shape
    nc = L // BLOCK
    proj = u @ w_in
    cuts = np.cumsum([B_QK_WIDTH, B_QK_WIDTH, B_WIDTH, B_WIDTH, B_WIDTH]).tolist()
    q, k, v, o_pre, z, gates = jnp.split(proj, cuts, axis=-1)
    gates = gates.astype(f32) + b_gates.astype(f32)
    vmask = valid[None, :, None]
    log_f = jnp.where(vmask, jax.nn.log_sigmoid(gates[..., B_HEADS:]), 0.0)
    i_log = jnp.where(vmask, gates[..., :B_HEADS], -jnp.inf)

    def chunk_gate(g):
        return g.reshape(bsz, nc, BLOCK, B_HEADS).transpose(0, 3, 1, 2)

    def heads(t, d):
        return t.reshape(bsz, nc, BLOCK, B_HEADS, d).transpose(0, 3, 1, 2, 4).astype(f32)

    log_f, i_log = chunk_gate(log_f), chunk_gate(i_log)
    qh = heads(q, B_QK_DIM)
    kh = heads(k, B_QK_DIM) * (B_QK_DIM ** -0.5)
    vh = heads(v, B_V_DIM)

    b = jnp.cumsum(log_f, axis=-1)
    g = b[..., -1]

    a = g[..., None] - b + i_log
    m_loc = a.max(axis=-1)
    w = jnp.exp(a - m_loc[..., None])
    c_chunk = jnp.einsum('bhnt,bhntk,bhntv->bhnkv', w, kh, vh)
    n_chunk = jnp.einsum('bhnt,bhntk->bhnk', w, kh)

    def step(carry, xs):
        c, n, m = carry
        cc, ncv, mc, gc = xs
        m_new = jnp.maximum(gc + m, mc)
        dec = jnp.exp(gc + m - m_new)
        inj = jnp.exp(mc - m_new)
        c_new = dec[..., None, None] * c + inj[..., None, None] * cc
        n_new = dec[..., None] * n + inj[..., None] * ncv
        return (c_new, n_new, m_new), (c, n, m)

    init = (jnp.zeros((bsz, B_HEADS, B_QK_DIM, B_V_DIM), f32),
            jnp.zeros((bsz, B_HEADS, B_QK_DIM), f32),
            jnp.zeros((bsz, B_HEADS), f32))
    xs = (jnp.moveaxis(c_chunk, 2, 0), jnp.moveaxis(n_chunk, 2, 0),
          jnp.moveaxis(m_loc, 2, 0), jnp.moveaxis(g, 2, 0))
    _, (c_prev, n_prev, m_prev) = lax.scan(step, init, xs)
    c_prev = jnp.moveaxis(c_prev, 0, 2)
    n_prev = jnp.moveaxis(n_prev, 0, 2)
    m_prev = jnp.moveaxis(m_prev, 0, 2)

    causal = jnp.tril(jnp.ones((BLOCK, BLOCK), dtype=bool))
    dlog = jnp.where(causal, b[..., :, None] - b[..., None, :] + i_log[..., None, :], -jnp.inf)
    inter = b + m_prev[..., None]
    m_t = jnp.maximum(inter, dlog.max(axis=-1))
    inter_w = jnp.exp(inter - m_t)
    attn = jnp.exp(dlog - m_t[..., None]) * jnp.einsum('bhntk,bhnsk->bhnts', qh, kh)
    num = (inter_w[..., None] * jnp.einsum('bhntk,bhnkv->bhntv', qh, c_prev)
           + jnp.einsum('bhnts,bhnsv->bhntv', attn, vh))
    den = inter_w * jnp.einsum('bhntk,bhnk->bhnt', qh, n_prev) + attn.sum(axis=-1)
    h_cell = num / jnp.maximum(jnp.abs(den), jnp.exp(-m_t))[..., None]
    h_cell = h_cell.transpose(0, 2, 3, 1, 4).reshape(bsz, L, B_WIDTH).astype(u.dtype)
    return jax.nn.sigmoid(o_pre) * h_cell * jax.nn.silu(z)

def setup_inputs(seed: int = 0) -> dict:
    key = jax.random.key(seed)
    ks = jax.random.split(key, 12)
    f32 = jnp.float32
    x = jax.random.normal(ks[0], (BATCH, SEQ, D_MODEL), f32)
    meta = jax.random.normal(ks[1], (N_META, D_MODEL), f32)
    norm_a = 1.0 + 0.02 * jax.random.normal(ks[2], (N_LAYERS_A, D_MODEL), f32)
    w_in_a = jax.random.normal(ks[3], (N_LAYERS_A, D_MODEL, A_IN), f32) * D_MODEL ** -0.5
    sinks_a = jax.random.normal(ks[4], (N_LAYERS_A, A_HEADS), f32)
    w_out_a = jax.random.normal(ks[5], (N_LAYERS_A, A_WIDTH, D_MODEL), f32) * A_WIDTH ** -0.5
    norm_b = 1.0 + 0.02 * jax.random.normal(ks[6], (N_LAYERS_B, D_MODEL), f32)
    w_in_b = jax.random.normal(ks[7], (N_LAYERS_B, D_MODEL, B_IN), f32) * D_MODEL ** -0.5
    i_bias = 0.1 * jax.random.normal(ks[8], (N_LAYERS_B, B_HEADS), f32)
    f_bias = jnp.linspace(3.0, 6.0, B_HEADS, dtype=f32)[None, :] + 0.1 * jax.random.normal(ks[9], (N_LAYERS_B, B_HEADS), f32)
    b_gates_b = jnp.concatenate([i_bias, f_bias], axis=-1)
    w_out_b = jax.random.normal(ks[10], (N_LAYERS_B, B_WIDTH, D_MODEL), f32) * B_WIDTH ** -0.5
    norm_f = 1.0 + 0.02 * jax.random.normal(ks[11], (D_MODEL,), f32)
    return {"x": x, "meta": meta, "norm_a": norm_a, "w_in_a": w_in_a, "sinks_a": sinks_a,
            "w_out_a": w_out_a, "norm_b": norm_b, "w_in_b": w_in_b, "b_gates_b": b_gates_b,
            "w_out_b": w_out_b, "norm_f": norm_f}

def reference(x, meta, norm_a, w_in_a, sinks_a, w_out_a, norm_b, w_in_b, b_gates_b, w_out_b, norm_f):
    bsz, seq, _ = x.shape
    L = N_PAD + N_META + seq
    h = jnp.concatenate([
        jnp.zeros((bsz, N_PAD, D_MODEL), x.dtype),
        jnp.broadcast_to(meta[None].astype(x.dtype), (bsz, N_META, D_MODEL)),
        x], axis=1)
    pos = jnp.arange(L) - N_PAD
    valid = pos >= 0
    for i in range(DEPTH):
        j = i // N_MIXERS
        if i % N_MIXERS == 0:
            y = swa_sink_mixer(rmsnorm(h, norm_a[j]), w_in_a[j], sinks_a[j], pos, valid)
            h = h + y @ w_out_a[j]
        else:
            y = mlstm_mixer(rmsnorm(h, norm_b[j]), w_in_b[j], b_gates_b[j], valid)
            h = h + y @ w_out_b[j]
    h = rmsnorm(h, norm_f)
    return h[:, N_PAD + N_META:]


_drawn_inputs = setup_inputs


def setup_inputs(seed=0):
    import zlib

    import numpy as np

    out = dict(_drawn_inputs(seed))
    spreads = {}
    factors = {'sinks_a': 4.371, 'norm_f': 2.828}
    for name, (base, spread) in spreads.items():
        noise = np.random.default_rng([zlib.crc32(name.encode()), seed]).standard_normal(out[name].shape)
        drawn = base * np.exp(spread * noise) if base else spread * noise
        out[name] = __import__('jax').numpy.asarray(drawn.astype(out[name].dtype))
    for name, factor in factors.items():
        out[name] = (out[name] * factor).astype(out[name].dtype)
    return out
```

```python
from contextlib import ExitStack

import concourse.bass as bass
from concourse import mybir

F32 = mybir.dt.float32
F32R = mybir.dt.float32r
ALU = mybir.AluOpType
ACT = mybir.ActivationFunctionType

P = 128
D = 1024
KT = D // P
META = 16
SEQ = 2048
T = META + SEQ
NB = 1 + SEQ // P
EPS = 1e-6

A_HEADS, A_KV, A_HD = 16, 2, 64
A_PAIRS = A_HEADS // 2
PAIRS_PER_KV = A_PAIRS // A_KV
A_K0 = A_HEADS * A_HD
A_V0 = A_K0 + A_KV * A_HD
A_Z0 = A_V0 + A_KV * A_HD
MASKED = -1.0e30

B_HEADS, B_QK, B_V = 8, 64, 128
B_K0 = B_HEADS * B_QK
B_V0 = 2 * B_HEADS * B_QK
B_O0 = B_V0 + B_HEADS * B_V
B_Z0 = B_O0 + B_HEADS * B_V
B_G0 = B_Z0 + B_HEADS * B_V

TILES = [(3 * t, min(3 * t + 3, NB)) for t in range(6)]
TW = 3 * P
PRE = 3


def start(b):
    return 0 if b == 0 else META + P * (b - 1)


def length(b):
    return META if b == 0 else P


def tile_cols(t):
    b0, b1 = TILES[t]
    return start(b0), start(b1 - 1) + length(b1 - 1)


class Phase:

    def __init__(self, nc, stack, name):
        self.nc, self.stack, self.name, self.all_sems = nc, stack, name, []

    def sb(self, name, shape, dtype=F32):
        return self.stack.enter_context(self.nc.sbuf_tensor(f"{self.name}_{name}", shape, dtype))

    def ps(self, name):
        return self.stack.enter_context(self.nc.psum_tensor(f"{self.name}_{name}", [P, 512], F32))

    def sems(self, *names):
        new = [self.stack.enter_context(self.nc.semaphore(f"{self.name}_{n}")) for n in names]
        self.all_sems += new
        return new

    def block(self):
        self.stack.callback(self.clear)
        return self.stack.enter_context(self.nc.Block())

    def clear(self):
        with self.nc.Block() as block:
            @block.sync
            def _(sp):
                for sem in self.all_sems:
                    sp.sem_clear(sem)


def product(pe, out, a_h, a_l, b_h, b_l, first, last):
    pe.matmul(out, a_h, b_h, start=first, stop=False)
    pe.matmul(out, a_l, b_h, start=False, stop=False)
    return pe.matmul(out, a_h, b_l, start=False, stop=last)


def over_blocks(eng, step, lags):
    for n in range(3):
        step(n, n % 2)
    with eng.Fori(0, (NB - 3) // 2) as i:
        step(3 + 2 * i, 1)
        step(4 + 2 * i, 0)
    for n in range(NB, NB + lags):
        step(n, n % 2)


def has(n, lag=0):
    return not isinstance(n, int) or 0 <= n - lag < NB


def size(n):
    return length(n) if isinstance(n, int) else P


def cols(n):
    return bass.ds(start(n), length(n)) if isinstance(n, int) else bass.ds(P * n - (P - META), P)


def norm_in(nc, x, meta, norm_g, ident, u_h, u_l):
    with ExitStack() as stack:
        ph = Phase(nc, stack, "n")
        x_in = [ph.sb(f"x{p}", [P, D]) for p in range(2)]
        xs = [ph.sb(f"xs{p}", [P, D]) for p in range(2)]
        gain = ph.sb("gain", [P, D])
        squares = ph.sb("squares", [P, D])
        stat = ph.sb("stat", [P, 6])
        eps = ph.sb("eps", [P, 1])
        turned = [[ph.ps(f"turned{p}{half}") for half in range(2)] for p in range(2)]
        x_loaded = ph.sems("x_loaded0", "x_loaded1")
        consts, gain_loaded, summed, rooted, inverted, scaled, transposed, rounded, remaindered = ph.sems(
            "consts", "gain_loaded", "summed", "rooted", "inverted", "scaled", "transposed", "rounded",
            "remaindered")
        block = ph.block()

        @block.sync
        def _(sp):
            sp.dma_start(gain[:, :], norm_g.partition_broadcast(P)
                         ).then_inc(gain_loaded, 16)

            def step(n, p):
                if not isinstance(n, int) or n >= 2:
                    sp.wait_ge(scaled, n - 1)
                src = meta if isinstance(n, int) and n == 0 else x[bass.ds(P * n - P, P), :]
                sp.dma_start(x_in[p][:size(n), :], src).then_inc(x_loaded[p], 16)
            over_blocks(sp, step, 0)

        @block.gpsimd
        def _(pool):
            pool.memset(eps[:, :], EPS).then_inc(consts, 1)

        @block.scalar
        def _(act):
            act.wait_ge(consts, 1)

            def step(n, p):
                if has(n):
                    m = size(n)
                    act.wait_ge(x_loaded[p], 16 * ((n // 2) + 1 if isinstance(n, int) else 1) if isinstance(n, int)
                                else 8 * n + (8 if p else 16))
                    if not isinstance(n, int) or n >= 1:
                        act.wait_ge(rooted, n)
                    if not isinstance(n, int) or n >= 2:
                        act.wait_ge(inverted, n - 1)
                    act.activation(squares[:m, :], x_in[p][:m, :], ACT.Square,
                                   accum_out=stat[:m, 3 * p:3 * p + 1]).then_inc(summed, 1)
                    act.wait_ge(summed, n + 1)
                    act.activation(stat[:m, 3 * p + 1:3 * p + 2], stat[:m, 3 * p:3 * p + 1], ACT.Sqrt,
                                   bias=eps[:m, :], scale=1.0 / D).then_inc(rooted, 1)
                if has(n, 1):
                    q = 1 - p
                    m = size(n - 1) if isinstance(n, int) else P
                    act.wait_ge(transposed, n)
                    for half in range(2):
                        src = turned[q][half][:, :].rearrange("p (k t) -> p k t", k=4)[:, :, :m]
                        act.activation(u_h[:, 4 * half:4 * half + 4, cols(n - 1)], src,
                                       ACT.Copy).then_inc(rounded, 1)
            over_blocks(act, step, 1)

        @block.vector
        def _(dve):
            dve.wait_ge(gain_loaded, 16)

            def step(n, p):
                if has(n):
                    m = size(n)
                    dve.wait_ge(rooted, n + 1)
                    if not isinstance(n, int) or n >= 2:
                        dve.wait_ge(transposed, n - 1)
                    dve.reciprocal(stat[:m, 3 * p + 2:3 * p + 3],
                                   stat[:m, 3 * p + 1:3 * p + 2]).then_inc(inverted, 1)
                    dve.wait_ge(inverted, n + 1)
                    dve.scalar_tensor_tensor(out=xs[p][:m, :], in0=x_in[p][:m, :],
                                             scalar=stat[:m, 3 * p + 2:3 * p + 3], in1=gain[:m, :],
                                             op0=ALU.mult, op1=ALU.mult).then_inc(scaled, 1)
                if has(n, 1):
                    q = 1 - p
                    m = size(n - 1) if isinstance(n, int) else P
                    dve.wait_ge(rounded, 2 * n)
                    for half in range(2):
                        src = turned[q][half][:, :].rearrange("p (k t) -> p k t", k=4)[:, :, :m]
                        ks = slice(4 * half, 4 * half + 4)
                        dve.tensor_tensor(u_l[:, ks, cols(n - 1)], src,
                                          u_h[:, ks, cols(n - 1)].bitcast(F32),
                                          ALU.subtract).then_inc(remaindered, 1)
            over_blocks(dve, step, 1)

        @block.tensor
        def _(pe):
            def step(n, p):
                m = size(n)
                pe.wait_ge(scaled, n + 1)
                if not isinstance(n, int) or n >= 2:
                    pe.wait_ge(remaindered, 2 * (n - 1))
                for k in range(KT):
                    last = pe.transpose(turned[p][k // 4][:, (k % 4) * P:(k % 4) * P + m],
                                        xs[p][:m, k * P:(k + 1) * P], ident[:m, :m])
                last.then_inc(transposed, 1)
            over_blocks(pe, step, 0)


def attention(nc, w_in, sinks, rope_table, ident, u_h, u_l, y_t):
    with ExitStack() as stack:
        ph = Phase(nc, stack, "a")
        k_h, k_l = ph.sb("k_h", [P, T], F32R), ph.sb("k_l", [P, T], F32R)
        v_h, v_l = ph.sb("v_h", [P, NB, A_HD], F32R), ph.sb("v_l", [P, NB, A_HD], F32R)
        raw = [ph.sb(f"raw{h}", [P, KT // 2, P]) for h in range(2)]
        w_h = {n: ph.sb(f"w{n}_h", [P, KT, P], F32R) for n in ("q", "z", "kv")}
        w_l = {n: ph.sb(f"w{n}_l", [P, KT, P], F32R) for n in ("q", "z", "kv")}
        rope = ph.sb("rope", [P, 2, TW])
        q_f, q_s = ph.sb("q_f", [P, TW]), ph.sb("q_s", [P, TW])
        q_h = [ph.sb(f"q_h{r}", [P, TW], F32R) for r in range(2)]
        q_l = [ph.sb(f"q_l{r}", [P, TW], F32R) for r in range(2)]
        gate = [ph.sb(f"gate{r}", [P, TW]) for r in range(2)]
        prob = [ph.sb(f"prob{r}", [P, 2, 2 * P]) for r in range(2)]
        pt_h, pt_l = ph.sb("pt_h", [P, 512], F32R), ph.sb("pt_l", [P, 512], F32R)
        y = [ph.sb(f"y{r}", [P, P]) for r in range(2)]
        mask = ph.sb("mask", [P, 2 * P])
        neg_sink = ph.sb("neg_sink", [P, A_HEADS])
        stat = [ph.sb(f"stat{r}", [P, 12]) for r in range(2)]
        MAX, NEG, SINK, SUM, ESINK, INV = (slice(2 * n, 2 * n + 2) for n in range(6))
        q_ps, z_ps = ph.ps("q_ps"), ph.ps("z_ps")
        s_ps = [ph.ps(f"s_ps{e}") for e in range(2)]
        pt_ps = [ph.ps(f"pt_ps{r}") for r in range(2)]
        o_ps = [ph.ps(f"o_ps{r}") for r in range(2)]
        raw_loaded = ph.sems("raw_loaded0", "raw_loaded1")
        y_stored = ph.sems("y_stored0", "y_stored1")
        (sinks_loaded, sinks_negated, mask_made, table_loaded, swapped) = ph.sems(
            "sinks_loaded", "sinks_negated", "mask_made", "table_loaded", "swapped")
        PE_SEMS = q_projected, z_projected, scored, turned, weighed, v_turned = ph.sems(
            "q_projected", "z_projected", "scored", "turned", "weighed", "v_turned")
        ACT_SEMS = w_rounded, q_copied, q_rounded, z_tanh, exped, pt_rounded, v_copied, v_rounded = ph.sems(
            "w_rounded", "q_copied", "q_rounded", "z_tanh", "exped", "pt_rounded", "v_copied", "v_rounded")
        (roped, roped_part, q_split, gated, maxed, negated, softened, summed, inverted, normalised, pt_split,
         y_made, v_split) = DVE_SEMS = ph.sems(
            "roped", "roped_part", "q_split", "gated", "maxed", "negated", "softened", "summed", "inverted",
            "normalised", "pt_split", "y_made", "v_split")
        w_split, waits_met_pe, waits_met_dve = ph.sems("w_split", "waits_met_pe", "waits_met_dve")
        block = ph.block()

        tile_of = lambda b: b // 3
        key0 = lambda b: start(max(b - 1, 0))
        keys = lambda b: start(b) + length(b) - key0(b)
        mask_at = lambda b: (P, P - META, 0)[min(b, 2)]

        def chunks(b):
            out = [] if b == 0 else [(0, length(b - 1), b - 1)]
            return out + [(keys(b) - length(b), length(b), b)]

        def before(n_blocks, b):
            return PRE + n_blocks + (b if b == 0 else b - 1)

        def read_count(i, t):
            return PRE + 17 * i + (15, 0, 3, 6, 9, 12)[t]

        def pt_parts(b, dst):
            ps = pt_ps[b % 2]
            if b >= 2:
                return [(0, 0, dst[:, :], ps[:, :], True)]
            view = lambda x, c, n: x[:n, 2 * P * c:2 * P * c + 2 * P].rearrange(
                "p (e t) -> p e t", e=2)[:, :, :length(b)]
            return [(0, 0, view(dst, c, n), view(ps, c, n), True) for c, (_, n, _) in enumerate(chunks(b))]

        def v_parts(t, dst):
            b0, b1 = TILES[t]
            ps = pt_ps[t % 2]
            out = []
            if b0 == 0:
                out.append((dst[:META, 0, :], ps[:META, :A_HD]))
                b0 = 1
            o = (b0 - TILES[t][0]) * A_HD
            out.append((dst[:, b0:b1, :], ps[:, o:o + (b1 - b0) * A_HD].rearrange("p (b d) -> p b d", d=A_HD)))
            return out

        @block.sync
        def _(sp):
            for y_slot in y_stored:
                sp.sem_inc(y_slot, 16)
            sp.dma_start(neg_sink[:, :], sinks.partition_broadcast(P)).then_inc(sinks_loaded, 16)

            def table(run, t):
                sp.wait_ge(roped, PRE + run)
                a, z = tile_cols(t)
                sp.dma_start(rope[:, :, :z - a], rope_table[:, :, a:z]).then_inc(table_loaded, 16)

            def swap(run, t):
                a, z = tile_cols(t)
                sp.wait_ge(q_copied, PRE + run + 1)
                for r in range(0, P, 64):
                    for x, z0 in ((0, 32), (32, 0)):
                        sp.dma_start(q_s[r + x:r + x + 32, :z - a],
                                     q_f[r + z0:r + z0 + 32, :z - a]).then_inc(swapped, 16)

            def store(i, b):
                sp.wait_ge(y_made, PRE + 17 * i + b + 1)
                sp.dma_start(y_t[bass.ds(P * i, P), start(b):start(b) + length(b)],
                             y[b % 2][:, :length(b)]).then_inc(y_stored[b % 2], 16)

            table(0, 0)
            swap(0, 0)
            with sp.Fori(0, A_KV) as g:
                for t in range(6):
                    table(30 * g + 1 + t, t)
                    swap(30 * g + 1 + t, t)
                with sp.Fori(0, PAIRS_PER_KV) as j:
                    i = g * PAIRS_PER_KV + j
                    for s in range(19):
                        if s < 18:
                            grp = s // 3
                            run = 6 * i + grp + 1 + 6 * (g + 1)
                            if s % 3 == 0:
                                table(run, (grp + 1) % 6)
                            if s % 3 == 1:
                                swap(run, (grp + 1) % 6)
                        if 0 <= s - 2 < NB:
                            store(i, s - 2)
            sp.wait_ge(y_stored[0], 16 * (1 + 9 * A_PAIRS))
            sp.wait_ge(y_stored[1], 16 * (1 + 8 * A_PAIRS))

        @block.gpsimd
        def _(pool):
            pool.sem_inc(w_split, PRE)
            pool.memset(mask[:, :], 0.0).then_inc(mask_made, 1)
            pool.wait_ge(mask_made, 1)
            pool.affine_select(out=mask[:, :P], in_=mask[:, :P], compare_op=ALU.is_gt, fill=MASKED, base=0,
                               pattern=[[1, P]], channel_multiplier=-1).then_inc(mask_made, 1)
            pool.affine_select(out=mask[:, P:], in_=mask[:, P:], compare_op=ALU.is_ge, fill=MASKED, base=0,
                               pattern=[[-1, P]], channel_multiplier=1).then_inc(mask_made, 1)

            def load(unit, *columns):
                for h in range(2):
                    pool.wait_ge(w_split, PRE + 2 * unit)
                    src = w_in[bass.ds(512 * h, 512), :].rearrange("(k p) n -> p k n", p=P)
                    for at, n, dst in columns:
                        pool.dma_start(raw[h][:, :, dst:dst + n], src[:, :, bass.ds(at, n)]).then_inc(
                            raw_loaded[h], 16)

            def split(unit, name):
                for h in range(2):
                    pool.wait_ge(w_rounded, PRE + 2 * unit + h + 1)
                    ks = slice(4 * h, 4 * h + 4)
                    pool.tensor_tensor(w_l[name][:, ks, :], raw[h][:, :, :], w_h[name][:, ks, :].bitcast(F32),
                                       ALU.subtract).then_inc(w_split, 1)

            load(0, (0, P, 0))
            split(0, "q")
            load(1, (A_Z0, P, 0))
            split(1, "z")
            with pool.Fori(0, A_KV) as g:
                load(2 + 9 * g, (A_K0 + A_HD * g, A_HD, 0), (A_V0 + A_HD * g, A_HD, A_HD))
                split(2 + 9 * g, "kv")
                with pool.Fori(0, PAIRS_PER_KV) as j:
                    i = g * PAIRS_PER_KV + j
                    unit = 3 + g + 2 * i
                    load(unit, (((i + 1) % A_PAIRS) * P, P, 0))
                    split(unit, "q")
                    load(unit + 1, (((i + 1) % A_PAIRS) * P + A_Z0, P, 0))
                    split(unit + 1, "z")

        @block.scalar
        def _(act):
            for sem in ACT_SEMS:
                act.sem_inc(sem, PRE)

            def round_w(loads, name, h):
                act.wait_ge(raw_loaded[h], 16 * loads)
                act.activation(w_h[name][:, 4 * h:4 * h + 4, :], raw[h][:, :, :], ACT.Copy).then_inc(w_rounded, 1)

            def copy_q(run, t):
                a, z = tile_cols(t)
                act.wait_ge(q_projected, PRE + run + 1)
                act.wait_ge(q_split, PRE + run)
                act.activation(q_f[:, :z - a], q_ps[:, :z - a], ACT.Copy).then_inc(q_copied, 1)

            def round_q(run, i, t):
                a, z = tile_cols(t)
                if i is not None:
                    act.wait_ge(scored, read_count(i, t))
                act.wait_ge(roped, PRE + run + 1)
                act.activation(q_h[t % 2][:, :z - a], q_f[:, :z - a], ACT.Copy).then_inc(q_rounded, 1)

            def tanh_z(i, t):
                a, z = tile_cols(t)
                act.wait_ge(z_projected, PRE + 6 * i + t + 1)
                act.wait_ge(y_made, PRE + 17 * i + (-2, 0, 3, 6, 9, 12)[t])
                act.activation(gate[t % 2][:, :z - a], z_ps[:, :z - a], ACT.Tanh, scale=0.5).then_inc(z_tanh, 1)

            def exponentials(i, b):
                m, r = length(b), b % 2
                act.wait_ge(softened, PRE + 17 * i + b + 1)
                for e in range(2):
                    part = prob[r][:m, e, :keys(b)]
                    act.activation(part, part, ACT.Exp, bias=stat[r][:m, NEG.start + e:NEG.start + e + 1],
                                   accum_out=stat[r][:m, SUM.start + e:SUM.start + e + 1])
                act.activation(stat[r][:m, ESINK], stat[r][:m, SINK], ACT.Exp).then_inc(exped, 1)

            def round_pt(i, b):
                act.wait_ge(turned, PRE + 17 * i + b + 1)
                act.wait_ge(weighed, PRE + 17 * i + b)
                for at, n, out, src, last in pt_parts(b, pt_h):
                    ins = act.activation(out, src, ACT.Copy)
                ins.then_inc(pt_rounded, 1)

            for h in range(2):
                round_w(1, "q", h)
            for h in range(2):
                round_w(2, "z", h)
            copy_q(0, 0)
            round_q(0, None, 0)
            with act.Fori(0, A_KV) as g:
                act.wait_ge(q_projected, PRE + 30 * g + 1)
                for h in range(2):
                    round_w(4 + 10 * g, "kv", h)
                for t in range(7):
                    if t < 6:
                        a, z = tile_cols(t)
                        run = 30 * g + 1 + t
                        act.wait_ge(q_projected, PRE + run + 1)
                        act.wait_ge(y_made, PRE + 68 * g)
                        act.wait_ge(v_turned, PRE + 6 * g + t)
                        act.activation(gate[1][:A_HD, :z - a], q_ps[A_HD:, :z - a], ACT.Copy).then_inc(v_copied, 1)
                        act.wait_ge(q_split, PRE + run)
                        for half in range(2):
                            ins = act.activation(q_f[A_HD * half:A_HD * half + A_HD, :z - a],
                                                 q_ps[:A_HD, :z - a], ACT.Copy)
                        ins.then_inc(q_copied, 1)
                    if t > 0:
                        act.wait_ge(v_turned, PRE + 6 * g + t)
                        for out, src in v_parts(t - 1, v_h):
                            ins = act.activation(out, src, ACT.Copy)
                        ins.then_inc(v_rounded, 1)
                    if t < 6:
                        act.wait_ge(roped, PRE + run + 1)
                        act.activation(k_h[:, a:z], q_f[:, :z - a], ACT.Copy).then_inc(q_rounded, 1)
                with act.Fori(0, PAIRS_PER_KV) as j:
                    i = g * PAIRS_PER_KV + j
                    for s in range(18):
                        grp = s // 3
                        run = 6 * i + grp + 1 + 6 * (g + 1)
                        if s < NB:
                            exponentials(i, s)
                        if s % 3 == 0:
                            tanh_z(i, grp)
                        if s > 0:
                            round_pt(i, s - 1)
                        if s % 3 == 1:
                            copy_q(run, (grp + 1) % 6)
                        if s % 3 == 2:
                            round_q(run, i, (grp + 1) % 6)
                        if s in (14, 15):
                            done = q_projected if s == 14 else z_projected
                            act.wait_ge(done, PRE + 6 * i + 6 + (6 * (g + 1) if s == 14 else 0))
                            for h in range(2):
                                round_w(5 + 2 * g + 2 * i + s - 14, "qz"[s - 14], h)

        @block.vector
        def _(dve):
            for sem in DVE_SEMS:
                dve.sem_inc(sem, PRE)
            dve.wait_ge(sinks_loaded, 16)
            dve.tensor_scalar(neg_sink[:, :], neg_sink[:, :], -1.0, None, ALU.mult).then_inc(sinks_negated, 1)
            dve.wait_ge(sinks_negated, 1)
            dve.wait_ge(mask_made, 3)

            def rotate(run, t):
                w = tile_cols(t)[1] - tile_cols(t)[0]
                dve.wait_ge(swapped, 64 * (run + 1))
                dve.wait_ge(table_loaded, 16 * (run + 1))
                dve.tensor_tensor(q_f[:, :w], q_f[:, :w], rope[:, 0, :w], ALU.mult)
                dve.tensor_tensor(q_s[:, :w], q_s[:, :w], rope[:, 1, :w], ALU.mult).then_inc(roped_part, 1)
                dve.wait_ge(roped_part, PRE + run + 1)
                dve.tensor_tensor(q_f[:, :w], q_f[:, :w], q_s[:, :w], ALU.add).then_inc(roped, 1)

            def split_q(run, out_l, out_h, w):
                dve.wait_ge(q_rounded, PRE + run + 1)
                dve.tensor_tensor(out_l, q_f[:, :w], out_h.bitcast(F32), ALU.subtract).then_inc(q_split, 1)

            def split_query(run, t):
                w = tile_cols(t)[1] - tile_cols(t)[0]
                split_q(run, q_l[t % 2][:, :w], q_h[t % 2][:, :w], w)

            def make_gate(i, t):
                w = tile_cols(t)[1] - tile_cols(t)[0]
                dve.wait_ge(z_tanh, PRE + 6 * i + t + 1)
                dve.scalar_tensor_tensor(out=gate[t % 2][:, :w], in0=gate[t % 2][:, :w], scalar=1.0,
                                         in1=z_ps[:, :w], op0=ALU.add, op1=ALU.mult).then_inc(gated, 1)

            def soften(i, b):
                m, r, n, c = length(b), b % 2, keys(b), mask_at(b)
                st = stat[r]
                dve.wait_ge(scored, PRE + 17 * i + b + 1)
                dve.wait_ge(turned, before(17 * i, b))
                dve.sem_inc(waits_met_dve, 1)
                for e in range(2):
                    ins = dve.tensor_tensor_reduce(
                        prob[r][:m, e, :n], s_ps[e][:m, :n], mask[:m, c:c + n],
                        A_HD ** -0.5, MASKED, ALU.add, ALU.max, st[:m, MAX.start + e:MAX.start + e + 1])
                ins.then_inc(maxed, 1)
                dve.wait_ge(maxed, PRE + 17 * i + b + 1)
                sink = neg_sink[:m, bass.ds(2 * i, 2)]
                dve.scalar_tensor_tensor(out=st[:m, NEG], in0=st[:m, MAX], scalar=-1.0, in1=sink,
                                         op0=ALU.mult, op1=ALU.min).then_inc(negated, 1)
                dve.wait_ge(negated, PRE + 17 * i + b + 1)
                dve.tensor_tensor(st[:m, SINK], st[:m, NEG], sink, ALU.subtract).then_inc(softened, 1)

            def normalise(i, b):
                m, r, n = length(b), b % 2, keys(b)
                st = stat[r]
                dve.wait_ge(exped, PRE + 17 * i + b + 1)
                dve.tensor_tensor(st[:m, SUM], st[:m, SUM], st[:m, ESINK], ALU.add).then_inc(summed, 1)
                dve.wait_ge(summed, PRE + 17 * i + b + 1)
                dve.reciprocal(st[:m, INV], st[:m, SUM]).then_inc(inverted, 1)
                dve.wait_ge(inverted, PRE + 17 * i + b + 1)
                for e in range(2):
                    ins = dve.tensor_scalar(prob[r][:m, e, :n], prob[r][:m, e, :n],
                                            st[:m, INV.start + e:INV.start + e + 1], None, ALU.mult)
                ins.then_inc(normalised, 1)

            def split_pt(i, b):
                dve.wait_ge(pt_rounded, PRE + 17 * i + b + 1)
                for (_, _, out, src, _), (_, _, high, _, _) in zip(pt_parts(b, pt_l), pt_parts(b, pt_h)):
                    ins = dve.tensor_tensor(out, src, high.bitcast(F32), ALU.subtract)
                ins.then_inc(pt_split, 1)

            def make_y(i, b):
                m, r, t = length(b), b % 2, tile_of(b)
                dve.wait_ge(weighed, PRE + 17 * i + b + 1)
                dve.wait_ge(gated, PRE + 6 * i + t + 1)
                dve.wait_ge(y_stored[r], 16 * (1 + (9 - r) * i + b // 2))
                c = start(b) - tile_cols(t)[0]
                for e in range(2):
                    rows = slice(A_HD * e, A_HD * e + A_HD)
                    ins = dve.scalar_tensor_tensor(out=y[r][rows, :m], in0=o_ps[r][:A_HD, m * e:m * e + m],
                                                   scalar=0.5, in1=gate[t % 2][rows, c:c + m],
                                                   op0=ALU.mult, op1=ALU.mult)
                ins.then_inc(y_made, 1)

            rotate(0, 0)
            split_query(0, 0)
            with dve.Fori(0, A_KV) as g:
                for t in range(7):
                    if t < 6:
                        a, z = tile_cols(t)
                        rotate(30 * g + 1 + t, t)
                    if t > 0:
                        dve.wait_ge(v_rounded, PRE + 6 * g + t)
                        for (out, src), (high, _) in zip(v_parts(t - 1, v_l), v_parts(t - 1, v_h)):
                            ins = dve.tensor_tensor(out, src, high.bitcast(F32), ALU.subtract)
                        ins.then_inc(v_split, 1)
                    if t < 6:
                        split_q(30 * g + 1 + t, k_l[:, a:z], k_h[:, a:z], z - a)
                with dve.Fori(0, PAIRS_PER_KV) as j:
                    i = g * PAIRS_PER_KV + j
                    for s in range(19):
                        grp = s // 3
                        run = 6 * i + grp + 1 + 6 * (g + 1)
                        if 0 <= s - 2 < NB:
                            make_y(i, s - 2)
                        if s < NB:
                            soften(i, s)
                            normalise(i, s)
                        if 0 <= s - 1 < NB:
                            split_pt(i, s - 1)
                        if s % 3 == 0 and s < 18:
                            make_gate(i, grp)
                        if s % 3 == 2:
                            rotate(run, (grp + 1) % 6)
                            split_query(run, (grp + 1) % 6)

        @block.tensor
        def _(pe):
            for sem in PE_SEMS:
                pe.sem_inc(sem, PRE)

            def project(ps, name, t, ks):
                a, z = tile_cols(t)
                for k in ks:
                    last = product(pe, ps[:, :z - a], w_h[name][:, k, :], w_l[name][:, k, :],
                                   u_h[:, k, a:z], u_l[:, k, a:z], k == 0, k == KT - 1)
                return last

            def project_part(run, i_w, m, t, part, unit):
                name, ks = "qz"[part // 3], (range(0, 3), range(3, 6), range(6, 8))[part % 3]
                if part == 0:
                    pe.wait_ge(q_copied, PRE + run)
                    if t == 0:
                        pe.wait_ge(w_split, PRE + 2 * unit + 2)
                if part == 3:
                    pe.wait_ge(gated, PRE + m)
                    if t == 0:
                        pe.wait_ge(w_split, PRE + 2 * unit + 4)
                last = project(q_ps if name == "q" else z_ps, name, t, ks)
                if part == 2:
                    last.then_inc(q_projected, 1)
                if part == 5:
                    last.then_inc(z_projected, 1)

            def scores(g, i, b):
                m, r, n, t = length(b), b % 2, keys(b), tile_of(b)
                c = start(b) - tile_cols(t)[0]
                if b == TILES[t][0]:
                    pe.wait_ge(q_split, PRE + 6 * i + t + 6 * (g + 1) + 1)
                pe.wait_ge(maxed, PRE + 17 * i + b)
                if b == 0:
                    pe.sem_inc(waits_met_pe, 1)
                for e in range(2):
                    rows = slice(A_HD * e, A_HD * e + A_HD)
                    last = product(pe, s_ps[e][:m, :n],
                                   q_h[t % 2][rows, c:c + m], q_l[t % 2][rows, c:c + m],
                                   k_h[rows, key0(b):key0(b) + n], k_l[rows, key0(b):key0(b) + n], True, True)
                last.then_inc(scored, 1)

            def turn(i, b):
                m, r = length(b), b % 2
                pe.wait_ge(normalised, PRE + 17 * i + b + 1)
                pe.wait_ge(pt_split, before(17 * i, b))
                if b == 0:
                    pe.sem_inc(waits_met_pe, 1)
                for c, (at, n, _) in enumerate(chunks(b)):
                    for e in range(2):
                        last = pe.transpose(pt_ps[r][:n, 2 * P * c + P * e:2 * P * c + P * e + m],
                                            prob[r][:m, e, at:at + n], ident[:m, :m])
                last.then_inc(turned, 1)

            def weigh(g, i, b):
                m, r = length(b), b % 2
                pe.wait_ge(pt_split, PRE + 17 * i + b + 1)
                if b == 0:
                    pe.wait_ge(v_split, PRE + 6 * g + 6)
                pe.wait_ge(y_made, before(17 * i, b))
                parts = chunks(b)
                view = lambda x, c, n: x[:n, 2 * P * c:2 * P * c + 2 * P].rearrange(
                    "p (e t) -> p e t", e=2)[:, :, :m]
                out = o_ps[r][:A_HD, :2 * m].rearrange("p (e t) -> p e t", e=2)
                for c, (_, n, kb) in enumerate(parts):
                    first, final = c == 0, c == len(parts) - 1
                    pe.matmul(out, v_h[:n, kb, :], view(pt_h, c, n), start=first, stop=False)
                    pe.matmul(out, v_l[:n, kb, :], view(pt_h, c, n), start=False, stop=False)
                    last = pe.matmul(out, v_h[:n, kb, :], view(pt_l, c, n), start=False, stop=final)
                last.then_inc(weighed, 1)

            for part in range(6):
                project_part(0, 0, 0, 0, part, 0)
            with pe.Fori(0, A_KV) as g:
                pe.wait_ge(w_split, PRE + 2 * (2 + 9 * g) + 2)
                pe.wait_ge(pt_split, PRE + 68 * g)
                for t in range(7):
                    if t < 6:
                        pe.wait_ge(q_copied, PRE + 30 * g + 1 + t)
                        project(q_ps, "kv", t, range(KT)).then_inc(q_projected, 1)
                    if t > 0:
                        pe.wait_ge(v_copied, PRE + 6 * g + t)
                        pe.wait_ge(v_split, PRE + 6 * g + t - 2)
                        pe.sem_inc(waits_met_pe, 1)
                        b0, b1 = TILES[t - 1]
                        for b in range(b0, b1):
                            c = start(b) - start(b0)
                            o = (b - b0) * A_HD
                            last = pe.transpose(pt_ps[(t - 1) % 2][:length(b), o:o + A_HD],
                                                gate[1][:A_HD, c:c + length(b)], ident[:A_HD, :A_HD])
                        last.then_inc(v_turned, 1)
                with pe.Fori(0, PAIRS_PER_KV) as j:
                    i = g * PAIRS_PER_KV + j
                    for s in range(18):
                        grp = s // 3
                        m = 6 * i + grp + 1
                        run, t, unit = m + 6 * (g + 1), (grp + 1) % 6, 3 + g + 2 * i
                        if s < NB:
                            scores(g, i, s)
                        project_part(run, i, m, t, 2 * (s % 3), unit)
                        if s > 0:
                            turn(i, s - 1)
                        project_part(run, i, m, t, 2 * (s % 3) + 1, unit)
                        if s > 0:
                            weigh(g, i, s - 1)


def project_out(nc, name, w_out, y_src, residual, norm_g, ident, stores):
    first_layer = len(stores) == 2
    n_blocks = NB if first_layer else NB - 1
    peeled = 5 if first_layer else 4
    mm_lag = 0 if first_layer else 1
    lag = mm_lag + 1

    def over(eng, step, lags):
        for n in range(peeled):
            step(n, n % 2)
        with eng.Fori(0, (n_blocks - peeled) // 2) as i:
            step(peeled + 2 * i, peeled % 2)
            step(peeled + 1 + 2 * i, 1 - peeled % 2)
        for n in range(n_blocks, n_blocks + lags):
            step(n, n % 2)

    def exists(n, lag=0):
        return not isinstance(n, int) or 0 <= n - lag < n_blocks

    def rows_of(n):
        return cols(n) if first_layer else bass.ds(P * n + META, P)

    def size_of(n):
        return size(n) if first_layer else P

    def used(n, ring=2):
        return not isinstance(n, int) or n >= ring

    with ExitStack() as stack:
        ph = Phase(nc, stack, name)
        w_h, w_l = ph.sb("w_h", [P, KT, D], F32R), ph.sb("w_l", [P, KT, D], F32R)
        raw = [ph.sb(f"raw{k}", [P, D]) for k in range(4)]
        gain, squares = ph.sb("gain", [P, D]), ph.sb("squares", [P, D])
        y_in = [ph.sb(f"y{p}", [P, D]) for p in range(2)]
        y_h = [ph.sb(f"y_h{p}", [P, KT, P], F32R) for p in range(2)]
        y_l = [ph.sb(f"y_l{p}", [P, KT, P], F32R) for p in range(2)]
        res = [ph.sb(f"res{p}", [P, D]) for p in range(2)]
        h = [ph.sb(f"h{p}", [P, D]) for p in range(2)]
        xs = [ph.sb(f"xs{p}", [P, D]) for p in range(2)]
        u_t = [ph.sb(f"u_t{p}", [P, KT, P]) for p in range(2)] if first_layer else None
        stat = [ph.sb(f"stat{p}", [P, 3]) for p in range(2)]
        eps = ph.sb("eps", [P, 1])
        acc = [[ph.ps(f"acc{p}{c}") for c in range(2)] for p in range(2)]
        turned_ps = [[ph.ps(f"turned{p}{c}") for c in range(2)] for p in range(2)]
        y_loaded = ph.sems("y_loaded0", "y_loaded1")
        res_loaded = ph.sems("res_loaded0", "res_loaded1")
        h_stored, u_stored = ph.sems("h_stored0", "h_stored1"), ph.sems("u_stored0", "u_stored1")
        raw_loaded = ph.sems(*(f"raw_loaded{k}" for k in range(4)))
        (gain_loaded, eps_made, w_rounded, w_split_pool, w_split_dve, y_rounded, y_split, multiplied, h_made, summed,
         rooted, inverted, scaled, turned, copied_act, copied_dve) = ph.sems(
            "gain_loaded", "eps_made", "w_rounded", "w_split_pool", "w_split_dve", "y_rounded", "y_split",
            "multiplied", "h_made", "summed", "rooted", "inverted", "scaled", "turned", "copied_act", "copied_dve")
        POOL_KS, DVE_KS = (2, 5), (0, 1, 3, 4, 6, 7)
        block = ph.block()
        loads = lambda n, p: 8 * n + (8 if p else 16)

        @block.sync
        def _(sp):
            def load_w(k):
                if k >= 4:
                    sp.wait_ge(w_split_pool, sum(j <= k - 4 for j in POOL_KS)) if k - 4 in POOL_KS else \
                        sp.wait_ge(w_split_dve, sum(j <= k - 4 for j in DVE_KS))
                sp.dma_start(raw[k % 4][:, :], w_out[P * k:P * k + P, :]).then_inc(raw_loaded[k % 4], 16)

            def step(n, p):
                m = size_of(n)
                if used(n):
                    sp.wait_ge(y_split, n - 1)
                if first_layer:
                    sp.dma_start(y_in[p][:, :].rearrange("p (k t) -> p k t", k=KT)[:, :, :m],
                                 y_src[:, cols(n)].rearrange("(k p) t -> p k t", p=P)).then_inc(y_loaded[p], 16)
                else:
                    sp.dma_start(y_in[p][:, :], y_src[rows_of(n), :]).then_inc(y_loaded[p], 16)
                if used(n):
                    sp.wait_ge(h_made, 2 * (n - 1))
                sp.dma_start(res[p][:m, :], residual(n)).then_inc(res_loaded[p], 16)
                if isinstance(n, int) and n == 0:
                    sp.dma_start(gain[:, :], norm_g.partition_broadcast(P)).then_inc(gain_loaded, 16)
                    for k in range(KT):
                        load_w(k)
            over(sp, step, 0)

        @block.gpsimd
        def _(pool):
            pool.memset(eps[:, :], EPS).then_inc(eps_made, 1)
            for k in POOL_KS:
                pool.wait_ge(w_rounded, k + 1)
                pool.tensor_tensor(w_l[:, k, :], raw[k % 4][:, :], w_h[:, k, :].bitcast(F32),
                                   ALU.subtract).then_inc(w_split_pool, 1)

            def step(n, p):
                if exists(n, lag):
                    b, q = n - lag, (p + lag) % 2
                    m = size_of(b)
                    if first_layer:
                        pool.wait_ge(h_made, 2 * (b + 1))
                        pool.dma_start(stores[0][rows_of(b), :], h[q][:m, :]).then_inc(h_stored[q], 16)
                    else:
                        pool.wait_ge(scaled, b + 1)
                        pool.dma_start(stores[0][bass.ds(P * b, P), :], xs[q][:, :]).then_inc(h_stored[q], 16)
                if first_layer and exists(n, 2):
                    b = n - 2
                    m = size_of(b)
                    pool.wait_ge(copied_act, b + 1)
                    pool.wait_ge(copied_dve, b + 1)
                    pool.dma_start(stores[1][:, rows_of(b)].rearrange("(k p) t -> p k t", p=P),
                                   u_t[p][:, :, :m]).then_inc(u_stored[p], 16)
            over(pool, step, 2)
            for p in range(2):
                stored = 16 * ((n_blocks + 1 - p) // 2)
                pool.wait_ge(h_stored[p], stored)
                if first_layer:
                    pool.wait_ge(u_stored[p], stored)

        @block.scalar
        def _(act):
            for k in range(KT):
                act.wait_ge(raw_loaded[k % 4], 16 * (k // 4 + 1))
                act.activation(w_h[:, k, :], raw[k % 4][:, :], ACT.Copy).then_inc(w_rounded, 1)
            act.wait_ge(eps_made, 1)

            def step(n, p):
                if exists(n):
                    m = size_of(n)
                    if used(n):
                        act.wait_ge(multiplied, n - 1)
                    if first_layer:
                        act.wait_ge(y_loaded[p], loads(n, p))
                        act.activation(y_h[p][:, :, :m],
                                       y_in[p][:, :].rearrange("p (k t) -> p k t", k=KT)[:, :, :m],
                                       ACT.Copy).then_inc(y_rounded, 1)
                    else:
                        act.wait_ge(turned, n + 1)
                        for c in range(2):
                            ins = act.activation(y_h[p][:, 4 * c:4 * c + 4, :],
                                                 turned_ps[p][c][:, :].rearrange("p (k t) -> p k t", k=4), ACT.Copy)
                        ins.then_inc(y_rounded, 1)
                if exists(n, lag):
                    b, q = n - lag, (p + lag) % 2
                    m = size_of(b)
                    act.wait_ge(h_made, 2 * (b + 1))
                    if used(n, lag + 1):
                        act.wait_ge(rooted, b)
                    if used(n, lag + 2):
                        act.wait_ge(inverted, b - 1)
                    act.activation(squares[:m, :], h[q][:m, :], ACT.Square,
                                   accum_out=stat[q][:m, 0:1]).then_inc(summed, 1)
                    act.wait_ge(summed, b + 1)
                    act.activation(stat[q][:m, 1:2], stat[q][:m, 0:1], ACT.Sqrt, bias=eps[:m, :],
                                   scale=1.0 / D).then_inc(rooted, 1)
                if first_layer and exists(n, 2):
                    b = n - 2
                    m = size_of(b)
                    act.wait_ge(turned, b + 1)
                    if used(n, 4):
                        act.wait_ge(u_stored[p], loads(b - 2, p))
                    act.activation(u_t[p][:, :4, :m],
                                   turned_ps[p][0][:, :].rearrange("p (k t) -> p k t", k=4)[:, :, :m],
                                   ACT.Copy).then_inc(copied_act, 1)
            over(act, step, 2)

        @block.vector
        def _(dve):
            for k in DVE_KS:
                dve.wait_ge(w_rounded, k + 1)
                dve.tensor_tensor(w_l[:, k, :], raw[k % 4][:, :], w_h[:, k, :].bitcast(F32),
                                  ALU.subtract).then_inc(w_split_dve, 1)
            dve.wait_ge(gain_loaded, 16)

            def step(n, p):
                if exists(n):
                    m = size_of(n)
                    dve.wait_ge(y_rounded, n + 1)
                    if first_layer:
                        dve.tensor_tensor(y_l[p][:, :, :m],
                                          y_in[p][:, :].rearrange("p (k t) -> p k t", k=KT)[:, :, :m],
                                          y_h[p][:, :, :m].bitcast(F32), ALU.subtract).then_inc(y_split, 1)
                    else:
                        for c in range(2):
                            ks = slice(4 * c, 4 * c + 4)
                            ins = dve.tensor_tensor(y_l[p][:, ks, :],
                                                    turned_ps[p][c][:, :].rearrange("p (k t) -> p k t", k=4),
                                                    y_h[p][:, ks, :].bitcast(F32), ALU.subtract)
                        ins.then_inc(y_split, 1)
                if exists(n, lag):
                    b, q = n - lag, (p + lag) % 2
                    m = size_of(b)
                    dve.wait_ge(multiplied, b + 1)
                    dve.wait_ge(res_loaded[q], loads(b, q))
                    if used(n, lag + 2):
                        dve.wait_ge(summed, b - 1)
                        if first_layer:
                            dve.wait_ge(h_stored[q], loads(b - 2, q))
                    for c in range(2):
                        dve.tensor_tensor(h[q][:m, 512 * c:512 * c + 512], acc[q][c][:m, :],
                                          res[q][:m, 512 * c:512 * c + 512], ALU.add).then_inc(h_made, 1)
                    dve.wait_ge(rooted, b + 1)
                    dve.reciprocal(stat[q][:m, 2:3], stat[q][:m, 1:2]).then_inc(inverted, 1)
                    dve.wait_ge(inverted, b + 1)
                    if used(n, lag + 2):
                        if first_layer:
                            dve.wait_ge(turned, b - 1)
                        else:
                            dve.wait_ge(h_stored[q], loads(b - 2, q))
                    dve.scalar_tensor_tensor(out=xs[q][:m, :], in0=h[q][:m, :], scalar=stat[q][:m, 2:3],
                                             in1=gain[:m, :], op0=ALU.mult, op1=ALU.mult).then_inc(scaled, 1)
                if first_layer and exists(n, 2):
                    b = n - 2
                    m = size_of(b)
                    dve.wait_ge(turned, b + 1)
                    if used(n, 4):
                        dve.wait_ge(u_stored[p], loads(b - 2, p))
                    dve.tensor_copy(u_t[p][:, 4:, :m],
                                    turned_ps[p][1][:, :].rearrange("p (k t) -> p k t", k=4)[:, :, :m]
                                    ).then_inc(copied_dve, 1)
            over(dve, step, 2)

        @block.tensor
        def _(pe):
            def turn(src, b, q, m):
                for k in range(KT):
                    last = pe.transpose(turned_ps[q][k // 4][:, (k % 4) * P:(k % 4) * P + m],
                                        src[q][:m, k * P:(k + 1) * P], ident[:m, :m])
                last.then_inc(turned, 1)

            def step(n, p):
                if not first_layer and exists(n):
                    pe.wait_ge(y_loaded[p], loads(n, p))
                    if used(n):
                        pe.wait_ge(y_split, n - 1)
                    turn(y_in, n, p, P)
                if exists(n, mm_lag):
                    b, q = n - mm_lag, (p + mm_lag) % 2
                    m = size_of(b)
                    pe.wait_ge(y_split, b + 1)
                    if used(n, mm_lag + 2):
                        pe.wait_ge(h_made, 2 * (b - 1))
                    for k in range(KT):
                        if isinstance(b, int) and b == 0:
                            names = (w_split_pool, POOL_KS) if k in POOL_KS else (w_split_dve, DVE_KS)
                            pe.wait_ge(names[0], sum(j <= k for j in names[1]))
                        for c in range(2):
                            last = product(pe, acc[q][c][:m, :], y_h[q][:, k, :m], y_l[q][:, k, :m],
                                           w_h[:, k, 512 * c:512 * c + 512], w_l[:, k, 512 * c:512 * c + 512],
                                           k == 0, k == KT - 1)
                    last.then_inc(multiplied, 1)
                if first_layer and exists(n, 1):
                    b, q = n - 1, 1 - p
                    m = size_of(b)
                    pe.wait_ge(scaled, b + 1)
                    if used(n, 3):
                        pe.wait_ge(copied_act, b - 1)
                        pe.wait_ge(copied_dve, b - 1)
                    turn(xs, b, q, m)
            over(pe, step, 1)


GATE_I, GATE_F = 0, 32


def gates(nc, u_t, w_in, b_gates, ident, u_h, u_l, head_cols, row_a, row_dec):
    H = B_HEADS
    with ExitStack() as stack:
        ph = Phase(nc, stack, "g")
        u_in = [ph.sb(f"u_in{r}", [P, KT, TW]) for r in range(2)]
        w_raw = ph.sb("w_raw", [P, KT, 64])
        w_h, w_l = ph.sb("w_h", [P, KT, 64], F32R), ph.sb("w_l", [P, KT, 64], F32R)
        bias = ph.sb("bias", [64, 1])
        rows = ph.sb("rows", [P, T])
        log_i, log_f = ph.sb("log_i", [H, T]), ph.sb("log_f", [H, T])
        keep, scratch = ph.sb("keep", [H, T]), ph.sb("scratch", [H, T])
        m_prev, dec = ph.sb("m_prev", [H, NB]), ph.sb("dec", [H, NB])
        g_ps = [ph.ps(f"g_ps{r}") for r in range(2)]
        c_ps = [ph.ps(f"c_ps{r}") for r in range(4)]
        u_loaded = ph.sems("u_loaded0", "u_loaded1")
        (w_cleared, w_loaded, w_rounded, w_split, cleared, u_rounded, u_split, projected, biased, step, act_step,
         turned, stored, filled) = ph.sems(
            "w_cleared", "w_loaded", "w_rounded", "w_split", "cleared", "u_rounded", "u_split", "projected",
            "biased", "step", "act_step", "turned", "stored", "filled")
        block = ph.block()
        PER_BANK = 5

        @block.sync
        def _(sp):
            sp.wait_ge(w_cleared, 1)
            src = w_in.rearrange("(k p) n -> p k n", p=P)
            sp.dma_start(w_raw[:, :, GATE_I:GATE_I + H], src[:, :, B_G0:B_G0 + H]).then_inc(w_loaded, 16)
            sp.dma_start(w_raw[:, :, GATE_F:GATE_F + H], src[:, :, B_G0 + H:B_G0 + 2 * H]).then_inc(w_loaded, 16)
            bias_src = b_gates.rearrange("(n a) -> n a", a=1)
            sp.dma_start(bias[GATE_I:GATE_I + H, :], bias_src[:H, :]).then_inc(w_loaded, 16)
            sp.dma_start(bias[GATE_F:GATE_F + H, :], bias_src[H:, :]).then_inc(w_loaded, 16)
            for t in range(6):
                a, z = tile_cols(t)
                if t >= 2:
                    sp.wait_ge(u_split, t - 1)
                sp.dma_start(u_in[t % 2][:, :, :z - a],
                             u_t[:, a:z].rearrange("(k p) t -> p k t", p=P)).then_inc(u_loaded[t % 2], 16)
            sp.wait_ge(step, 9)
            sp.dma_start(row_a.rearrange("(h t) -> h t", h=H), log_i[:, :]).then_inc(stored, 16)
            sp.wait_ge(act_step, 3)
            sp.dma_start(row_dec.rearrange("(h b) -> h b", h=H), dec[:, :]).then_inc(stored, 16)
            sp.wait_ge(stored, 32)

        @block.gpsimd
        def _(pool):
            pool.memset(w_raw[:, :, :], 0.0).then_inc(w_cleared, 1)
            pool.memset(rows[:, :], 0.0).then_inc(cleared, 1)
            pool.wait_ge(w_rounded, 1)
            pool.tensor_tensor(w_l[:, :, :], w_raw[:, :, :], w_h[:, :, :].bitcast(F32),
                               ALU.subtract).then_inc(w_split, 1)
            pool.memset(keep[:, :], 1.0).then_inc(cleared, 1)
            pool.wait_ge(cleared, 2)
            pool.memset(keep[:, 0:1], 0.0)
            pool.memset(keep[:, META:T:P], 0.0).then_inc(cleared, 1)

        @block.scalar
        def _(act):
            act.wait_ge(w_loaded, 64)
            act.activation(w_h[:, :, :], w_raw[:, :, :], ACT.Copy).then_inc(w_rounded, 1)
            for t in range(6):
                a, z = tile_cols(t)
                act.wait_ge(u_loaded[t % 2], 16 * (t // 2 + 1))
                act.activation(u_h[:, :, a:z], u_in[t % 2][:, :, :z - a], ACT.Copy).then_inc(u_rounded, 1)
            act.wait_ge(step, 1)
            act.activation(scratch[:, :], scratch[:, :], ACT.Exp).then_inc(act_step, 1)
            act.wait_ge(step, 2)
            act.activation(scratch[:, :], scratch[:, :], ACT.Ln).then_inc(act_step, 1)
            act.wait_ge(step, 10)
            act.activation(dec[:, :], dec[:, :], ACT.Exp).then_inc(act_step, 1)
            for c in range(4):
                n = min(PER_BANK, NB - PER_BANK * c)
                act.wait_ge(turned, c + 1)
                act.wait_ge(filled, c + 1)
                src = c_ps[c][:, :96 * n].rearrange("p (b q) -> p b q", q=96)
                bs = slice(PER_BANK * c, PER_BANK * c + n)
                act.activation(head_cols[:, 1, bs, :], src[:, :, 32:32 + H], ACT.Exp)
                act.activation(head_cols[:, 2, bs, :], src[:, :, 64:64 + H], ACT.Exp, scale=-1.0)

        @block.vector
        def _(dve):
            dve.wait_ge(w_loaded, 64)
            for t in range(7):
                if t < 6:
                    a, z = tile_cols(t)
                    dve.wait_ge(u_rounded, t + 1)
                    dve.tensor_tensor(u_l[:, :, a:z], u_in[t % 2][:, :, :z - a], u_h[:, :, a:z].bitcast(F32),
                                      ALU.subtract).then_inc(u_split, 1)
                if t > 0:
                    a, z = tile_cols(t - 1)
                    ps = g_ps[(t - 1) % 2]
                    dve.wait_ge(projected, t)
                    dve.tensor_scalar(log_i[:, a:z], ps[GATE_I:GATE_I + H, :z - a],
                                      bias[GATE_I:GATE_I + H, :], None, ALU.add)
                    dve.tensor_scalar(log_f[:, a:z], ps[GATE_F:GATE_F + H, :z - a],
                                      bias[GATE_F:GATE_F + H, :], None, ALU.add).then_inc(biased, 1)
            dve.wait_ge(biased, 6)
            dve.scalar_tensor_tensor(out=scratch[:, :], in0=log_f[:, :], scalar=-1.0, in1=log_f[:, :],
                                     op0=ALU.mult, op1=ALU.min).then_inc(step, 1)
            dve.wait_ge(act_step, 1)
            dve.tensor_scalar(scratch[:, :], scratch[:, :], 1.0, None, ALU.add).then_inc(step, 1)
            dve.wait_ge(act_step, 2)
            dve.scalar_tensor_tensor(out=log_f[:, :], in0=log_f[:, :], scalar=0.0, in1=scratch[:, :],
                                     op0=ALU.min, op1=ALU.subtract).then_inc(step, 1)
            dve.wait_ge(step, 3)
            dve.wait_ge(cleared, 3)
            dve.tensor_tensor_scan(scratch[:, :], keep[:, :], log_f[:, :], 0.0, ALU.mult, ALU.add).then_inc(step, 1)
            dve.tensor_tensor_scan(rows[64:64 + H, :], log_f[:, :], log_i[:, :], 0.0, ALU.add,
                                   ALU.max).then_inc(step, 1)
            dve.wait_ge(step, 5)
            dve.tensor_tensor(rows[0:H, :], log_i[:, :], scratch[:, :], ALU.subtract).then_inc(step, 1)
            dve.tensor_copy(log_f[:, :], rows[64:64 + H, :]).then_inc(step, 1)
            dve.memset(m_prev[:, 0:1], 0.0)
            dve.tensor_copy(m_prev[:, 1:NB], rows[64:64 + H, META - 1:T - 1:P]).then_inc(step, 1)
            dve.wait_ge(step, 8)
            dve.tensor_tensor(log_i[:, :], scratch[:, :], log_f[:, :], ALU.subtract).then_inc(step, 1)
            dve.wait_ge(step, 9)
            dve.tensor_tensor(dec[:, 0:1], log_i[:, META - 1:META], m_prev[:, 0:1], ALU.add)
            dve.tensor_tensor(dec[:, 1:], log_i[:, META + P - 1:T:P], m_prev[:, 1:], ALU.add).then_inc(step, 1)
            for b in range(NB):
                c = slice(start(b), start(b) + length(b))
                ins = dve.tensor_scalar(rows[32:32 + H, c], log_i[:, c], m_prev[:, b:b + 1], None, ALU.add)
            ins.then_inc(step, 1)
            for c in range(4):
                n = min(PER_BANK, NB - PER_BANK * c)
                dve.wait_ge(turned, c + 1)
                bs = slice(PER_BANK * c, PER_BANK * c + n)
                dve.tensor_copy(head_cols[:, 0, bs, :],
                                c_ps[c][:, :96 * n].rearrange("p (b q) -> p b q", q=96)[:, :, :H]).then_inc(filled, 1)

        @block.tensor
        def _(pe):
            for t in range(6):
                a, z = tile_cols(t)
                pe.wait_ge(u_split, t + 1)
                if t == 0:
                    pe.wait_ge(w_split, 1)
                if t >= 2:
                    pe.wait_ge(biased, t - 1)
                for k in range(KT):
                    last = product(pe, g_ps[t % 2][:64, :z - a], w_h[:, k, :], w_l[:, k, :],
                                   u_h[:, k, a:z], u_l[:, k, a:z], k == 0, k == KT - 1)
                last.then_inc(projected, 1)
            pe.wait_ge(step, 11)
            for b in range(NB):
                c = start(b)
                o = 96 * (b % PER_BANK)
                last = pe.transpose(c_ps[b // PER_BANK][:, o:o + 96], rows[:96, c:c + P], ident[:96, :96])
                if b % PER_BANK == PER_BANK - 1 or b == NB - 1:
                    last.then_inc(turned, 1)


def mlstm(nc, w_in, ident, u_h, u_l, head_cols, row_a, row_dec, y_out):
    VW = B_V + 2
    with ExitStack() as stack:
        ph = Phase(nc, stack, "m")
        raw_qk, raw_v = ph.sb("raw_qk", [P, KT, P]), ph.sb("raw_v", [P, KT, 3 * P])
        wqk_h, wqk_l = ph.sb("wqk_h", [P, KT, P], F32R), ph.sb("wqk_l", [P, KT, P], F32R)
        wv_h, wv_l = ph.sb("wv_h", [P, KT, 3 * P], F32R), ph.sb("wv_l", [P, KT, 3 * P], F32R)
        row = [ph.sb(f"row{r}", [P, TW]) for r in range(2)]
        decay = ph.sb("decay", [B_QK, NB])
        col = ph.sb("col", [P, 3, NB])
        q_h = [ph.sb(f"q_h{r}", [B_QK, TW], F32R) for r in range(2)]
        q_l = [ph.sb(f"q_l{r}", [B_QK, TW], F32R) for r in range(2)]
        k_both = ph.sb("k_both", [P, TW])
        k_f = [k_both[:B_QK, :], k_both[B_QK:, :]]
        ident_of = [ident[:B_QK, :B_QK], ident[B_QK:, B_QK:]]
        k_h = [ph.sb(f"k_h{r}", [B_QK, TW], F32R) for r in range(2)]
        k_l = [ph.sb(f"k_l{r}", [B_QK, TW], F32R) for r in range(2)]
        v_h = [ph.sb(f"v_h{r}", [P, VW], F32R) for r in range(2)]
        v_l = [ph.sb(f"v_l{r}", [P, VW], F32R) for r in range(2)]
        gate = [ph.sb(f"gate{r}", [P, P]) for r in range(2)]
        weight = ph.sb("weight", [P, P])
        score = ph.sb("score", [P, P])
        s_h = [ph.sb(f"s_h{r}", [P, P], F32R) for r in range(2)]
        s_l = [ph.sb(f"s_l{r}", [P, P], F32R) for r in range(2)]
        k_w = ph.sb("k_w", [P, B_QK])
        kw_h = [ph.sb(f"kw_h{r}", [P, B_QK], F32R) for r in range(2)]
        kw_l = [ph.sb(f"kw_l{r}", [P, B_QK], F32R) for r in range(2)]
        state = ph.sb("state", [B_QK, VW])
        state_h, state_l = ph.sb("state_h", [B_QK, VW], F32R), ph.sb("state_l", [B_QK, VW], F32R)
        mix = ph.sb("mix", [P, VW])
        den = ph.sb("den", [P, 3])
        y = [ph.sb(f"y{r}", [P, P]) for r in range(2)]
        bound = ph.sb("bound", [P, P])
        qk_ps, s_ps, kn_ps, grow_ps = ph.ps("qk_ps"), ph.ps("s_ps"), ph.ps("kn_ps"), ph.ps("grow_ps")
        v_ps = [ph.ps(f"v_ps{r}") for r in range(2)]
        mix_ps = [ph.ps(f"mix_ps{r}") for r in range(2)]
        y_stored = ph.sems("y_stored0", "y_stored1")
        row_loaded = ph.sems("row_loaded0", "row_loaded1")
        qk_loaded, v_loaded, decay_loaded, set_up = ph.sems("qk_loaded", "v_loaded", "decay_loaded", "set_up")
        PE_SEMS = qk_projected, v_projected, scored, k_turned, mixed, grown = ph.sems(
            "qk_projected", "v_projected", "scored", "k_turned", "mixed", "grown")
        ACT_SEMS = (wqk_rounded, wv_rounded, q_rounded, k_rounded, k_copied, v_rounded, og_tanh, weighed,
                    s_rounded, kw_rounded, state_rounded) = ph.sems(
            "wqk_rounded", "wv_rounded", "q_rounded", "k_rounded", "k_copied", "v_rounded", "og_tanh", "weighed",
            "s_rounded", "kw_rounded", "state_rounded")
        DVE_SEMS = (wv_split_dve, col_copied, qk_split, v_split, bounded, z_gated, gated, scaled, s_split, k_weighed,
                    kw_split, grown_state, state_split, summed, den_abs, den_max, inverted, y_made) = ph.sems(
            "wv_split_dve", "col_copied", "qk_split", "v_split", "bounded", "z_gated", "gated", "scaled", "s_split",
            "k_weighed", "kw_split", "grown_state", "state_split", "summed", "den_abs", "den_max", "inverted",
            "y_made")
        POOL_SEMS = wqk_split, wv_split_pool = ph.sems("wqk_split", "wv_split_pool")
        waits_met_pe, waits_met_sp = ph.sems("waits_met_pe", "waits_met_sp")
        block = ph.block()

        def before(count, b):
            return PRE + count + (b if b == 0 else b - 1)

        def tile_used(i, t):
            return PRE + 17 * i + (15, 0, 3, 6, 9, 12)[t]

        def in_tile(b):
            c = start(b) - tile_cols(b // 3)[0]
            return slice(c, c + length(b))

        @block.sync
        def _(sp):
            for sem in y_stored:
                sp.sem_inc(sem, 16)

            def load_weights(unit, head):
                src = w_in.rearrange("(k p) n -> p k n", p=P)
                sp.wait_ge(wqk_split, PRE + unit)
                sp.sem_inc(waits_met_sp, 1)
                for j, at in enumerate((0, B_K0)):
                    sp.dma_start(raw_qk[:, :, B_QK * j:B_QK * j + B_QK],
                                 src[:, :, bass.ds(head * B_QK + at, B_QK)]).then_inc(qk_loaded, 16)
                sp.wait_ge(wv_split_pool, PRE + 2 * unit)
                sp.wait_ge(wv_split_dve, PRE + 2 * unit)
                sp.sem_inc(waits_met_sp, 1)
                for j, at in enumerate((B_V0, B_O0, B_Z0)):
                    sp.dma_start(raw_v[:, :, P * j:P * j + P],
                                 src[:, :, bass.ds(head * P + at, P)]).then_inc(v_loaded, 16)

            def load_row(i, t):
                a, z = tile_cols(t)
                sp.wait_ge(bounded, PRE + 17 * i + (-2, 0, 3, 6, 9, 12)[t])
                sp.sem_inc(waits_met_sp, 1)
                sp.dma_start(row[t % 2][:, :z - a],
                             row_a[bass.ds(i * T + a, z - a)].partition_broadcast(P)).then_inc(row_loaded[t % 2], 16)

            load_weights(0, 0)
            with sp.Fori(0, B_HEADS) as i:
                load_row(i, 0)
                sp.wait_ge(grown_state, PRE + 16 * i)
                sp.sem_inc(waits_met_sp, 1)
                sp.dma_start(decay[:, :], row_dec[bass.ds(i * NB, NB)].partition_broadcast(B_QK)
                             ).then_inc(decay_loaded, 16)
                load_row(i, 1)
                load_weights(i + 1, (i + 1) % B_HEADS)
                for s in range(20):
                    if s in (3, 6, 9, 12):
                        load_row(i, s // 3 + 1)
                    b = s - 3
                    if b >= 0:
                        sp.wait_ge(y_made, PRE + 17 * i + b + 1)
                        sp.dma_start(y_out[start(b):start(b) + length(b), bass.ds(i * P, P)],
                                     y[b % 2][:length(b), :]).then_inc(y_stored[b % 2], 16)
            sp.wait_ge(y_stored[0], 16 * (1 + 9 * B_HEADS))
            sp.wait_ge(y_stored[1], 16 * (1 + 8 * B_HEADS))

        @block.gpsimd
        def _(pool):
            for sem in POOL_SEMS:
                pool.sem_inc(sem, PRE)
            for r in range(2):
                pool.memset(v_h[r][:, :].bitcast(F32), 0.0)
                pool.memset(v_l[r][:, :].bitcast(F32), 0.0).then_inc(set_up, 1)
            pool.memset(bound[:, :], 0.0).then_inc(set_up, 1)
            pool.wait_ge(set_up, 3)
            for r in range(2):
                pool.memset(v_h[r][:, B_V:B_V + 1].bitcast(F32), 1.0)
            pool.affine_select(out=bound[:, :], in_=bound[:, :], compare_op=ALU.is_ge, fill=MASKED, base=0,
                               pattern=[[1, P]], channel_multiplier=-1).then_inc(set_up, 1)

            def split_qk(unit):
                pool.wait_ge(wqk_rounded, PRE + unit + 1)
                pool.tensor_tensor(wqk_l[:, :, :], raw_qk[:, :, :], wqk_h[:, :, :].bitcast(F32),
                                   ALU.subtract).then_inc(wqk_split, 1)

            def split_v(unit):
                for n, ks in ((2, slice(2, 4)), (4, slice(6, 8))):
                    pool.wait_ge(wv_rounded, PRE + 4 * unit + n)
                    pool.tensor_tensor(wv_l[:, ks, :], raw_v[:, ks, :], wv_h[:, ks, :].bitcast(F32),
                                       ALU.subtract).then_inc(wv_split_pool, 1)

            split_qk(0)
            split_v(0)
            with pool.Fori(0, B_HEADS) as i:
                split_qk(i + 1)
                split_v(i + 1)

        @block.scalar
        def _(act):
            for sem in ACT_SEMS:
                act.sem_inc(sem, PRE)

            def round_qk_weights(unit):
                act.wait_ge(qk_loaded, 32 * (unit + 1))
                act.wait_ge(qk_projected, PRE + 6 * unit)
                act.activation(wqk_h[:, :, :], raw_qk[:, :, :], ACT.Copy).then_inc(wqk_rounded, 1)

            def round_v_weights(unit):
                act.wait_ge(v_loaded, 48 * (unit + 1))
                act.wait_ge(v_projected, PRE + 17 * unit)
                for n in range(4):
                    ks = slice(2 * n, 2 * n + 2)
                    act.activation(wv_h[:, ks, :], raw_v[:, ks, :], ACT.Copy).then_inc(wv_rounded, 1)

            def round_qk(i, t, m):
                w, r = tile_cols(t)[1] - tile_cols(t)[0], t % 2
                act.wait_ge(qk_projected, PRE + m + 1)
                if i is not None:
                    act.wait_ge(mixed, tile_used(i, t))
                act.activation(q_h[r][:, :w], qk_ps[:B_QK, :w], ACT.Copy)
                act.activation(k_f[r][:, :w], qk_ps[B_QK:, :w], ACT.Copy, scale=B_QK ** -0.5).then_inc(k_copied, 1)
                act.wait_ge(k_copied, PRE + m + 1)
                act.activation(k_h[r][:, :w], k_f[r][:, :w], ACT.Copy).then_inc(k_rounded, 1)

            round_qk_weights(0)
            round_v_weights(0)
            act.wait_ge(set_up, 4)
            round_qk(None, 0, 0)
            with act.Fori(0, B_HEADS) as i:
                for s in range(18):
                    r, m = s % 2, length(s)
                    if s < NB:
                        act.wait_ge(v_projected, PRE + 17 * i + s + 1)
                        act.wait_ge(mixed, before(17 * i, s))
                        act.wait_ge(grown, before(16 * i, s))
                        act.activation(v_h[r][:m, :B_V], v_ps[r][:m, :B_V], ACT.Copy).then_inc(v_rounded, 1)
                        act.wait_ge(y_made, before(17 * i, s))
                        o, z = v_ps[r][:m, B_V:2 * B_V], v_ps[r][:m, 2 * B_V:3 * B_V]
                        act.activation(o, o, ACT.Tanh, scale=0.5)
                        act.activation(gate[r][:m, :], z, ACT.Tanh, scale=0.5).then_inc(og_tanh, 1)
                        act.wait_ge(bounded, PRE + 17 * i + s + 1)
                        act.activation(weight[:m, :m], weight[:m, :m], ACT.Exp).then_inc(weighed, 1)
                    if s >= 2:
                        act.wait_ge(grown_state, PRE + 16 * i + s - 1)
                        act.wait_ge(mixed, PRE + 17 * i + s - 1)
                        act.activation(state_h[:, :], state[:, :], ACT.Copy).then_inc(state_rounded, 1)
                    if s < NB:
                        act.wait_ge(scaled, PRE + 17 * i + s + 1)
                        act.activation(s_h[r][:m, :m], score[:m, :m], ACT.Copy).then_inc(s_rounded, 1)
                    if s < NB - 1:
                        act.wait_ge(k_weighed, PRE + 16 * i + s + 1)
                        act.activation(kw_h[r][:m, :], k_w[:m, :], ACT.Copy).then_inc(kw_rounded, 1)
                    if s % 3 == 2:
                        round_qk(i, (s // 3 + 1) % 6, 6 * i + s // 3 + 1)
                    if s == 14:
                        round_qk_weights(i + 1)
                    if s == 17:
                        round_v_weights(i + 1)

        @block.vector
        def _(dve):
            for sem in DVE_SEMS:
                dve.sem_inc(sem, PRE)

            def split_v_weights(unit):
                for n, ks in ((1, slice(0, 2)), (3, slice(4, 6))):
                    dve.wait_ge(wv_rounded, PRE + 4 * unit + n)
                    dve.tensor_tensor(wv_l[:, ks, :], raw_v[:, ks, :], wv_h[:, ks, :].bitcast(F32),
                                      ALU.subtract).then_inc(wv_split_dve, 1)

            def split_qk(t, m):
                w, r = tile_cols(t)[1] - tile_cols(t)[0], t % 2
                dve.wait_ge(k_rounded, PRE + m + 1)
                dve.tensor_tensor(q_l[r][:, :w], qk_ps[:B_QK, :w], q_h[r][:, :w].bitcast(F32), ALU.subtract)
                dve.scalar_tensor_tensor(out=k_l[r][:, :w], in0=qk_ps[B_QK:, :w], scalar=B_QK ** -0.5,
                                         in1=k_h[r][:, :w].bitcast(F32), op0=ALU.mult,
                                         op1=ALU.subtract).then_inc(qk_split, 1)

            def grow(i, b):
                dve.wait_ge(grown, PRE + 16 * i + b + 1)
                dve.wait_ge(state_split, PRE + 16 * i + b)
                if b == 0:
                    ins = dve.tensor_copy(state[:, :], grow_ps[:B_QK, :VW])
                else:
                    dve.wait_ge(grown_state, PRE + 16 * i + b)
                    ins = dve.scalar_tensor_tensor(out=state[:, :], in0=state[:, :], scalar=decay[:, b:b + 1],
                                                   in1=grow_ps[:B_QK, :VW], op0=ALU.mult, op1=ALU.add)
                ins.then_inc(grown_state, 1)

            def split_state(i, b):
                dve.wait_ge(state_rounded, PRE + 16 * i + b + 1)
                dve.tensor_tensor(state_l[:, :], state[:, :], state_h[:, :].bitcast(F32),
                                  ALU.subtract).then_inc(state_split, 1)

            def make_y(i, b):
                m, r = length(b), b % 2
                n = 17 * i + b
                dve.wait_ge(mixed, PRE + n + 1)
                dve.wait_ge(y_made, PRE + n)
                if b == 0:
                    ins = dve.tensor_copy(mix[:m, :B_V + 1], mix_ps[r][:m, :B_V + 1])
                else:
                    ins = dve.tensor_scalar(mix[:m, :B_V + 1], mix_ps[r][:m, 256:256 + B_V + 1],
                                            col[:m, 1, b:b + 1], None, ALU.mult)
                ins.then_inc(summed, 1)
                dve.wait_ge(summed, PRE + 2 * n + 1)
                if b == 0:
                    dve.sem_inc(summed, 1)
                else:
                    dve.tensor_tensor(mix[:m, :B_V + 1], mix[:m, :B_V + 1], mix_ps[r][:m, :B_V + 1],
                                      ALU.add).then_inc(summed, 1)
                dve.wait_ge(summed, PRE + 2 * n + 2)
                dve.scalar_tensor_tensor(out=den[:m, 0:1], in0=mix[:m, B_V:B_V + 1], scalar=-1.0,
                                         in1=mix[:m, B_V:B_V + 1], op0=ALU.mult, op1=ALU.max).then_inc(den_abs, 1)
                dve.wait_ge(den_abs, PRE + n + 1)
                dve.tensor_scalar(den[:m, 1:2], den[:m, 0:1], col[:m, 2, b:b + 1], 4.0, ALU.max,
                                  ALU.mult).then_inc(den_max, 1)
                dve.wait_ge(den_max, PRE + n + 1)
                dve.reciprocal(den[:m, 2:3], den[:m, 1:2]).then_inc(inverted, 1)
                dve.wait_ge(inverted, PRE + n + 1)
                dve.wait_ge(y_stored[r], 16 * (1 + (9 - r) * i + b // 2))
                dve.scalar_tensor_tensor(out=y[r][:m, :], in0=mix[:m, :B_V], scalar=den[:m, 2:3],
                                         in1=gate[r][:m, :], op0=ALU.mult, op1=ALU.mult).then_inc(y_made, 1)

            split_v_weights(0)
            dve.wait_ge(set_up, 4)
            split_qk(0, 0)
            with dve.Fori(0, B_HEADS) as i:
                for s in range(19):
                    r, m, n = s % 2, length(s), 17 * i + s
                    if s < NB:
                        if s == 0:
                            dve.wait_ge(y_made, PRE + 17 * i)
                            dve.tensor_copy(col[:, :, :], head_cols[:, :, :, bass.ds(i, 1)].rearrange(
                                "p q b o -> p q (b o)")).then_inc(col_copied, 1)
                            dve.wait_ge(col_copied, PRE + i + 1)
                        if s % 3 == 0:
                            t = s // 3
                            dve.wait_ge(row_loaded[t % 2], 16 * (3 * i + t // 2 + 1))
                        dve.wait_ge(scaled, PRE + n)
                        dve.wait_ge(k_weighed, PRE + 16 * i + min(s, 16))
                        dve.scalar_tensor_tensor(out=weight[:m, :m], in0=row[(s // 3) % 2][:m, in_tile(s)],
                                                 scalar=col[:m, 0, s:s + 1], in1=bound[:m, :m],
                                                 op0=ALU.add, op1=ALU.min).then_inc(bounded, 1)
                    if s == 2:
                        dve.wait_ge(decay_loaded, 16 * (i + 1))
                    if 0 <= s - 2 < NB - 1:
                        grow(i, s - 2)
                    if 0 <= s - 2 < NB:
                        make_y(i, s - 2)
                    if s < NB:
                        dve.wait_ge(og_tanh, PRE + n + 1)
                        dve.wait_ge(mixed, before(17 * i, s))
                        dve.wait_ge(grown, before(16 * i, s))
                        dve.tensor_tensor(v_l[r][:m, :B_V], v_ps[r][:m, :B_V], v_h[r][:m, :B_V].bitcast(F32),
                                          ALU.subtract).then_inc(v_split, 1)
                        dve.scalar_tensor_tensor(out=gate[r][:m, :], in0=gate[r][:m, :], scalar=1.0,
                                                 in1=v_ps[r][:m, 2 * P:3 * P], op0=ALU.add,
                                                 op1=ALU.mult).then_inc(z_gated, 1)
                        dve.wait_ge(z_gated, PRE + n + 1)
                        dve.scalar_tensor_tensor(out=gate[r][:m, :], in0=v_ps[r][:m, P:2 * P], scalar=1.0,
                                                 in1=gate[r][:m, :], op0=ALU.add, op1=ALU.mult).then_inc(gated, 1)
                        dve.wait_ge(weighed, PRE + n + 1)
                        dve.wait_ge(scored, PRE + n + 1)
                        dve.wait_ge(s_split, PRE + n)
                        dve.tensor_tensor(score[:m, :m], s_ps[:m, :m], weight[:m, :m], ALU.mult
                                          ).then_inc(scaled, 1)
                    if s < NB - 1:
                        dve.wait_ge(k_turned, PRE + 16 * i + s + 1)
                        dve.wait_ge(kw_split, PRE + 16 * i + s)
                        dve.tensor_scalar(k_w[:m, :], kn_ps[:m, :B_QK], weight[:m, m - 1:m], None,
                                          ALU.mult).then_inc(k_weighed, 1)
                    if 0 <= s - 2 < NB - 1:
                        split_state(i, s - 2)
                    if s < NB:
                        dve.wait_ge(s_rounded, PRE + n + 1)
                        dve.tensor_tensor(s_l[r][:m, :m], score[:m, :m], s_h[r][:m, :m].bitcast(F32),
                                          ALU.subtract).then_inc(s_split, 1)
                    if s < NB - 1:
                        dve.wait_ge(kw_rounded, PRE + 16 * i + s + 1)
                        dve.tensor_tensor(kw_l[r][:m, :], k_w[:m, :], kw_h[r][:m, :].bitcast(F32),
                                          ALU.subtract).then_inc(kw_split, 1)
                    if s % 3 == 2:
                        split_qk((s // 3 + 1) % 6, 6 * i + s // 3 + 1)
                    if s == 17:
                        split_v_weights(i + 1)

        @block.tensor
        def _(pe):
            for sem in PE_SEMS:
                pe.sem_inc(sem, PRE)

            def project_qk(m, t, ks):
                a, z = tile_cols(t)
                if ks[0] == 0:
                    pe.wait_ge(qk_split, PRE + m)
                for k in ks:
                    last = product(pe, qk_ps[:, :z - a], wqk_h[:, k, :], wqk_l[:, k, :], u_h[:, k, a:z],
                                   u_l[:, k, a:z], k == 0, k == KT - 1)
                if ks[-1] == KT - 1:
                    last.then_inc(qk_projected, 1)

            def project_v(i, b):
                m, r = length(b), b % 2
                c = slice(start(b), start(b) + m)
                pe.wait_ge(gated, before(17 * i, b))
                for k in range(KT):
                    if b == 0 and k % 2 == 0:
                        split, n = (wv_split_dve, wv_split_pool)[k // 2 % 2], k // 4 + 1
                        pe.wait_ge(split, PRE + 2 * i + n)
                    last = product(pe, v_ps[r][:m, :3 * P], u_h[:, k, c], u_l[:, k, c], wv_h[:, k, :], wv_l[:, k, :],
                                   k == 0, k == KT - 1)
                last.then_inc(v_projected, 1)

            pe.wait_ge(wqk_split, PRE + 1)
            project_qk(0, 0, range(KT))
            with pe.Fori(0, B_HEADS) as i:
                for s in range(18):
                    r, m, n = s % 2, length(s), 17 * i + s
                    if s < NB:
                        project_v(i, s)
                        if s % 3 == 0:
                            pe.wait_ge(qk_split, PRE + 6 * i + s // 3 + 1)
                        pe.wait_ge(scaled, PRE + n)
                        if s == 0:
                            pe.sem_inc(waits_met_pe, 1)
                        tr, c = (s // 3) % 2, in_tile(s)
                        product(pe, s_ps[:m, :m], k_h[tr][:, c], k_l[tr][:, c], q_h[tr][:, c], q_l[tr][:, c],
                                True, True).then_inc(scored, 1)
                    if s < NB - 1:
                        pe.wait_ge(k_weighed, PRE + 16 * i + s)
                        pe.sem_inc(waits_met_pe, 1)
                        pe.transpose(kn_ps[:m, :B_QK], k_f[tr][:, c], ident_of[tr]).then_inc(k_turned, 1)
                    if s == 15:
                        pe.wait_ge(wqk_split, PRE + i + 2)
                    project_qk(6 * i + s // 3 + 1, (s // 3 + 1) % 6, (range(0, 3), range(3, 6), range(6, 8))[s % 3])
                    if s > 0:
                        b, q = s - 1, 1 - r
                        m, n = length(b), n - 1
                        tr, c = (b // 3) % 2, in_tile(b)
                        pe.wait_ge(s_split, PRE + n + 1)
                        pe.wait_ge(summed, PRE + 34 * i + 2 * (b if b == 0 else b - 1))
                        if b == 0:
                            pe.sem_inc(waits_met_pe, 1)
                        last = product(pe, mix_ps[q][:m, :VW], s_h[q][:m, :m], s_l[q][:m, :m], v_h[q][:m, :],
                                       v_l[q][:m, :], True, True)
                        if b > 0:
                            pe.wait_ge(state_split, PRE + 16 * i + b)
                            last = product(pe, mix_ps[q][:m, 256:256 + VW], q_h[tr][:, c], q_l[tr][:, c],
                                           state_h[:, :], state_l[:, :], True, True)
                        last.then_inc(mixed, 1)
                        if b < NB - 1:
                            pe.wait_ge(kw_split, PRE + 16 * i + b + 1)
                            pe.wait_ge(grown_state, PRE + 16 * i + b)
                            if b == 0:
                                pe.sem_inc(waits_met_pe, 1)
                            product(pe, grow_ps[:B_QK, :VW], kw_h[q][:m, :], kw_l[q][:m, :], v_h[q][:m, :],
                                    v_l[q][:m, :], True, True).then_inc(grown, 1)


def decoder(nc, x, meta, norm_a, w_in_a, sinks_a, w_out_a, norm_b, w_in_b, b_gates_b, w_out_b, norm_f, rope_table,
            out):
    x, out = x[0], out[0]
    y_t = nc.dram_tensor("y_t", [D, T], F32).ap()
    h1 = nc.dram_tensor("h1", [T, D], F32).ap()
    u_t = nc.dram_tensor("u_t", [D, T], F32).ap()
    y_b = nc.dram_tensor("y_b", [T, D], F32).ap()
    row_a = nc.dram_tensor("row_a", [B_HEADS * T], F32).ap()
    row_dec = nc.dram_tensor("row_dec", [B_HEADS * NB], F32).ap()
    with ExitStack() as stack:
        ident = stack.enter_context(nc.sbuf_tensor("ident", [P, P], F32))
        ident_made = stack.enter_context(nc.semaphore("ident_made"))
        with nc.Block() as block:
            @block.gpsimd
            def _(pool):
                pool.memset(ident[:, :], 0.0).then_inc(ident_made, 1)
                pool.wait_ge(ident_made, 1)
                pool.affine_select(out=ident[:, :], in_=ident[:, :], compare_op=ALU.not_equal, fill=1.0, base=0,
                                   pattern=[[-1, P]], channel_multiplier=1).then_inc(ident_made, 1)

        def u_tiles(inner, layer):
            return [inner.enter_context(nc.sbuf_tensor(f"u{layer}_{part}", [P, KT, T], F32R)) for part in "hl"]

        with ExitStack() as inner:
            u_h, u_l = u_tiles(inner, 0)
            norm_in(nc, x, meta, norm_a[0], ident, u_h, u_l)
            attention(nc, w_in_a[0], sinks_a[0], rope_table, ident, u_h, u_l, y_t)
        project_out(nc, "pa", w_out_a[0], y_t,
                    lambda n: meta if isinstance(n, int) and n == 0 else x[bass.ds(P * n - P, P), :],
                    norm_b[0], ident, (h1, u_t))
        with ExitStack() as inner:
            u_h, u_l = u_tiles(inner, 1)
            head_cols = inner.enter_context(nc.sbuf_tensor("head_cols", [P, 3, NB, B_HEADS], F32))
            gates(nc, u_t, w_in_b[0], b_gates_b[0], ident, u_h, u_l, head_cols, row_a, row_dec)
            mlstm(nc, w_in_b[0], ident, u_h, u_l, head_cols, row_a, row_dec, y_b)
        project_out(nc, "pb", w_out_b[0], y_b, lambda n: h1[bass.ds(P * n + META, P), :], norm_f, ident, (out,))


def rope_constants():
    import numpy as np
    half = A_HD // 2
    inv = np.float32(10000.0) ** (-np.arange(half, dtype=np.float32) / np.float32(half))
    angle = (np.arange(T, dtype=np.float32)[None, :] * inv[:, None].astype(np.float32)).astype(np.float32)
    table = np.empty((P // half, half, 2, T), np.float32)
    table[:, :, 0] = np.cos(angle)
    table[0::2, :, 1] = -np.sin(angle)
    table[1::2, :, 1] = np.sin(angle)
    return table.reshape(P, 2, T)


_INS = ["x", "meta", "norm_a", "w_in_a", "sinks_a", "w_out_a", "norm_b", "w_in_b", "b_gates_b", "w_out_b", "norm_f"]


def kernel(**inputs):
    import numpy as np
    from concourse import bacc
    from concourse.bass_utils import run_bass_kernel_spmd

    nc = bacc.Bacc("TRN2", target_bir_lowering=False, num_devices=1)
    arrays = {f"in_{name}": np.ascontiguousarray(inputs[name]) for name in _INS}
    arrays["in_rope"] = rope_constants()
    args = [nc.dram_tensor(name, a.shape, mybir.dt.from_np(a.dtype), kind="ExternalInput").ap()
            for name, a in arrays.items()]
    args.append(nc.dram_tensor("out_dram", (1, SEQ, D), F32, kind="ExternalOutput").ap())
    decoder(nc, *args)
    return run_bass_kernel_spmd(nc, [arrays], core_ids=[0]).results[0]["out_dram"]
```

```python
from contextlib import ExitStack

import concourse.bass as bass
from concourse import mybir

F32 = mybir.dt.float32
F32R = mybir.dt.float32r
ALU = mybir.AluOpType
ACT = mybir.ActivationFunctionType

P = 128
D = 1024
KT = D // P
META = 16
SEQ = 2048
T = META + SEQ
NB = 1 + SEQ // P
EPS = 1e-6

A_HEADS, A_KV, A_HD = 16, 2, 64
A_PAIRS = A_HEADS // 2
A_K0 = A_HEADS * A_HD
A_V0 = A_K0 + A_KV * A_HD
A_Z0 = A_V0 + A_KV * A_HD
MASKED = -1.0e30

B_HEADS, B_QK, B_V = 8, 64, 128
B_K0 = B_HEADS * B_QK
B_V0 = 2 * B_HEADS * B_QK
B_O0 = B_V0 + B_HEADS * B_V
B_Z0 = B_O0 + B_HEADS * B_V
B_G0 = B_Z0 + B_HEADS * B_V

TILES = [(3 * t, min(3 * t + 3, NB)) for t in range(6)]
TW = 3 * P
PRE = 3


def start(b):
    return 0 if b == 0 else META + P * (b - 1)


def length(b):
    return META if b == 0 else P


def tile_cols(t):
    b0, b1 = TILES[t]
    return start(b0), start(b1 - 1) + length(b1 - 1)


class Phase:

    def __init__(self, nc, stack, name):
        self.nc, self.stack, self.name, self.all_sems = nc, stack, name, []

    def sb(self, name, shape, dtype=F32):
        return self.stack.enter_context(self.nc.sbuf_tensor(f"{self.name}_{name}", shape, dtype))

    def ps(self, name):
        return self.stack.enter_context(self.nc.psum_tensor(f"{self.name}_{name}", [P, 512], F32))

    def sems(self, *names):
        new = [self.stack.enter_context(self.nc.semaphore(f"{self.name}_{n}")) for n in names]
        self.all_sems += new
        return new

    def block(self):
        self.stack.callback(self.clear)
        return self.stack.enter_context(self.nc.Block())

    def clear(self):
        with self.nc.Block() as block:
            @block.sync
            def _(sp):
                for sem in self.all_sems:
                    sp.sem_clear(sem)


def product(pe, out, a_h, a_l, b_h, b_l, first, last):
    pe.matmul(out, a_h, b_h, start=first, stop=False)
    pe.matmul(out, a_l, b_h, start=False, stop=False)
    return pe.matmul(out, a_h, b_l, start=False, stop=last)


def over_blocks(eng, step, lags):
    for n in range(3):
        step(n, n % 2)
    with eng.Fori(0, (NB - 3) // 2) as i:
        step(3 + 2 * i, 1)
        step(4 + 2 * i, 0)
    for n in range(NB, NB + lags):
        step(n, n % 2)


def has(n, lag=0):
    return not isinstance(n, int) or 0 <= n - lag < NB


def size(n):
    return length(n) if isinstance(n, int) else P


def cols(n):
    return bass.ds(start(n), length(n)) if isinstance(n, int) else bass.ds(P * n - (P - META), P)


def norm_in(nc, x, meta, norm_g, ident, u_h, u_l):
    with ExitStack() as stack:
        ph = Phase(nc, stack, "n")
        x_in = [ph.sb(f"x{p}", [P, D]) for p in range(2)]
        xs = [ph.sb(f"xs{p}", [P, D]) for p in range(2)]
        gain = ph.sb("gain", [P, D])
        squares = ph.sb("squares", [P, D])
        stat = ph.sb("stat", [P, 6])
        eps = ph.sb("eps", [P, 1])
        turned = [[ph.ps(f"turned{p}{half}") for half in range(2)] for p in range(2)]
        x_loaded = ph.sems("x_loaded0", "x_loaded1")
        consts, gain_loaded, summed, rooted, inverted, scaled, transposed, rounded, remaindered = ph.sems(
            "consts", "gain_loaded", "summed", "rooted", "inverted", "scaled", "transposed", "rounded",
            "remaindered")
        block = ph.block()

        @block.sync
        def _(sp):
            sp.dma_start(gain[:, :], norm_g.partition_broadcast(P)
                         ).then_inc(gain_loaded, 16)

            def step(n, p):
                if not isinstance(n, int) or n >= 2:
                    sp.wait_ge(scaled, n - 1)
                src = meta if isinstance(n, int) and n == 0 else x[bass.ds(P * n - P, P), :]
                sp.dma_start(x_in[p][:size(n), :], src).then_inc(x_loaded[p], 16)
            over_blocks(sp, step, 0)

        @block.gpsimd
        def _(pool):
            pool.memset(eps[:, :], EPS).then_inc(consts, 1)

        @block.scalar
        def _(act):
            act.wait_ge(consts, 1)

            def step(n, p):
                if has(n):
                    m = size(n)
                    act.wait_ge(x_loaded[p], 16 * ((n // 2) + 1 if isinstance(n, int) else 1) if isinstance(n, int)
                                else 8 * n + (8 if p else 16))
                    if not isinstance(n, int) or n >= 1:
                        act.wait_ge(rooted, n)
                    if not isinstance(n, int) or n >= 2:
                        act.wait_ge(inverted, n - 1)
                    act.activation(squares[:m, :], x_in[p][:m, :], ACT.Square,
                                   accum_out=stat[:m, 3 * p:3 * p + 1]).then_inc(summed, 1)
                    act.wait_ge(summed, n + 1)
                    act.activation(stat[:m, 3 * p + 1:3 * p + 2], stat[:m, 3 * p:3 * p + 1], ACT.Sqrt,
                                   bias=eps[:m, :], scale=1.0 / D).then_inc(rooted, 1)
                if has(n, 1):
                    q = 1 - p
                    m = size(n - 1) if isinstance(n, int) else P
                    act.wait_ge(transposed, n)
                    for half in range(2):
                        src = turned[q][half][:, :].rearrange("p (k t) -> p k t", k=4)[:, :, :m]
                        act.activation(u_h[:, 4 * half:4 * half + 4, cols(n - 1)], src,
                                       ACT.Copy).then_inc(rounded, 1)
            over_blocks(act, step, 1)

        @block.vector
        def _(dve):
            dve.wait_ge(gain_loaded, 16)

            def step(n, p):
                if has(n):
                    m = size(n)
                    dve.wait_ge(rooted, n + 1)
                    if not isinstance(n, int) or n >= 2:
                        dve.wait_ge(transposed, n - 1)
                    dve.reciprocal(stat[:m, 3 * p + 2:3 * p + 3],
                                   stat[:m, 3 * p + 1:3 * p + 2]).then_inc(inverted, 1)
                    dve.wait_ge(inverted, n + 1)
                    dve.scalar_tensor_tensor(out=xs[p][:m, :], in0=x_in[p][:m, :],
                                             scalar=stat[:m, 3 * p + 2:3 * p + 3], in1=gain[:m, :],
                                             op0=ALU.mult, op1=ALU.mult).then_inc(scaled, 1)
                if has(n, 1):
                    q = 1 - p
                    m = size(n - 1) if isinstance(n, int) else P
                    dve.wait_ge(rounded, 2 * n)
                    for half in range(2):
                        src = turned[q][half][:, :].rearrange("p (k t) -> p k t", k=4)[:, :, :m]
                        ks = slice(4 * half, 4 * half + 4)
                        dve.tensor_tensor(u_l[:, ks, cols(n - 1)], src,
                                          u_h[:, ks, cols(n - 1)].bitcast(F32),
                                          ALU.subtract).then_inc(remaindered, 1)
            over_blocks(dve, step, 1)

        @block.tensor
        def _(pe):
            def step(n, p):
                m = size(n)
                pe.wait_ge(scaled, n + 1)
                if not isinstance(n, int) or n >= 2:
                    pe.wait_ge(remaindered, 2 * (n - 1))
                for k in range(KT):
                    last = pe.transpose(turned[p][k // 4][:, (k % 4) * P:(k % 4) * P + m],
                                        xs[p][:m, k * P:(k + 1) * P], ident[:m, :m])
                last.then_inc(transposed, 1)
            over_blocks(pe, step, 0)


def attention(nc, w_in, sinks, rope_table, ident, u_h, u_l, y_t):
    with ExitStack() as stack:
        ph = Phase(nc, stack, "a")
        k_h, k_l = ph.sb("k_h", [P, T], F32R), ph.sb("k_l", [P, T], F32R)
        v_h, v_l = ph.sb("v_h", [P, NB, P], F32R), ph.sb("v_l", [P, NB, P], F32R)
        raw = [ph.sb(f"raw{h}", [P, KT // 2, P]) for h in range(2)]
        w_h = {n: ph.sb(f"w{n}_h", [P, KT, P], F32R) for n in ("q", "z")}
        w_l = {n: ph.sb(f"w{n}_l", [P, KT, P], F32R) for n in ("q", "z")}
        rope = ph.sb("rope", [P, 2, TW])
        q_f, q_s = ph.sb("q_f", [P, TW]), ph.sb("q_s", [P, TW])
        q_h = [ph.sb(f"q_h{r}", [P, TW], F32R) for r in range(2)]
        q_l = [ph.sb(f"q_l{r}", [P, TW], F32R) for r in range(2)]
        gate = [ph.sb(f"gate{r}", [P, TW]) for r in range(2)]
        prob = [ph.sb(f"prob{r}", [P, 2, 1 + 2 * P]) for r in range(2)]
        pt_h, pt_l = ph.sb("pt_h", [P, 512], F32R), ph.sb("pt_l", [P, 512], F32R)
        y = [ph.sb(f"y{r}", [P, P]) for r in range(2)]
        mask = ph.sb("mask", [P, 2 * P])
        neg_sink = ph.sb("neg_sink", [P, A_HEADS])
        sink = ph.sb("sink", [P, 2])
        stat = [ph.sb(f"stat{r}", [P, 6]) for r in range(2)]
        NEG, SUM, INV = (slice(2 * n, 2 * n + 2) for n in range(3))
        q_ps, z_ps = ph.ps("q_ps"), ph.ps("z_ps")
        s_ps = [ph.ps(f"s_ps{e}") for e in range(2)]
        pt_ps = [ph.ps(f"pt_ps{r}") for r in range(2)]
        o_ps = [ph.ps(f"o_ps{r}") for r in range(2)]
        raw_loaded = ph.sems("raw_loaded0", "raw_loaded1")
        y_stored = ph.sems("y_stored0", "y_stored1")
        (sinks_loaded, sinks_negated, mask_made, table_loaded) = ph.sems(
            "sinks_loaded", "sinks_negated", "mask_made", "table_loaded")
        PE_SEMS = q_projected, z_projected, scored, turned, weighed, v_turned = ph.sems(
            "q_projected", "z_projected", "scored", "turned", "weighed", "v_turned")
        ACT_SEMS = w_rounded, swapped, q_rounded, z_tanh, exped, pt_rounded, v_copied, v_rounded = ph.sems(
            "w_rounded", "swapped", "q_rounded", "z_tanh", "exped", "pt_rounded", "v_copied", "v_rounded")
        (roped, roped_cos, q_split, gated, sink_set, maxed, inverted, normalised, pt_split,
         y_made, v_split) = DVE_SEMS = ph.sems(
            "roped", "roped_cos", "q_split", "gated", "sink_set", "maxed", "inverted",
            "normalised", "pt_split", "y_made", "v_split")
        POOL_SEMS = w_split, roped_sin = ph.sems("w_split", "roped_sin")
        waits_met_pe, waits_met_dve, waits_met_sp = ph.sems("waits_met_pe", "waits_met_dve", "waits_met_sp")
        block = ph.block()

        tile_of = lambda b: b // 3
        key0 = lambda b: start(max(b - 1, 0))
        keys = lambda b: start(b) + length(b) - key0(b)
        mask_at = lambda b: (P, P - META, 0)[min(b, 2)]

        def chunks(b):
            out = [] if b == 0 else [(0, length(b - 1), b - 1)]
            return out + [(keys(b) - length(b), length(b), b)]

        def before(n_blocks, b):
            return PRE + n_blocks + (b if b == 0 else b - 1)

        def read_count(i, t):
            return PRE + 17 * i + (15, 0, 3, 6, 9, 12)[t]

        def pt_parts(b, dst):
            ps = pt_ps[b % 2]
            if b >= 2:
                return [(0, 0, dst[:, :], ps[:, :], True)]
            view = lambda x, c, n: x[:n, 2 * P * c:2 * P * c + 2 * P].rearrange(
                "p (e t) -> p e t", e=2)[:, :, :length(b)]
            return [(0, 0, view(dst, c, n), view(ps, c, n), True) for c, (_, n, _) in enumerate(chunks(b))]

        def v_parts(t, dst):
            b0, b1 = TILES[t]
            ps = pt_ps[t % 2]
            out = []
            if b0 == 0:
                out.append((dst[:META, 0, :], ps[:META, :P]))
                b0 = 1
            o = (b0 - TILES[t][0]) * P
            out.append((dst[:, b0:b1, :], ps[:, o:o + (b1 - b0) * P].rearrange("p (b d) -> p b d", d=P)))
            return out

        @block.sync
        def _(sp):
            for y_slot in y_stored:
                sp.sem_inc(y_slot, 16)
            sp.dma_start(neg_sink[:, :], sinks.partition_broadcast(P)).then_inc(sinks_loaded, 16)

            def table(run, t):
                sp.wait_ge(roped, PRE + run)
                a, z = tile_cols(t)
                sp.dma_start(rope[:, :, :z - a], rope_table[:, :, a:z]).then_inc(table_loaded, 16)

            def load(unit, *columns):
                sp.wait_ge(w_split, PRE + 2 * unit)
                sp.sem_inc(waits_met_sp, 1)
                for h in range(2):
                    src = w_in[bass.ds(512 * h, 512), :].rearrange("(k p) n -> p k n", p=P)
                    for e, at in enumerate(columns):
                        sp.dma_start(raw[h][:, :, A_HD * e:A_HD * e + A_HD], src[:, :, bass.ds(at, A_HD)]
                                       ).then_inc(raw_loaded[h], 16)

            def load_pair(unit, i, c0):
                load(unit, A_HD * i + c0, A_HD * i + (c0 + A_HD * A_PAIRS))

            def store(i, b):
                sp.wait_ge(y_made, PRE + 17 * i + b + 1)
                sp.dma_start(y_t[bass.ds(P * i, P), start(b):start(b) + length(b)],
                             y[b % 2][:, :length(b)]).then_inc(y_stored[b % 2], 16)

            load(0, A_K0, A_K0 + A_HD)
            load(1, A_V0, A_V0 + A_HD)
            load_pair(2, 0, 0)
            for run in range(6):
                table(run, run)
            load_pair(3, 0, A_Z0)
            table(6, 0)
            with sp.Fori(0, A_PAIRS) as i:
                for s in range(19):
                    if s < 18:
                        run = 6 * i + s // 3 + 7
                        if s % 3 == 0:
                            table(run, (s // 3 + 1) % 6)
                        if s == 1:
                            load_pair(4 + 2 * i, (i + 1) % A_PAIRS, 0)
                        if s == 14:
                            load_pair(5 + 2 * i, (i + 1) % A_PAIRS, A_Z0)
                    if 0 <= s - 2 < NB:
                        store(i, s - 2)
            sp.wait_ge(y_stored[0], 16 * (1 + 9 * A_PAIRS))
            sp.wait_ge(y_stored[1], 16 * (1 + 8 * A_PAIRS))

        @block.gpsimd
        def _(pool):
            for sem in POOL_SEMS:
                pool.sem_inc(sem, PRE)
            pool.memset(mask[:, :], 0.0).then_inc(mask_made, 1)
            pool.wait_ge(mask_made, 1)
            pool.affine_select(out=mask[:, :P], in_=mask[:, :P], compare_op=ALU.is_gt, fill=MASKED, base=0,
                               pattern=[[1, P]], channel_multiplier=-1).then_inc(mask_made, 1)
            pool.affine_select(out=mask[:, P:], in_=mask[:, P:], compare_op=ALU.is_ge, fill=MASKED, base=0,
                               pattern=[[-1, P]], channel_multiplier=1).then_inc(mask_made, 1)

            def split(unit, name):
                for h in range(2):
                    pool.wait_ge(w_rounded, PRE + 2 * unit + h + 1)
                    ks = slice(4 * h, 4 * h + 4)
                    pool.tensor_tensor(w_l[name][:, ks, :], raw[h][:, :, :], w_h[name][:, ks, :].bitcast(F32),
                                       ALU.subtract).then_inc(w_split, 1)

            def rotate(run, t):
                w = tile_cols(t)[1] - tile_cols(t)[0]
                pool.wait_ge(swapped, PRE + run + 1)
                pool.wait_ge(table_loaded, 16 * (run + 1))
                pool.tensor_tensor(q_s[:, :w], q_s[:, :w], rope[:, 1, :w], ALU.mult).then_inc(roped_sin, 1)

            split(0, "q")
            split(1, "z")
            for t in range(6):
                rotate(t, t)
            split(2, "q")
            split(3, "z")
            rotate(6, 0)
            with pool.Fori(0, A_PAIRS) as i:
                for t in range(1, 5):
                    rotate(6 * i + t + 6, t)
                split(4 + 2 * i, "q")
                rotate(6 * i + 11, 5)
                split(5 + 2 * i, "z")
                rotate(6 * i + 12, 0)

        @block.scalar
        def _(act):
            for sem in ACT_SEMS:
                act.sem_inc(sem, PRE)

            def round_w(unit, name):
                for h in range(2):
                    act.wait_ge(raw_loaded[h], 32 * (unit + 1))
                    act.activation(w_h[name][:, 4 * h:4 * h + 4, :], raw[h][:, :, :], ACT.Copy
                                   ).then_inc(w_rounded, 1)

            def swap(run, t):
                a, z = tile_cols(t)
                act.wait_ge(q_projected, PRE + run + 1)
                act.wait_ge(roped, PRE + run)
                for r in range(0, P, 64):
                    for x, z0 in ((0, 32), (32, 0)):
                        ins = act.activation(q_s[r + x:r + x + 32, :z - a], q_ps[r + z0:r + z0 + 32, :z - a],
                                             ACT.Copy)
                ins.then_inc(swapped, 1)

            def round_q(run, i, t):
                a, z = tile_cols(t)
                if i is not None:
                    act.wait_ge(scored, read_count(i, t))
                act.wait_ge(roped, PRE + run + 1)
                act.activation(q_h[t % 2][:, :z - a], q_f[:, :z - a], ACT.Copy).then_inc(q_rounded, 1)

            def tanh_z(i, t):
                a, z = tile_cols(t)
                act.wait_ge(z_projected, PRE + 6 * i + t + 7)
                act.wait_ge(y_made, PRE + 17 * i + (-2, 0, 3, 6, 9, 12)[t])
                act.activation(gate[t % 2][:, :z - a], z_ps[:, :z - a], ACT.Tanh, scale=0.5).then_inc(z_tanh, 1)

            def exponentials(i, b):
                m, r, n = length(b), b % 2, keys(b) + 1
                act.wait_ge(maxed, PRE + 17 * i + b + 1)
                for e in range(2):
                    ins = act.activation(prob[r][:m, e, :n], prob[r][:m, e, :n], ACT.Exp,
                                         bias=stat[r][:m, NEG.start + e:NEG.start + e + 1], scale=-1.0,
                                         accum_out=stat[r][:m, SUM.start + e:SUM.start + e + 1])
                ins.then_inc(exped, 1)

            def round_pt(i, b):
                act.wait_ge(turned, PRE + 17 * i + b + 1)
                act.wait_ge(weighed, PRE + 17 * i + b)
                for at, n, out, src, last in pt_parts(b, pt_h):
                    ins = act.activation(out, src, ACT.Copy)
                ins.then_inc(pt_rounded, 1)

            round_w(0, "q")
            round_w(1, "z")
            for t in range(7):
                if t < 6:
                    swap(t, t)
                if t > 0:
                    act.wait_ge(v_turned, PRE + t)
                    for out, src in v_parts(t - 1, v_h):
                        ins = act.activation(out, src, ACT.Copy)
                    ins.then_inc(v_rounded, 1)
                if t < 6:
                    a, z = tile_cols(t)
                    act.wait_ge(roped, PRE + t + 1)
                    act.activation(k_h[:, a:z], q_f[:, :z - a], ACT.Copy).then_inc(q_rounded, 1)
                    if t == 5:
                        act.wait_ge(q_projected, PRE + 6)
                        round_w(2, "q")
                    act.wait_ge(z_projected, PRE + t + 1)
                    act.activation(gate[t % 2][:, :z - a], z_ps[:, :z - a], ACT.Copy).then_inc(v_copied, 1)
            round_w(3, "z")
            swap(6, 0)
            round_q(6, None, 0)
            with act.Fori(0, A_PAIRS) as i:
                for s in range(18):
                    t, run = (s // 3 + 1) % 6, 6 * i + s // 3 + 7
                    if s > 0:
                        round_pt(i, s - 1)
                    if s < NB:
                        exponentials(i, s)
                    if s % 3 == 0:
                        tanh_z(i, s // 3)
                    if s % 3 == 1:
                        swap(run, t)
                    if s % 3 == 2:
                        round_q(run, i, t)
                    if s == 13:
                        act.wait_ge(q_projected, PRE + 6 * i + 12)
                        round_w(4 + 2 * i, "q")
                    if s == 15:
                        act.wait_ge(z_projected, PRE + 6 * i + 12)
                        round_w(5 + 2 * i, "z")

        @block.vector
        def _(dve):
            for sem in DVE_SEMS:
                dve.sem_inc(sem, PRE)
            dve.wait_ge(sinks_loaded, 16)
            dve.tensor_scalar(neg_sink[:, :], neg_sink[:, :], -1.0, None, ALU.mult).then_inc(sinks_negated, 1)
            dve.wait_ge(sinks_negated, 1)
            dve.wait_ge(mask_made, 3)

            def rotate_cos(run, t):
                w = tile_cols(t)[1] - tile_cols(t)[0]
                dve.wait_ge(swapped, PRE + run + 1)
                dve.wait_ge(table_loaded, 16 * (run + 1))
                dve.wait_ge(q_split, PRE + run)
                dve.tensor_tensor(q_f[:, :w], q_ps[:, :w], rope[:, 0, :w], ALU.mult).then_inc(roped_cos, 1)

            def rotate_sum(run, t):
                w = tile_cols(t)[1] - tile_cols(t)[0]
                dve.wait_ge(roped_cos, PRE + run + 1)
                dve.wait_ge(roped_sin, PRE + run + 1)
                dve.tensor_tensor(q_f[:, :w], q_f[:, :w], q_s[:, :w], ALU.add).then_inc(roped, 1)

            def split_q(run, out_l, out_h, w):
                dve.wait_ge(q_rounded, PRE + run + 1)
                dve.tensor_tensor(out_l, q_f[:, :w], out_h.bitcast(F32), ALU.subtract).then_inc(q_split, 1)

            def split_query(run, t):
                w = tile_cols(t)[1] - tile_cols(t)[0]
                split_q(run, q_l[t % 2][:, :w], q_h[t % 2][:, :w], w)

            def make_gate(i, t):
                w = tile_cols(t)[1] - tile_cols(t)[0]
                dve.wait_ge(z_tanh, PRE + 6 * i + t + 1)
                dve.scalar_tensor_tensor(out=gate[t % 2][:, :w], in0=gate[t % 2][:, :w], scalar=1.0,
                                         in1=z_ps[:, :w], op0=ALU.add, op1=ALU.mult).then_inc(gated, 1)

            def soften(i, b):
                m, r, n, c = length(b), b % 2, keys(b), mask_at(b)
                if b == 0:
                    dve.wait_ge(maxed, PRE + 17 * i)
                    dve.tensor_copy(sink[:, :], neg_sink[:, :].rearrange("p (e i) -> p e i", e=2)[:, :, bass.ds(i, 1)].rearrange("p e i -> p (e i)")
                                    ).then_inc(sink_set, 1)
                    dve.wait_ge(sink_set, PRE + i + 1)
                dve.wait_ge(turned, before(17 * i, b))
                dve.tensor_copy(prob[r][:m, :, 0], sink[:m, :])
                dve.wait_ge(scored, PRE + 17 * i + b + 1)
                dve.sem_inc(waits_met_dve, 1)
                for e in range(2):
                    ins = dve.tensor_tensor_reduce(
                        prob[r][:m, e, 1:n + 1], s_ps[e][:m, :n], mask[:m, c:c + n],
                        -A_HD ** -0.5, sink[:m, e:e + 1], ALU.add, ALU.min,
                        stat[r][:m, NEG.start + e:NEG.start + e + 1])
                ins.then_inc(maxed, 1)

            def normalise(i, b):
                m, r, n = length(b), b % 2, keys(b)
                st = stat[r]
                dve.wait_ge(exped, PRE + 17 * i + b + 1)
                dve.reciprocal(st[:m, INV], st[:m, SUM]).then_inc(inverted, 1)
                dve.wait_ge(inverted, PRE + 17 * i + b + 1)
                for e in range(2):
                    ins = dve.tensor_scalar(prob[r][:m, e, 1:n + 1], prob[r][:m, e, 1:n + 1],
                                            st[:m, INV.start + e:INV.start + e + 1], None, ALU.mult)
                ins.then_inc(normalised, 1)

            def split_pt(i, b):
                dve.wait_ge(pt_rounded, PRE + 17 * i + b + 1)
                for (_, _, out, src, _), (_, _, high, _, _) in zip(pt_parts(b, pt_l), pt_parts(b, pt_h)):
                    ins = dve.tensor_tensor(out, src, high.bitcast(F32), ALU.subtract)
                ins.then_inc(pt_split, 1)

            def make_y(i, b):
                m, r, t = length(b), b % 2, tile_of(b)
                dve.wait_ge(weighed, PRE + 17 * i + b + 1)
                dve.wait_ge(gated, PRE + 6 * i + t + 1)
                dve.wait_ge(y_stored[r], 16 * (1 + (9 - r) * i + b // 2))
                c = start(b) - tile_cols(t)[0]
                for e in range(2):
                    rows = slice(A_HD * e, A_HD * e + A_HD)
                    ins = dve.scalar_tensor_tensor(out=y[r][rows, :m], in0=o_ps[r][rows, m * e:m * e + m],
                                                   scalar=0.5, in1=gate[t % 2][rows, c:c + m],
                                                   op0=ALU.mult, op1=ALU.mult)
                ins.then_inc(y_made, 1)

            for t in range(7):
                if t > 0:
                    dve.wait_ge(v_rounded, PRE + t)
                    for (out, src), (high, _) in zip(v_parts(t - 1, v_l), v_parts(t - 1, v_h)):
                        ins = dve.tensor_tensor(out, src, high.bitcast(F32), ALU.subtract)
                    ins.then_inc(v_split, 1)
                rotate_cos(t, t % 6)
                rotate_sum(t, t % 6)
                if t < 6:
                    a, z = tile_cols(t)
                    split_q(t, k_l[:, a:z], k_h[:, a:z], z - a)
            split_query(6, 0)
            with dve.Fori(0, A_PAIRS) as i:
                for s in range(19):
                    t, run = (s // 3 + 1) % 6, 6 * i + s // 3 + 7
                    if 0 <= s - 2 < NB:
                        make_y(i, s - 2)
                    if s < NB:
                        soften(i, s)
                    if s % 3 == 2:
                        rotate_cos(run, t)
                    if 0 <= s - 1 < NB:
                        split_pt(i, s - 1)
                    if s % 3 == 2:
                        rotate_sum(run, t)
                    if s < NB:
                        normalise(i, s)
                    if s % 3 == 0 and s < 18:
                        make_gate(i, s // 3)
                    if s % 3 == 2:
                        split_query(run, t)

        @block.tensor
        def _(pe):
            for sem in PE_SEMS:
                pe.sem_inc(sem, PRE)

            def project(ps, name, t, ks):
                a, z = tile_cols(t)
                for k in ks:
                    last = product(pe, ps[:, :z - a], w_h[name][:, k, :], w_l[name][:, k, :],
                                   u_h[:, k, a:z], u_l[:, k, a:z], k == 0, k == KT - 1)
                return last

            def project_part(i, m, t, part):
                name, ks = "qz"[part // 3], (range(0, 3), range(3, 6), range(6, 8))[part % 3]
                if part == 0:
                    pe.wait_ge(roped_cos, PRE + m + 6)
                    if t == 0:
                        pe.wait_ge(w_split, PRE + 2 * (2 * i + 4) + 2)
                if part == 3:
                    pe.wait_ge(gated, PRE + m)
                    if t == 0:
                        pe.wait_ge(w_split, PRE + 2 * (2 * i + 5) + 2)
                last = project(q_ps if name == "q" else z_ps, name, t, ks)
                if part == 2:
                    last.then_inc(q_projected, 1)
                if part == 5:
                    last.then_inc(z_projected, 1)

            def scores(i, b):
                m, r, n, t = length(b), b % 2, keys(b), tile_of(b)
                c = start(b) - tile_cols(t)[0]
                if b == TILES[t][0]:
                    pe.wait_ge(q_split, PRE + 6 * i + t + 7)
                pe.wait_ge(maxed, PRE + 17 * i + b)
                if b == 0:
                    pe.sem_inc(waits_met_pe, 1)
                for e in range(2):
                    rows = slice(A_HD * e, A_HD * e + A_HD)
                    last = product(pe, s_ps[e][:m, :n],
                                   q_h[t % 2][rows, c:c + m], q_l[t % 2][rows, c:c + m],
                                   k_h[rows, key0(b):key0(b) + n], k_l[rows, key0(b):key0(b) + n], True, True)
                last.then_inc(scored, 1)

            def turn(i, b):
                m, r = length(b), b % 2
                pe.wait_ge(normalised, PRE + 17 * i + b + 1)
                pe.wait_ge(pt_split, before(17 * i, b))
                if b == 0:
                    pe.sem_inc(waits_met_pe, 1)
                for c, (at, n, _) in enumerate(chunks(b)):
                    for e in range(2):
                        last = pe.transpose(pt_ps[r][:n, 2 * P * c + P * e:2 * P * c + P * e + m],
                                            prob[r][:m, e, 1 + at:1 + at + n], ident[:m, :m])
                last.then_inc(turned, 1)

            def weigh(i, b):
                m, r = length(b), b % 2
                pe.wait_ge(pt_split, PRE + 17 * i + b + 1)
                pe.wait_ge(y_made, before(17 * i, b))
                parts = chunks(b)
                view = lambda x, c, n: x[:n, 2 * P * c:2 * P * c + 2 * P].rearrange(
                    "p (e t) -> p e t", e=2)[:, :, :m]
                out = o_ps[r][:, :2 * m].rearrange("p (e t) -> p e t", e=2)
                for c, (_, n, kb) in enumerate(parts):
                    first, final = c == 0, c == len(parts) - 1
                    pe.matmul(out, v_h[:n, kb, :], view(pt_h, c, n), start=first, stop=False)
                    pe.matmul(out, v_l[:n, kb, :], view(pt_h, c, n), start=False, stop=False)
                    last = pe.matmul(out, v_h[:n, kb, :], view(pt_l, c, n), start=False, stop=final)
                last.then_inc(weighed, 1)

            for t in range(7):
                if t < 6:
                    if t == 0:
                        pe.wait_ge(w_split, PRE + 2)
                    pe.wait_ge(roped_cos, PRE + t)
                    project(q_ps, "q", t, range(KT)).then_inc(q_projected, 1)
                if t > 0:
                    pe.wait_ge(v_copied, PRE + t)
                    if t >= 3:
                        pe.wait_ge(v_split, PRE + t - 2)
                    b0, b1 = TILES[t - 1]
                    for b in range(b0, b1):
                        c = start(b) - start(b0)
                        o = (b - b0) * P
                        last = pe.transpose(pt_ps[(t - 1) % 2][:length(b), o:o + P],
                                            gate[(t - 1) % 2][:, c:c + length(b)], ident[:, :])
                    last.then_inc(v_turned, 1)
                if t < 6:
                    if t == 0:
                        pe.wait_ge(w_split, PRE + 4)
                    pe.wait_ge(v_copied, PRE + t)
                    project(z_ps, "z", t, range(KT)).then_inc(z_projected, 1)
            pe.wait_ge(roped_cos, PRE + 6)
            pe.wait_ge(w_split, PRE + 6)
            project(q_ps, "q", 0, range(KT)).then_inc(q_projected, 1)
            pe.wait_ge(v_copied, PRE + 6)
            pe.wait_ge(w_split, PRE + 8)
            project(z_ps, "z", 0, range(KT)).then_inc(z_projected, 1)
            pe.wait_ge(v_split, PRE + 6)
            with pe.Fori(0, A_PAIRS) as i:
                for s in range(18):
                    m, t = 6 * i + s // 3 + 1, (s // 3 + 1) % 6
                    if s < NB:
                        scores(i, s)
                    if s > 0:
                        turn(i, s - 1)
                    project_part(i, m, t, 2 * (s % 3))
                    project_part(i, m, t, 2 * (s % 3) + 1)
                    if s > 0:
                        weigh(i, s - 1)


def project_out(nc, name, w_out, y_src, residual, norm_g, ident, stores):
    first_layer = len(stores) == 2
    n_blocks = NB if first_layer else NB - 1
    peeled = 5 if first_layer else 4
    mm_lag = 0 if first_layer else 1
    lag = mm_lag + 1

    def over(eng, step, lags):
        for n in range(peeled):
            step(n, n % 2)
        with eng.Fori(0, (n_blocks - peeled) // 2) as i:
            step(peeled + 2 * i, peeled % 2)
            step(peeled + 1 + 2 * i, 1 - peeled % 2)
        for n in range(n_blocks, n_blocks + lags):
            step(n, n % 2)

    def exists(n, lag=0):
        return not isinstance(n, int) or 0 <= n - lag < n_blocks

    def rows_of(n):
        return cols(n) if first_layer else bass.ds(P * n + META, P)

    def size_of(n):
        return size(n) if first_layer else P

    def used(n, ring=2):
        return not isinstance(n, int) or n >= ring

    with ExitStack() as stack:
        ph = Phase(nc, stack, name)
        w_h, w_l = ph.sb("w_h", [P, KT, D], F32R), ph.sb("w_l", [P, KT, D], F32R)
        raw = [ph.sb(f"raw{k}", [P, D]) for k in range(4)]
        gain, squares = ph.sb("gain", [P, D]), ph.sb("squares", [P, D])
        y_in = [ph.sb(f"y{p}", [P, D]) for p in range(2)]
        y_h = [ph.sb(f"y_h{p}", [P, KT, P], F32R) for p in range(2)]
        y_l = [ph.sb(f"y_l{p}", [P, KT, P], F32R) for p in range(2)]
        res = [ph.sb(f"res{p}", [P, D]) for p in range(2)]
        h = [ph.sb(f"h{p}", [P, D]) for p in range(2)]
        xs = [ph.sb(f"xs{p}", [P, D]) for p in range(2)]
        u_t = [ph.sb(f"u_t{p}", [P, KT, P]) for p in range(2)] if first_layer else None
        stat = [ph.sb(f"stat{p}", [P, 3]) for p in range(2)]
        eps = ph.sb("eps", [P, 1])
        acc = [[ph.ps(f"acc{p}{c}") for c in range(2)] for p in range(2)]
        turned_ps = [[ph.ps(f"turned{p}{c}") for c in range(2)] for p in range(2)]
        y_loaded = ph.sems("y_loaded0", "y_loaded1")
        res_loaded = ph.sems("res_loaded0", "res_loaded1")
        h_stored, u_stored = ph.sems("h_stored0", "h_stored1"), ph.sems("u_stored0", "u_stored1")
        raw_loaded = ph.sems(*(f"raw_loaded{k}" for k in range(4)))
        (gain_loaded, eps_made, w_rounded, w_split_pool, w_split_dve, y_rounded, y_split, multiplied, h_made, summed,
         rooted, inverted, scaled, turned, copied_act, copied_dve) = ph.sems(
            "gain_loaded", "eps_made", "w_rounded", "w_split_pool", "w_split_dve", "y_rounded", "y_split",
            "multiplied", "h_made", "summed", "rooted", "inverted", "scaled", "turned", "copied_act", "copied_dve")
        POOL_KS, DVE_KS = (2, 5), (0, 1, 3, 4, 6, 7)
        block = ph.block()
        loads = lambda n, p: 8 * n + (8 if p else 16)

        @block.sync
        def _(sp):
            def load_w(k):
                if k >= 4:
                    sp.wait_ge(w_split_pool, sum(j <= k - 4 for j in POOL_KS)) if k - 4 in POOL_KS else \
                        sp.wait_ge(w_split_dve, sum(j <= k - 4 for j in DVE_KS))
                for e in range(2):
                    half = slice(P // 2 * e, P // 2 * e + P // 2)
                    at = D // 2 * e + P // 2 * k if first_layer else P * k + P // 2 * e
                    sp.dma_start(raw[k % 4][half, :], w_out[at:at + P // 2, :]).then_inc(raw_loaded[k % 4], 16)

            def step(n, p):
                m = size_of(n)
                if used(n):
                    sp.wait_ge(y_split, n - 1)
                if first_layer:
                    sp.dma_start(y_in[p][:, :].rearrange("p (k t) -> p k t", k=KT)[:, :, :m],
                                 y_src[:, cols(n)].rearrange("(k p) t -> p k t", p=P)).then_inc(y_loaded[p], 16)
                else:
                    sp.dma_start(y_in[p][:, :], y_src[rows_of(n), :]).then_inc(y_loaded[p], 16)
                if used(n):
                    sp.wait_ge(h_made, 2 * (n - 1))
                sp.dma_start(res[p][:m, :], residual(n)).then_inc(res_loaded[p], 16)
                if isinstance(n, int) and n == 0:
                    sp.dma_start(gain[:, :], norm_g.partition_broadcast(P)).then_inc(gain_loaded, 16)
                    for k in range(KT):
                        load_w(k)
            over(sp, step, 0)

        @block.gpsimd
        def _(pool):
            pool.memset(eps[:, :], EPS).then_inc(eps_made, 1)
            for k in POOL_KS:
                pool.wait_ge(w_rounded, k + 1)
                pool.tensor_tensor(w_l[:, k, :], raw[k % 4][:, :], w_h[:, k, :].bitcast(F32),
                                   ALU.subtract).then_inc(w_split_pool, 1)

            def step(n, p):
                if exists(n, lag):
                    b, q = n - lag, (p + lag) % 2
                    m = size_of(b)
                    if first_layer:
                        pool.wait_ge(h_made, 2 * (b + 1))
                        pool.dma_start(stores[0][rows_of(b), :], h[q][:m, :]).then_inc(h_stored[q], 16)
                    else:
                        pool.wait_ge(scaled, b + 1)
                        pool.dma_start(stores[0][bass.ds(P * b, P), :], xs[q][:, :]).then_inc(h_stored[q], 16)
                if first_layer and exists(n, 2):
                    b = n - 2
                    m = size_of(b)
                    pool.wait_ge(copied_act, b + 1)
                    pool.wait_ge(copied_dve, b + 1)
                    pool.dma_start(stores[1][:, rows_of(b)].rearrange("(k p) t -> p k t", p=P),
                                   u_t[p][:, :, :m]).then_inc(u_stored[p], 16)
            over(pool, step, 2)
            for p in range(2):
                stored = 16 * ((n_blocks + 1 - p) // 2)
                pool.wait_ge(h_stored[p], stored)
                if first_layer:
                    pool.wait_ge(u_stored[p], stored)

        @block.scalar
        def _(act):
            for k in range(KT):
                act.wait_ge(raw_loaded[k % 4], 32 * (k // 4 + 1))
                act.activation(w_h[:, k, :], raw[k % 4][:, :], ACT.Copy).then_inc(w_rounded, 1)
            act.wait_ge(eps_made, 1)

            def step(n, p):
                if exists(n):
                    m = size_of(n)
                    if used(n):
                        act.wait_ge(multiplied, n - 1)
                    if first_layer:
                        act.wait_ge(y_loaded[p], loads(n, p))
                        act.activation(y_h[p][:, :, :m],
                                       y_in[p][:, :].rearrange("p (k t) -> p k t", k=KT)[:, :, :m],
                                       ACT.Copy).then_inc(y_rounded, 1)
                    else:
                        act.wait_ge(turned, n + 1)
                        for c in range(2):
                            ins = act.activation(y_h[p][:, 4 * c:4 * c + 4, :],
                                                 turned_ps[p][c][:, :].rearrange("p (k t) -> p k t", k=4), ACT.Copy)
                        ins.then_inc(y_rounded, 1)
                if exists(n, lag):
                    b, q = n - lag, (p + lag) % 2
                    m = size_of(b)
                    act.wait_ge(h_made, 2 * (b + 1))
                    if used(n, lag + 1):
                        act.wait_ge(rooted, b)
                    if used(n, lag + 2):
                        act.wait_ge(inverted, b - 1)
                    act.activation(squares[:m, :], h[q][:m, :], ACT.Square,
                                   accum_out=stat[q][:m, 0:1]).then_inc(summed, 1)
                    act.wait_ge(summed, b + 1)
                    act.activation(stat[q][:m, 1:2], stat[q][:m, 0:1], ACT.Sqrt, bias=eps[:m, :],
                                   scale=1.0 / D).then_inc(rooted, 1)
                if first_layer and exists(n, 2):
                    b = n - 2
                    m = size_of(b)
                    act.wait_ge(turned, b + 1)
                    if used(n, 4):
                        act.wait_ge(u_stored[p], loads(b - 2, p))
                    act.activation(u_t[p][:, :4, :m],
                                   turned_ps[p][0][:, :].rearrange("p (k t) -> p k t", k=4)[:, :, :m],
                                   ACT.Copy).then_inc(copied_act, 1)
            over(act, step, 2)

        @block.vector
        def _(dve):
            for k in DVE_KS:
                dve.wait_ge(w_rounded, k + 1)
                dve.tensor_tensor(w_l[:, k, :], raw[k % 4][:, :], w_h[:, k, :].bitcast(F32),
                                  ALU.subtract).then_inc(w_split_dve, 1)
            dve.wait_ge(gain_loaded, 16)

            def step(n, p):
                if exists(n):
                    m = size_of(n)
                    dve.wait_ge(y_rounded, n + 1)
                    if first_layer:
                        dve.tensor_tensor(y_l[p][:, :, :m],
                                          y_in[p][:, :].rearrange("p (k t) -> p k t", k=KT)[:, :, :m],
                                          y_h[p][:, :, :m].bitcast(F32), ALU.subtract).then_inc(y_split, 1)
                    else:
                        for c in range(2):
                            ks = slice(4 * c, 4 * c + 4)
                            ins = dve.tensor_tensor(y_l[p][:, ks, :],
                                                    turned_ps[p][c][:, :].rearrange("p (k t) -> p k t", k=4),
                                                    y_h[p][:, ks, :].bitcast(F32), ALU.subtract)
                        ins.then_inc(y_split, 1)
                if exists(n, lag):
                    b, q = n - lag, (p + lag) % 2
                    m = size_of(b)
                    dve.wait_ge(multiplied, b + 1)
                    dve.wait_ge(res_loaded[q], loads(b, q))
                    if used(n, lag + 2):
                        dve.wait_ge(summed, b - 1)
                        if first_layer:
                            dve.wait_ge(h_stored[q], loads(b - 2, q))
                    for c in range(2):
                        dve.tensor_tensor(h[q][:m, 512 * c:512 * c + 512], acc[q][c][:m, :],
                                          res[q][:m, 512 * c:512 * c + 512], ALU.add).then_inc(h_made, 1)
                    dve.wait_ge(rooted, b + 1)
                    dve.reciprocal(stat[q][:m, 2:3], stat[q][:m, 1:2]).then_inc(inverted, 1)
                    dve.wait_ge(inverted, b + 1)
                    if used(n, lag + 2):
                        if first_layer:
                            dve.wait_ge(turned, b - 1)
                        else:
                            dve.wait_ge(h_stored[q], loads(b - 2, q))
                    dve.scalar_tensor_tensor(out=xs[q][:m, :], in0=h[q][:m, :], scalar=stat[q][:m, 2:3],
                                             in1=gain[:m, :], op0=ALU.mult, op1=ALU.mult).then_inc(scaled, 1)
                if first_layer and exists(n, 2):
                    b = n - 2
                    m = size_of(b)
                    dve.wait_ge(turned, b + 1)
                    if used(n, 4):
                        dve.wait_ge(u_stored[p], loads(b - 2, p))
                    dve.tensor_copy(u_t[p][:, 4:, :m],
                                    turned_ps[p][1][:, :].rearrange("p (k t) -> p k t", k=4)[:, :, :m]
                                    ).then_inc(copied_dve, 1)
            over(dve, step, 2)

        @block.tensor
        def _(pe):
            def turn(src, b, q, m):
                for k in range(KT):
                    last = pe.transpose(turned_ps[q][k // 4][:, (k % 4) * P:(k % 4) * P + m],
                                        src[q][:m, k * P:(k + 1) * P], ident[:m, :m])
                last.then_inc(turned, 1)

            def step(n, p):
                if not first_layer and exists(n):
                    pe.wait_ge(y_loaded[p], loads(n, p))
                    if used(n):
                        pe.wait_ge(y_split, n - 1)
                    turn(y_in, n, p, P)
                if exists(n, mm_lag):
                    b, q = n - mm_lag, (p + mm_lag) % 2
                    m = size_of(b)
                    pe.wait_ge(y_split, b + 1)
                    if used(n, mm_lag + 2):
                        pe.wait_ge(h_made, 2 * (b - 1))
                    for k in range(KT):
                        if isinstance(b, int) and b == 0:
                            names = (w_split_pool, POOL_KS) if k in POOL_KS else (w_split_dve, DVE_KS)
                            pe.wait_ge(names[0], sum(j <= k for j in names[1]))
                        for c in range(2):
                            last = product(pe, acc[q][c][:m, :], y_h[q][:, k, :m], y_l[q][:, k, :m],
                                           w_h[:, k, 512 * c:512 * c + 512], w_l[:, k, 512 * c:512 * c + 512],
                                           k == 0, k == KT - 1)
                    last.then_inc(multiplied, 1)
                if first_layer and exists(n, 1):
                    b, q = n - 1, 1 - p
                    m = size_of(b)
                    pe.wait_ge(scaled, b + 1)
                    if used(n, 3):
                        pe.wait_ge(copied_act, b - 1)
                        pe.wait_ge(copied_dve, b - 1)
                    turn(xs, b, q, m)
            over(pe, step, 1)


GATE_I, GATE_F = 0, 32


def gates(nc, u_t, w_in, b_gates, ident, u_h, u_l, head_cols, row_a, row_dec):
    H = B_HEADS
    with ExitStack() as stack:
        ph = Phase(nc, stack, "g")
        u_in = [ph.sb(f"u_in{r}", [P, KT, TW]) for r in range(2)]
        w_raw = ph.sb("w_raw", [P, KT, 64])
        w_h, w_l = ph.sb("w_h", [P, KT, 64], F32R), ph.sb("w_l", [P, KT, 64], F32R)
        bias = ph.sb("bias", [64, 1])
        rows = ph.sb("rows", [P, T])
        log_i, log_f = ph.sb("log_i", [H, T]), ph.sb("log_f", [H, T])
        keep, scratch = ph.sb("keep", [H, T]), ph.sb("scratch", [H, T])
        m_prev, dec = ph.sb("m_prev", [H, NB]), ph.sb("dec", [H, NB])
        g_ps = [ph.ps(f"g_ps{r}") for r in range(2)]
        c_ps = [ph.ps(f"c_ps{r}") for r in range(4)]
        u_loaded = ph.sems("u_loaded0", "u_loaded1")
        (w_cleared, w_loaded, w_rounded, w_split, cleared, u_rounded, u_split, projected, biased, step, act_step,
         turned, stored, filled) = ph.sems(
            "w_cleared", "w_loaded", "w_rounded", "w_split", "cleared", "u_rounded", "u_split", "projected",
            "biased", "step", "act_step", "turned", "stored", "filled")
        block = ph.block()
        PER_BANK = 5

        @block.sync
        def _(sp):
            sp.wait_ge(w_cleared, 1)
            src = w_in.rearrange("(k p) n -> p k n", p=P)
            sp.dma_start(w_raw[:, :, GATE_I:GATE_I + H], src[:, :, B_G0:B_G0 + H]).then_inc(w_loaded, 16)
            sp.dma_start(w_raw[:, :, GATE_F:GATE_F + H], src[:, :, B_G0 + H:B_G0 + 2 * H]).then_inc(w_loaded, 16)
            bias_src = b_gates.rearrange("(n a) -> n a", a=1)
            sp.dma_start(bias[GATE_I:GATE_I + H, :], bias_src[:H, :]).then_inc(w_loaded, 16)
            sp.dma_start(bias[GATE_F:GATE_F + H, :], bias_src[H:, :]).then_inc(w_loaded, 16)
            for t in range(6):
                a, z = tile_cols(t)
                if t >= 2:
                    sp.wait_ge(u_split, t - 1)
                sp.dma_start(u_in[t % 2][:, :, :z - a],
                             u_t[:, a:z].rearrange("(k p) t -> p k t", p=P)).then_inc(u_loaded[t % 2], 16)
            sp.wait_ge(step, 9)
            sp.dma_start(row_a.rearrange("(h t) -> h t", h=H), log_i[:, :]).then_inc(stored, 16)
            sp.wait_ge(act_step, 3)
            sp.dma_start(row_dec.rearrange("(h b) -> h b", h=H), dec[:, :]).then_inc(stored, 16)
            sp.wait_ge(stored, 32)

        @block.gpsimd
        def _(pool):
            pool.memset(w_raw[:, :, :], 0.0).then_inc(w_cleared, 1)
            pool.memset(rows[:, :], 0.0).then_inc(cleared, 1)
            pool.wait_ge(w_rounded, 1)
            pool.tensor_tensor(w_l[:, :, :], w_raw[:, :, :], w_h[:, :, :].bitcast(F32),
                               ALU.subtract).then_inc(w_split, 1)
            pool.memset(keep[:, :], 1.0).then_inc(cleared, 1)
            pool.wait_ge(cleared, 2)
            pool.memset(keep[:, 0:1], 0.0)
            pool.memset(keep[:, META:T:P], 0.0).then_inc(cleared, 1)

        @block.scalar
        def _(act):
            act.wait_ge(w_loaded, 64)
            act.activation(w_h[:, :, :], w_raw[:, :, :], ACT.Copy).then_inc(w_rounded, 1)
            for t in range(6):
                a, z = tile_cols(t)
                act.wait_ge(u_loaded[t % 2], 16 * (t // 2 + 1))
                act.activation(u_h[:, :, a:z], u_in[t % 2][:, :, :z - a], ACT.Copy).then_inc(u_rounded, 1)
            act.wait_ge(step, 1)
            act.activation(scratch[:, :], scratch[:, :], ACT.Exp).then_inc(act_step, 1)
            act.wait_ge(step, 2)
            act.activation(scratch[:, :], scratch[:, :], ACT.Ln).then_inc(act_step, 1)
            act.wait_ge(step, 10)
            act.activation(dec[:, :], dec[:, :], ACT.Exp).then_inc(act_step, 1)
            for c in range(4):
                n = min(PER_BANK, NB - PER_BANK * c)
                act.wait_ge(turned, c + 1)
                act.wait_ge(filled, c + 1)
                src = c_ps[c][:, :96 * n].rearrange("p (b q) -> p b q", q=96)
                bs = slice(PER_BANK * c, PER_BANK * c + n)
                act.activation(head_cols[:, 1, bs, :], src[:, :, 32:32 + H], ACT.Exp)
                act.activation(head_cols[:, 2, bs, :], src[:, :, 64:64 + H], ACT.Exp, scale=-1.0)

        @block.vector
        def _(dve):
            dve.wait_ge(w_loaded, 64)
            for t in range(7):
                if t < 6:
                    a, z = tile_cols(t)
                    dve.wait_ge(u_rounded, t + 1)
                    dve.tensor_tensor(u_l[:, :, a:z], u_in[t % 2][:, :, :z - a], u_h[:, :, a:z].bitcast(F32),
                                      ALU.subtract).then_inc(u_split, 1)
                if t > 0:
                    a, z = tile_cols(t - 1)
                    ps = g_ps[(t - 1) % 2]
                    dve.wait_ge(projected, t)
                    dve.tensor_scalar(log_i[:, a:z], ps[GATE_I:GATE_I + H, :z - a],
                                      bias[GATE_I:GATE_I + H, :], None, ALU.add)
                    dve.tensor_scalar(log_f[:, a:z], ps[GATE_F:GATE_F + H, :z - a],
                                      bias[GATE_F:GATE_F + H, :], None, ALU.add).then_inc(biased, 1)
            dve.wait_ge(biased, 6)
            dve.scalar_tensor_tensor(out=scratch[:, :], in0=log_f[:, :], scalar=-1.0, in1=log_f[:, :],
                                     op0=ALU.mult, op1=ALU.min).then_inc(step, 1)
            dve.wait_ge(act_step, 1)
            dve.tensor_scalar(scratch[:, :], scratch[:, :], 1.0, None, ALU.add).then_inc(step, 1)
            dve.wait_ge(act_step, 2)
            dve.scalar_tensor_tensor(out=log_f[:, :], in0=log_f[:, :], scalar=0.0, in1=scratch[:, :],
                                     op0=ALU.min, op1=ALU.subtract).then_inc(step, 1)
            dve.wait_ge(step, 3)
            dve.wait_ge(cleared, 3)
            dve.tensor_tensor_scan(scratch[:, :], keep[:, :], log_f[:, :], 0.0, ALU.mult, ALU.add).then_inc(step, 1)
            dve.tensor_tensor_scan(rows[64:64 + H, :], log_f[:, :], log_i[:, :], 0.0, ALU.add,
                                   ALU.max).then_inc(step, 1)
            dve.wait_ge(step, 5)
            dve.tensor_tensor(rows[0:H, :], log_i[:, :], scratch[:, :], ALU.subtract).then_inc(step, 1)
            dve.tensor_copy(log_f[:, :], rows[64:64 + H, :]).then_inc(step, 1)
            dve.memset(m_prev[:, 0:1], 0.0)
            dve.tensor_copy(m_prev[:, 1:NB], rows[64:64 + H, META - 1:T - 1:P]).then_inc(step, 1)
            dve.wait_ge(step, 8)
            dve.tensor_tensor(log_i[:, :], scratch[:, :], log_f[:, :], ALU.subtract).then_inc(step, 1)
            dve.wait_ge(step, 9)
            dve.tensor_tensor(dec[:, 0:1], log_i[:, META - 1:META], m_prev[:, 0:1], ALU.add)
            dve.tensor_tensor(dec[:, 1:], log_i[:, META + P - 1:T:P], m_prev[:, 1:], ALU.add).then_inc(step, 1)
            for b in range(NB):
                c = slice(start(b), start(b) + length(b))
                ins = dve.tensor_scalar(rows[32:32 + H, c], log_i[:, c], m_prev[:, b:b + 1], None, ALU.add)
            ins.then_inc(step, 1)
            for c in range(4):
                n = min(PER_BANK, NB - PER_BANK * c)
                dve.wait_ge(turned, c + 1)
                bs = slice(PER_BANK * c, PER_BANK * c + n)
                dve.tensor_copy(head_cols[:, 0, bs, :],
                                c_ps[c][:, :96 * n].rearrange("p (b q) -> p b q", q=96)[:, :, :H]).then_inc(filled, 1)

        @block.tensor
        def _(pe):
            for t in range(6):
                a, z = tile_cols(t)
                pe.wait_ge(u_split, t + 1)
                if t == 0:
                    pe.wait_ge(w_split, 1)
                if t >= 2:
                    pe.wait_ge(biased, t - 1)
                for k in range(KT):
                    last = product(pe, g_ps[t % 2][:64, :z - a], w_h[:, k, :], w_l[:, k, :],
                                   u_h[:, k, a:z], u_l[:, k, a:z], k == 0, k == KT - 1)
                last.then_inc(projected, 1)
            pe.wait_ge(step, 11)
            for b in range(NB):
                c = start(b)
                o = 96 * (b % PER_BANK)
                last = pe.transpose(c_ps[b // PER_BANK][:, o:o + 96], rows[:96, c:c + P], ident[:96, :96])
                if b % PER_BANK == PER_BANK - 1 or b == NB - 1:
                    last.then_inc(turned, 1)


def mlstm(nc, w_in, ident, u_h, u_l, head_cols, row_a, row_dec, y_out):
    VW = B_V + 2
    with ExitStack() as stack:
        ph = Phase(nc, stack, "m")
        raw_qk, raw_v = ph.sb("raw_qk", [P, KT, P]), ph.sb("raw_v", [P, KT, 3 * P])
        wqk_h, wqk_l = ph.sb("wqk_h", [P, KT, P], F32R), ph.sb("wqk_l", [P, KT, P], F32R)
        wv_h, wv_l = ph.sb("wv_h", [P, KT, 3 * P], F32R), ph.sb("wv_l", [P, KT, 3 * P], F32R)
        row = [ph.sb(f"row{r}", [P, TW]) for r in range(2)]
        decay = ph.sb("decay", [B_QK, NB])
        col = ph.sb("col", [P, 3, NB])
        q_h = [ph.sb(f"q_h{r}", [B_QK, TW], F32R) for r in range(2)]
        q_l = [ph.sb(f"q_l{r}", [B_QK, TW], F32R) for r in range(2)]
        k_both = ph.sb("k_both", [P, TW])
        k_f = [k_both[:B_QK, :], k_both[B_QK:, :]]
        ident_of = [ident[:B_QK, :B_QK], ident[B_QK:, B_QK:]]
        k_h = [ph.sb(f"k_h{r}", [B_QK, TW], F32R) for r in range(2)]
        k_l = [ph.sb(f"k_l{r}", [B_QK, TW], F32R) for r in range(2)]
        v_h = [ph.sb(f"v_h{r}", [P, VW], F32R) for r in range(2)]
        v_l = [ph.sb(f"v_l{r}", [P, VW], F32R) for r in range(2)]
        gate = [ph.sb(f"gate{r}", [P, P]) for r in range(2)]
        weight = ph.sb("weight", [P, P])
        score = ph.sb("score", [P, P])
        s_h = [ph.sb(f"s_h{r}", [P, P], F32R) for r in range(2)]
        s_l = [ph.sb(f"s_l{r}", [P, P], F32R) for r in range(2)]
        k_w = ph.sb("k_w", [P, B_QK])
        kw_h = [ph.sb(f"kw_h{r}", [P, B_QK], F32R) for r in range(2)]
        kw_l = [ph.sb(f"kw_l{r}", [P, B_QK], F32R) for r in range(2)]
        state = ph.sb("state", [B_QK, VW])
        state_h, state_l = ph.sb("state_h", [B_QK, VW], F32R), ph.sb("state_l", [B_QK, VW], F32R)
        mix = ph.sb("mix", [P, VW])
        den = ph.sb("den", [P, 3])
        y = [ph.sb(f"y{r}", [P, P]) for r in range(2)]
        bound = ph.sb("bound", [P, P])
        qk_ps, s_ps, kn_ps, grow_ps = ph.ps("qk_ps"), ph.ps("s_ps"), ph.ps("kn_ps"), ph.ps("grow_ps")
        v_ps = [ph.ps(f"v_ps{r}") for r in range(2)]
        mix_ps = [ph.ps(f"mix_ps{r}") for r in range(2)]
        y_stored = ph.sems("y_stored0", "y_stored1")
        row_loaded = ph.sems("row_loaded0", "row_loaded1")
        qk_loaded, v_loaded, decay_loaded, set_up = ph.sems("qk_loaded", "v_loaded", "decay_loaded", "set_up")
        PE_SEMS = qk_projected, v_projected, scored, k_turned, mixed, grown = ph.sems(
            "qk_projected", "v_projected", "scored", "k_turned", "mixed", "grown")
        ACT_SEMS = (wqk_rounded, wv_rounded, q_rounded, k_rounded, k_copied, v_rounded, og_tanh, weighed,
                    s_rounded, kw_rounded, state_rounded) = ph.sems(
            "wqk_rounded", "wv_rounded", "q_rounded", "k_rounded", "k_copied", "v_rounded", "og_tanh", "weighed",
            "s_rounded", "kw_rounded", "state_rounded")
        DVE_SEMS = (wv_split_dve, col_copied, qk_split, v_split, bounded, z_gated, gated, scaled, s_split, k_weighed,
                    kw_split, grown_state, state_split, summed, den_abs, den_max, inverted, y_made) = ph.sems(
            "wv_split_dve", "col_copied", "qk_split", "v_split", "bounded", "z_gated", "gated", "scaled", "s_split",
            "k_weighed", "kw_split", "grown_state", "state_split", "summed", "den_abs", "den_max", "inverted",
            "y_made")
        POOL_SEMS = wqk_split, wv_split_pool = ph.sems("wqk_split", "wv_split_pool")
        waits_met_pe, waits_met_sp = ph.sems("waits_met_pe", "waits_met_sp")
        block = ph.block()

        def before(count, b):
            return PRE + count + (b if b == 0 else b - 1)

        def tile_used(i, t):
            return PRE + 17 * i + (15, 0, 3, 6, 9, 12)[t]

        def in_tile(b):
            c = start(b) - tile_cols(b // 3)[0]
            return slice(c, c + length(b))

        @block.sync
        def _(sp):
            for sem in y_stored:
                sp.sem_inc(sem, 16)

            def load_weights(unit, head):
                src = w_in.rearrange("(k p) n -> p k n", p=P)
                sp.wait_ge(wqk_split, PRE + unit)
                sp.sem_inc(waits_met_sp, 1)
                for j, at in enumerate((0, B_K0)):
                    sp.dma_start(raw_qk[:, :, B_QK * j:B_QK * j + B_QK],
                                 src[:, :, bass.ds(head * B_QK + at, B_QK)]).then_inc(qk_loaded, 16)
                sp.wait_ge(wv_split_pool, PRE + 2 * unit)
                sp.wait_ge(wv_split_dve, PRE + 2 * unit)
                sp.sem_inc(waits_met_sp, 1)
                for j, at in enumerate((B_V0, B_O0, B_Z0)):
                    sp.dma_start(raw_v[:, :, P * j:P * j + P],
                                 src[:, :, bass.ds(head * P + at, P)]).then_inc(v_loaded, 16)

            def load_row(i, t):
                a, z = tile_cols(t)
                sp.wait_ge(bounded, PRE + 17 * i + (-2, 0, 3, 6, 9, 12)[t])
                sp.sem_inc(waits_met_sp, 1)
                sp.dma_start(row[t % 2][:, :z - a],
                             row_a[bass.ds(i * T + a, z - a)].partition_broadcast(P)).then_inc(row_loaded[t % 2], 16)

            load_weights(0, 0)
            with sp.Fori(0, B_HEADS) as i:
                load_row(i, 0)
                sp.wait_ge(grown_state, PRE + 16 * i)
                sp.sem_inc(waits_met_sp, 1)
                sp.dma_start(decay[:, :], row_dec[bass.ds(i * NB, NB)].partition_broadcast(B_QK)
                             ).then_inc(decay_loaded, 16)
                load_row(i, 1)
                load_weights(i + 1, (i + 1) % B_HEADS)
                for s in range(20):
                    if s in (3, 6, 9, 12):
                        load_row(i, s // 3 + 1)
                    b = s - 3
                    if b >= 0:
                        sp.wait_ge(y_made, PRE + 17 * i + b + 1)
                        sp.dma_start(y_out[start(b):start(b) + length(b), bass.ds(i * P, P)],
                                     y[b % 2][:length(b), :]).then_inc(y_stored[b % 2], 16)
            sp.wait_ge(y_stored[0], 16 * (1 + 9 * B_HEADS))
            sp.wait_ge(y_stored[1], 16 * (1 + 8 * B_HEADS))

        @block.gpsimd
        def _(pool):
            for sem in POOL_SEMS:
                pool.sem_inc(sem, PRE)
            for r in range(2):
                pool.memset(v_h[r][:, :].bitcast(F32), 0.0)
                pool.memset(v_l[r][:, :].bitcast(F32), 0.0).then_inc(set_up, 1)
            pool.memset(bound[:, :], 0.0).then_inc(set_up, 1)
            pool.wait_ge(set_up, 3)
            for r in range(2):
                pool.memset(v_h[r][:, B_V:B_V + 1].bitcast(F32), 1.0)
            pool.affine_select(out=bound[:, :], in_=bound[:, :], compare_op=ALU.is_ge, fill=MASKED, base=0,
                               pattern=[[1, P]], channel_multiplier=-1).then_inc(set_up, 1)

            def split_qk(unit):
                pool.wait_ge(wqk_rounded, PRE + unit + 1)
                pool.tensor_tensor(wqk_l[:, :, :], raw_qk[:, :, :], wqk_h[:, :, :].bitcast(F32),
                                   ALU.subtract).then_inc(wqk_split, 1)

            def split_v(unit):
                for n, ks in ((2, slice(2, 4)), (4, slice(6, 8))):
                    pool.wait_ge(wv_rounded, PRE + 4 * unit + n)
                    pool.tensor_tensor(wv_l[:, ks, :], raw_v[:, ks, :], wv_h[:, ks, :].bitcast(F32),
                                       ALU.subtract).then_inc(wv_split_pool, 1)

            split_qk(0)
            split_v(0)
            with pool.Fori(0, B_HEADS) as i:
                split_qk(i + 1)
                split_v(i + 1)

        @block.scalar
        def _(act):
            for sem in ACT_SEMS:
                act.sem_inc(sem, PRE)

            def round_qk_weights(unit):
                act.wait_ge(qk_loaded, 32 * (unit + 1))
                act.wait_ge(qk_projected, PRE + 6 * unit)
                act.activation(wqk_h[:, :, :], raw_qk[:, :, :], ACT.Copy).then_inc(wqk_rounded, 1)

            def round_v_weights(unit):
                act.wait_ge(v_loaded, 48 * (unit + 1))
                act.wait_ge(v_projected, PRE + 17 * unit)
                for n in range(4):
                    ks = slice(2 * n, 2 * n + 2)
                    act.activation(wv_h[:, ks, :], raw_v[:, ks, :], ACT.Copy).then_inc(wv_rounded, 1)

            def round_qk(i, t, m):
                w, r = tile_cols(t)[1] - tile_cols(t)[0], t % 2
                act.wait_ge(qk_projected, PRE + m + 1)
                if i is not None:
                    act.wait_ge(mixed, tile_used(i, t))
                act.activation(q_h[r][:, :w], qk_ps[:B_QK, :w], ACT.Copy)
                act.activation(k_f[r][:, :w], qk_ps[B_QK:, :w], ACT.Copy, scale=B_QK ** -0.5).then_inc(k_copied, 1)
                act.wait_ge(k_copied, PRE + m + 1)
                act.activation(k_h[r][:, :w], k_f[r][:, :w], ACT.Copy).then_inc(k_rounded, 1)

            round_qk_weights(0)
            round_v_weights(0)
            act.wait_ge(set_up, 4)
            round_qk(None, 0, 0)
            with act.Fori(0, B_HEADS) as i:
                for s in range(18):
                    r, m = s % 2, length(s)
                    if s < NB:
                        act.wait_ge(v_projected, PRE + 17 * i + s + 1)
                        act.wait_ge(mixed, before(17 * i, s))
                        act.wait_ge(grown, before(16 * i, s))
                        act.activation(v_h[r][:m, :B_V], v_ps[r][:m, :B_V], ACT.Copy).then_inc(v_rounded, 1)
                        act.wait_ge(y_made, before(17 * i, s))
                        o, z = v_ps[r][:m, B_V:2 * B_V], v_ps[r][:m, 2 * B_V:3 * B_V]
                        act.activation(o, o, ACT.Tanh, scale=0.5)
                        act.activation(gate[r][:m, :], z, ACT.Tanh, scale=0.5).then_inc(og_tanh, 1)
                        act.wait_ge(bounded, PRE + 17 * i + s + 1)
                        act.activation(weight[:m, :m], weight[:m, :m], ACT.Exp).then_inc(weighed, 1)
                    if s >= 2:
                        act.wait_ge(grown_state, PRE + 16 * i + s - 1)
                        act.wait_ge(mixed, PRE + 17 * i + s - 1)
                        act.activation(state_h[:, :], state[:, :], ACT.Copy).then_inc(state_rounded, 1)
                    if s < NB:
                        act.wait_ge(scaled, PRE + 17 * i + s + 1)
                        act.activation(s_h[r][:m, :m], score[:m, :m], ACT.Copy).then_inc(s_rounded, 1)
                    if s < NB - 1:
                        act.wait_ge(k_weighed, PRE + 16 * i + s + 1)
                        act.activation(kw_h[r][:m, :], k_w[:m, :], ACT.Copy).then_inc(kw_rounded, 1)
                    if s % 3 == 2:
                        round_qk(i, (s // 3 + 1) % 6, 6 * i + s // 3 + 1)
                    if s == 14:
                        round_qk_weights(i + 1)
                    if s == 17:
                        round_v_weights(i + 1)

        @block.vector
        def _(dve):
            for sem in DVE_SEMS:
                dve.sem_inc(sem, PRE)

            def split_v_weights(unit):
                for n, ks in ((1, slice(0, 2)), (3, slice(4, 6))):
                    dve.wait_ge(wv_rounded, PRE + 4 * unit + n)
                    dve.tensor_tensor(wv_l[:, ks, :], raw_v[:, ks, :], wv_h[:, ks, :].bitcast(F32),
                                      ALU.subtract).then_inc(wv_split_dve, 1)

            def split_qk(t, m):
                w, r = tile_cols(t)[1] - tile_cols(t)[0], t % 2
                dve.wait_ge(k_rounded, PRE + m + 1)
                dve.tensor_tensor(q_l[r][:, :w], qk_ps[:B_QK, :w], q_h[r][:, :w].bitcast(F32), ALU.subtract)
                dve.scalar_tensor_tensor(out=k_l[r][:, :w], in0=qk_ps[B_QK:, :w], scalar=B_QK ** -0.5,
                                         in1=k_h[r][:, :w].bitcast(F32), op0=ALU.mult,
                                         op1=ALU.subtract).then_inc(qk_split, 1)

            def grow(i, b):
                dve.wait_ge(grown, PRE + 16 * i + b + 1)
                dve.wait_ge(state_split, PRE + 16 * i + b)
                if b == 0:
                    ins = dve.tensor_copy(state[:, :], grow_ps[:B_QK, :VW])
                else:
                    dve.wait_ge(grown_state, PRE + 16 * i + b)
                    ins = dve.scalar_tensor_tensor(out=state[:, :], in0=state[:, :], scalar=decay[:, b:b + 1],
                                                   in1=grow_ps[:B_QK, :VW], op0=ALU.mult, op1=ALU.add)
                ins.then_inc(grown_state, 1)

            def split_state(i, b):
                dve.wait_ge(state_rounded, PRE + 16 * i + b + 1)
                dve.tensor_tensor(state_l[:, :], state[:, :], state_h[:, :].bitcast(F32),
                                  ALU.subtract).then_inc(state_split, 1)

            def make_y(i, b):
                m, r = length(b), b % 2
                n = 17 * i + b
                dve.wait_ge(mixed, PRE + n + 1)
                dve.wait_ge(y_made, PRE + n)
                if b == 0:
                    ins = dve.tensor_copy(mix[:m, :B_V + 1], mix_ps[r][:m, :B_V + 1])
                else:
                    ins = dve.tensor_scalar(mix[:m, :B_V + 1], mix_ps[r][:m, 256:256 + B_V + 1],
                                            col[:m, 1, b:b + 1], None, ALU.mult)
                ins.then_inc(summed, 1)
                dve.wait_ge(summed, PRE + 2 * n + 1)
                if b == 0:
                    dve.sem_inc(summed, 1)
                else:
                    dve.tensor_tensor(mix[:m, :B_V + 1], mix[:m, :B_V + 1], mix_ps[r][:m, :B_V + 1],
                                      ALU.add).then_inc(summed, 1)
                dve.wait_ge(summed, PRE + 2 * n + 2)
                dve.scalar_tensor_tensor(out=den[:m, 0:1], in0=mix[:m, B_V:B_V + 1], scalar=-1.0,
                                         in1=mix[:m, B_V:B_V + 1], op0=ALU.mult, op1=ALU.max).then_inc(den_abs, 1)
                dve.wait_ge(den_abs, PRE + n + 1)
                dve.tensor_scalar(den[:m, 1:2], den[:m, 0:1], col[:m, 2, b:b + 1], 4.0, ALU.max,
                                  ALU.mult).then_inc(den_max, 1)
                dve.wait_ge(den_max, PRE + n + 1)
                dve.reciprocal(den[:m, 2:3], den[:m, 1:2]).then_inc(inverted, 1)
                dve.wait_ge(inverted, PRE + n + 1)
                dve.wait_ge(y_stored[r], 16 * (1 + (9 - r) * i + b // 2))
                dve.scalar_tensor_tensor(out=y[r][:m, :], in0=mix[:m, :B_V], scalar=den[:m, 2:3],
                                         in1=gate[r][:m, :], op0=ALU.mult, op1=ALU.mult).then_inc(y_made, 1)

            split_v_weights(0)
            dve.wait_ge(set_up, 4)
            split_qk(0, 0)
            with dve.Fori(0, B_HEADS) as i:
                for s in range(19):
                    r, m, n = s % 2, length(s), 17 * i + s
                    if s < NB:
                        if s == 0:
                            dve.wait_ge(y_made, PRE + 17 * i)
                            dve.tensor_copy(col[:, :, :], head_cols[:, :, :, bass.ds(i, 1)].rearrange(
                                "p q b o -> p q (b o)")).then_inc(col_copied, 1)
                            dve.wait_ge(col_copied, PRE + i + 1)
                        if s % 3 == 0:
                            t = s // 3
                            dve.wait_ge(row_loaded[t % 2], 16 * (3 * i + t // 2 + 1))
                        dve.wait_ge(scaled, PRE + n)
                        dve.wait_ge(k_weighed, PRE + 16 * i + min(s, 16))
                        dve.scalar_tensor_tensor(out=weight[:m, :m], in0=row[(s // 3) % 2][:m, in_tile(s)],
                                                 scalar=col[:m, 0, s:s + 1], in1=bound[:m, :m],
                                                 op0=ALU.add, op1=ALU.min).then_inc(bounded, 1)
                    if s == 2:
                        dve.wait_ge(decay_loaded, 16 * (i + 1))
                    if 0 <= s - 2 < NB - 1:
                        grow(i, s - 2)
                    if 0 <= s - 2 < NB:
                        make_y(i, s - 2)
                    if s < NB:
                        dve.wait_ge(og_tanh, PRE + n + 1)
                        dve.wait_ge(mixed, before(17 * i, s))
                        dve.wait_ge(grown, before(16 * i, s))
                        dve.tensor_tensor(v_l[r][:m, :B_V], v_ps[r][:m, :B_V], v_h[r][:m, :B_V].bitcast(F32),
                                          ALU.subtract).then_inc(v_split, 1)
                        dve.scalar_tensor_tensor(out=gate[r][:m, :], in0=gate[r][:m, :], scalar=1.0,
                                                 in1=v_ps[r][:m, 2 * P:3 * P], op0=ALU.add,
                                                 op1=ALU.mult).then_inc(z_gated, 1)
                        dve.wait_ge(z_gated, PRE + n + 1)
                        dve.scalar_tensor_tensor(out=gate[r][:m, :], in0=v_ps[r][:m, P:2 * P], scalar=1.0,
                                                 in1=gate[r][:m, :], op0=ALU.add, op1=ALU.mult).then_inc(gated, 1)
                        dve.wait_ge(weighed, PRE + n + 1)
                        dve.wait_ge(scored, PRE + n + 1)
                        dve.wait_ge(s_split, PRE + n)
                        dve.tensor_tensor(score[:m, :m], s_ps[:m, :m], weight[:m, :m], ALU.mult
                                          ).then_inc(scaled, 1)
                    if s < NB - 1:
                        dve.wait_ge(k_turned, PRE + 16 * i + s + 1)
                        dve.wait_ge(kw_split, PRE + 16 * i + s)
                        dve.tensor_scalar(k_w[:m, :], kn_ps[:m, :B_QK], weight[:m, m - 1:m], None,
                                          ALU.mult).then_inc(k_weighed, 1)
                    if 0 <= s - 2 < NB - 1:
                        split_state(i, s - 2)
                    if s < NB:
                        dve.wait_ge(s_rounded, PRE + n + 1)
                        dve.tensor_tensor(s_l[r][:m, :m], score[:m, :m], s_h[r][:m, :m].bitcast(F32),
                                          ALU.subtract).then_inc(s_split, 1)
                    if s < NB - 1:
                        dve.wait_ge(kw_rounded, PRE + 16 * i + s + 1)
                        dve.tensor_tensor(kw_l[r][:m, :], k_w[:m, :], kw_h[r][:m, :].bitcast(F32),
                                          ALU.subtract).then_inc(kw_split, 1)
                    if s % 3 == 2:
                        split_qk((s // 3 + 1) % 6, 6 * i + s // 3 + 1)
                    if s == 17:
                        split_v_weights(i + 1)

        @block.tensor
        def _(pe):
            for sem in PE_SEMS:
                pe.sem_inc(sem, PRE)

            def project_qk(m, t, ks):
                a, z = tile_cols(t)
                if ks[0] == 0:
                    pe.wait_ge(qk_split, PRE + m)
                for k in ks:
                    last = product(pe, qk_ps[:, :z - a], wqk_h[:, k, :], wqk_l[:, k, :], u_h[:, k, a:z],
                                   u_l[:, k, a:z], k == 0, k == KT - 1)
                if ks[-1] == KT - 1:
                    last.then_inc(qk_projected, 1)

            def project_v(i, b):
                m, r = length(b), b % 2
                c = slice(start(b), start(b) + m)
                pe.wait_ge(gated, before(17 * i, b))
                for k in range(KT):
                    if b == 0 and k % 2 == 0:
                        split, n = (wv_split_dve, wv_split_pool)[k // 2 % 2], k // 4 + 1
                        pe.wait_ge(split, PRE + 2 * i + n)
                    last = product(pe, v_ps[r][:m, :3 * P], u_h[:, k, c], u_l[:, k, c], wv_h[:, k, :], wv_l[:, k, :],
                                   k == 0, k == KT - 1)
                last.then_inc(v_projected, 1)

            pe.wait_ge(wqk_split, PRE + 1)
            project_qk(0, 0, range(KT))
            with pe.Fori(0, B_HEADS) as i:
                for s in range(18):
                    r, m, n = s % 2, length(s), 17 * i + s
                    if s < NB:
                        project_v(i, s)
                        if s % 3 == 0:
                            pe.wait_ge(qk_split, PRE + 6 * i + s // 3 + 1)
                        pe.wait_ge(scaled, PRE + n)
                        if s == 0:
                            pe.sem_inc(waits_met_pe, 1)
                        tr, c = (s // 3) % 2, in_tile(s)
                        product(pe, s_ps[:m, :m], k_h[tr][:, c], k_l[tr][:, c], q_h[tr][:, c], q_l[tr][:, c],
                                True, True).then_inc(scored, 1)
                    if s < NB - 1:
                        pe.wait_ge(k_weighed, PRE + 16 * i + s)
                        pe.sem_inc(waits_met_pe, 1)
                        pe.transpose(kn_ps[:m, :B_QK], k_f[tr][:, c], ident_of[tr]).then_inc(k_turned, 1)
                    if s == 15:
                        pe.wait_ge(wqk_split, PRE + i + 2)
                    project_qk(6 * i + s // 3 + 1, (s // 3 + 1) % 6, (range(0, 3), range(3, 6), range(6, 8))[s % 3])
                    if s > 0:
                        b, q = s - 1, 1 - r
                        m, n = length(b), n - 1
                        tr, c = (b // 3) % 2, in_tile(b)
                        pe.wait_ge(s_split, PRE + n + 1)
                        pe.wait_ge(summed, PRE + 34 * i + 2 * (b if b == 0 else b - 1))
                        if b == 0:
                            pe.sem_inc(waits_met_pe, 1)
                        last = product(pe, mix_ps[q][:m, :VW], s_h[q][:m, :m], s_l[q][:m, :m], v_h[q][:m, :],
                                       v_l[q][:m, :], True, True)
                        if b > 0:
                            pe.wait_ge(state_split, PRE + 16 * i + b)
                            last = product(pe, mix_ps[q][:m, 256:256 + VW], q_h[tr][:, c], q_l[tr][:, c],
                                           state_h[:, :], state_l[:, :], True, True)
                        last.then_inc(mixed, 1)
                        if b < NB - 1:
                            pe.wait_ge(kw_split, PRE + 16 * i + b + 1)
                            pe.wait_ge(grown_state, PRE + 16 * i + b)
                            if b == 0:
                                pe.sem_inc(waits_met_pe, 1)
                            product(pe, grow_ps[:B_QK, :VW], kw_h[q][:m, :], kw_l[q][:m, :], v_h[q][:m, :],
                                    v_l[q][:m, :], True, True).then_inc(grown, 1)


def decoder(nc, x, meta, norm_a, w_in_a, sinks_a, w_out_a, norm_b, w_in_b, b_gates_b, w_out_b, norm_f, rope_table,
            out):
    x, out = x[0], out[0]
    y_t = nc.dram_tensor("y_t", [D, T], F32).ap()
    h1 = nc.dram_tensor("h1", [T, D], F32).ap()
    u_t = nc.dram_tensor("u_t", [D, T], F32).ap()
    y_b = nc.dram_tensor("y_b", [T, D], F32).ap()
    row_a = nc.dram_tensor("row_a", [B_HEADS * T], F32).ap()
    row_dec = nc.dram_tensor("row_dec", [B_HEADS * NB], F32).ap()
    with ExitStack() as stack:
        ident = stack.enter_context(nc.sbuf_tensor("ident", [P, P], F32))
        ident_made = stack.enter_context(nc.semaphore("ident_made"))
        with nc.Block() as block:
            @block.gpsimd
            def _(pool):
                pool.memset(ident[:, :], 0.0).then_inc(ident_made, 1)
                pool.wait_ge(ident_made, 1)
                pool.affine_select(out=ident[:, :], in_=ident[:, :], compare_op=ALU.not_equal, fill=1.0, base=0,
                                   pattern=[[-1, P]], channel_multiplier=1).then_inc(ident_made, 1)

        def u_tiles(inner, layer):
            return [inner.enter_context(nc.sbuf_tensor(f"u{layer}_{part}", [P, KT, T], F32R)) for part in "hl"]

        with ExitStack() as inner:
            u_h, u_l = u_tiles(inner, 0)
            norm_in(nc, x, meta, norm_a[0], ident, u_h, u_l)
            attention(nc, w_in_a[0], sinks_a[0], rope_table, ident, u_h, u_l, y_t)
        project_out(nc, "pa", w_out_a[0], y_t,
                    lambda n: meta if isinstance(n, int) and n == 0 else x[bass.ds(P * n - P, P), :],
                    norm_b[0], ident, (h1, u_t))
        with ExitStack() as inner:
            u_h, u_l = u_tiles(inner, 1)
            head_cols = inner.enter_context(nc.sbuf_tensor("head_cols", [P, 3, NB, B_HEADS], F32))
            gates(nc, u_t, w_in_b[0], b_gates_b[0], ident, u_h, u_l, head_cols, row_a, row_dec)
            mlstm(nc, w_in_b[0], ident, u_h, u_l, head_cols, row_a, row_dec, y_b)
        project_out(nc, "pb", w_out_b[0], y_b, lambda n: h1[bass.ds(P * n + META, P), :], norm_f, ident, (out,))


def rope_constants():
    import numpy as np
    half = A_HD // 2
    inv = np.float32(10000.0) ** (-np.arange(half, dtype=np.float32) / np.float32(half))
    angle = (np.arange(T, dtype=np.float32)[None, :] * inv[:, None].astype(np.float32)).astype(np.float32)
    table = np.empty((P // half, half, 2, T), np.float32)
    table[:, :, 0] = np.cos(angle)
    table[0::2, :, 1] = -np.sin(angle)
    table[1::2, :, 1] = np.sin(angle)
    return table.reshape(P, 2, T)


_INS = ["x", "meta", "norm_a", "w_in_a", "sinks_a", "w_out_a", "norm_b", "w_in_b", "b_gates_b", "w_out_b", "norm_f"]


def kernel(**inputs):
    import numpy as np
    from concourse import bacc
    from concourse.bass_utils import run_bass_kernel_spmd

    nc = bacc.Bacc("TRN2", target_bir_lowering=False, num_devices=1)
    arrays = {f"in_{name}": np.ascontiguousarray(inputs[name]) for name in _INS}
    arrays["in_rope"] = rope_constants()
    args = [nc.dram_tensor(name, a.shape, mybir.dt.from_np(a.dtype), kind="ExternalInput").ap()
            for name, a in arrays.items()]
    args.append(nc.dram_tensor("out_dram", (1, SEQ, D), F32, kind="ExternalOutput").ap())
    decoder(nc, *args)
    return run_bass_kernel_spmd(nc, [arrays], core_ids=[0]).results[0]["out_dram"]
```

```python
from contextlib import ExitStack

import concourse.bass as bass
from concourse import mybir

F32 = mybir.dt.float32
F32R = mybir.dt.float32r
ALU = mybir.AluOpType
ACT = mybir.ActivationFunctionType

P = 128
D = 1024
KT = D // P
META = 16
SEQ = 2048
T = META + SEQ
NB = 1 + SEQ // P
EPS = 1e-6

A_HEADS, A_KV, A_HD = 16, 2, 64
A_PAIRS = A_HEADS // 2
A_K0 = A_HEADS * A_HD
A_V0 = A_K0 + A_KV * A_HD
A_Z0 = A_V0 + A_KV * A_HD
MASKED = -1.0e30

B_HEADS, B_QK, B_V = 8, 64, 128
B_K0 = B_HEADS * B_QK
B_V0 = 2 * B_HEADS * B_QK
B_O0 = B_V0 + B_HEADS * B_V
B_Z0 = B_O0 + B_HEADS * B_V
B_G0 = B_Z0 + B_HEADS * B_V

TILES = [(3 * t, min(3 * t + 3, NB)) for t in range(6)]
TW = 3 * P
PRE = 3


def start(b):
    return 0 if b == 0 else META + P * (b - 1)


def length(b):
    return META if b == 0 else P


def tile_cols(t):
    b0, b1 = TILES[t]
    return start(b0), start(b1 - 1) + length(b1 - 1)


class Phase:

    def __init__(self, nc, stack, name):
        self.nc, self.stack, self.name, self.all_sems = nc, stack, name, []

    def sb(self, name, shape, dtype=F32):
        return self.stack.enter_context(self.nc.sbuf_tensor(f"{self.name}_{name}", shape, dtype))

    def ps(self, name):
        return self.stack.enter_context(self.nc.psum_tensor(f"{self.name}_{name}", [P, 512], F32))

    def sems(self, *names):
        new = [self.stack.enter_context(self.nc.semaphore(f"{self.name}_{n}")) for n in names]
        self.all_sems += new
        return new

    def block(self):
        self.stack.callback(self.clear)
        return self.stack.enter_context(self.nc.Block())

    def clear(self):
        with self.nc.Block() as block:
            @block.sync
            def _(sp):
                for sem in self.all_sems:
                    sp.sem_clear(sem)


def product(pe, out, a_h, a_l, b_h, b_l, first, last):
    pe.matmul(out, a_h, b_h, start=first, stop=False)
    pe.matmul(out, a_l, b_h, start=False, stop=False)
    return pe.matmul(out, a_h, b_l, start=False, stop=last)


def over_blocks(eng, step, lags):
    for n in range(5):
        step(n, n % 4)
    with eng.Fori(0, (NB - 5) // 4) as i:
        for j in range(4):
            step(4 * i + (5 + j), (5 + j) % 4)
    for n in range(NB, NB + lags):
        step(n, n % 4)


def has(n, lag=0):
    return not isinstance(n, int) or 0 <= n - lag < NB


def size(n):
    return length(n) if isinstance(n, int) else P


def cols(n):
    return bass.ds(start(n), length(n)) if isinstance(n, int) else bass.ds(P * n - (P - META), P)


def load_pair_weights(sp, raw, w_in, columns, loaded):
    for h in range(2):
        src = w_in[bass.ds(D // 2 * h, D // 2), :].rearrange("(k p) n -> p k n", p=P)
        for e, at in enumerate(columns):
            sp.dma_start(raw[h][:, :, A_HD * e:A_HD * e + A_HD], src[:, :, bass.ds(at, A_HD)]
                         ).then_inc(loaded[h], 16)


def norm_in(nc, x, meta, norm_g, w_in, ident, u_h, u_l, weights):
    raw, w_h, w_l = weights
    with ExitStack() as stack:
        ph = Phase(nc, stack, "n")
        x_in = [ph.sb(f"x{r}", [P, D]) for r in range(4)]
        xs = [ph.sb(f"xs{p}", [P, D]) for p in range(2)]
        gain = ph.sb("gain", [P, D])
        squares = ph.sb("squares", [P, D])
        stat = ph.sb("stat", [P, 6])
        eps = ph.sb("eps", [P, 1])
        turned = [[ph.ps(f"turned{p}{half}") for half in range(2)] for p in range(2)]
        x_loaded = ph.sems(*(f"x_loaded{r}" for r in range(4)))
        (consts, gain_loaded, summed, rooted, inverted, scaled, transposed, rounded, remaindered, k_loaded, v_loaded,
         k_rounded, k_split) = ph.sems(
            "consts", "gain_loaded", "summed", "rooted", "inverted", "scaled", "transposed", "rounded",
            "remaindered", "k_loaded", "v_loaded", "k_rounded", "k_split")
        block = ph.block()
        used = lambda n, ring: not isinstance(n, int) or n >= ring

        @block.sync
        def _(sp):
            def step(n, r):
                if used(n, 4):
                    sp.wait_ge(scaled, n - 3)
                src = meta if isinstance(n, int) and n == 0 else x[bass.ds(P * n - P, P), :]
                sp.dma_start(x_in[r][:size(n), :], src).then_inc(x_loaded[r], 16)
                if isinstance(n, int) and n == 0:
                    sp.dma_start(gain[:, :], norm_g.partition_broadcast(P)).then_inc(gain_loaded, 16)
                if isinstance(n, int) and n == 3:
                    load_pair_weights(sp, raw, w_in, (A_K0, A_K0 + A_HD), (k_loaded, k_loaded))
            over_blocks(sp, step, 0)
            sp.wait_ge(k_split, 2)
            load_pair_weights(sp, raw, w_in, (A_V0, A_V0 + A_HD), (v_loaded, v_loaded))
            sp.wait_ge(v_loaded, 64)

        @block.gpsimd
        def _(pool):
            pool.memset(eps[:, :], EPS).then_inc(consts, 1)
            for h in range(2):
                pool.wait_ge(k_rounded, h + 1)
                ks = slice(4 * h, 4 * h + 4)
                pool.tensor_tensor(w_l["q"][:, ks, :], raw[h][:, :, :], w_h["q"][:, ks, :].bitcast(F32),
                                   ALU.subtract).then_inc(k_split, 1)

        @block.scalar
        def _(act):
            act.wait_ge(consts, 1)

            def step(n, r):
                p = r % 2
                if has(n):
                    m = size(n)
                    act.wait_ge(x_loaded[r], 4 * n + (16 - 4 * r))
                    if used(n, 1):
                        act.wait_ge(rooted, n)
                    if used(n, 2):
                        act.wait_ge(inverted, n - 1)
                    act.activation(squares[:m, :], x_in[r][:m, :], ACT.Square,
                                   accum_out=stat[:m, 3 * p:3 * p + 1]).then_inc(summed, 1)
                    act.wait_ge(summed, n + 1)
                    act.activation(stat[:m, 3 * p + 1:3 * p + 2], stat[:m, 3 * p:3 * p + 1], ACT.Sqrt,
                                   bias=eps[:m, :], scale=1.0 / D).then_inc(rooted, 1)
                if has(n, 2):
                    m = size(n - 2) if isinstance(n, int) else P
                    act.wait_ge(transposed, n - 1)
                    for half in range(2):
                        src = turned[p][half][:, :].rearrange("p (k t) -> p k t", k=4)[:, :, :m]
                        act.activation(u_h[:, 4 * half:4 * half + 4, cols(n - 2)], src,
                                       ACT.Copy).then_inc(rounded, 1)
                if isinstance(n, int) and n == 4:
                    act.wait_ge(k_loaded, 64)
                    for h in range(2):
                        act.activation(w_h["q"][:, 4 * h:4 * h + 4, :], raw[h][:, :, :], ACT.Copy
                                       ).then_inc(k_rounded, 1)
            over_blocks(act, step, 2)

        @block.vector
        def _(dve):
            dve.wait_ge(gain_loaded, 16)

            def step(n, r):
                p = r % 2
                if has(n):
                    m = size(n)
                    dve.wait_ge(rooted, n + 1)
                    if used(n, 2):
                        dve.wait_ge(transposed, n - 1)
                    dve.reciprocal(stat[:m, 3 * p + 2:3 * p + 3],
                                   stat[:m, 3 * p + 1:3 * p + 2]).then_inc(inverted, 1)
                    dve.wait_ge(inverted, n + 1)
                    dve.scalar_tensor_tensor(out=xs[p][:m, :], in0=x_in[r][:m, :],
                                             scalar=stat[:m, 3 * p + 2:3 * p + 3], in1=gain[:m, :],
                                             op0=ALU.mult, op1=ALU.mult).then_inc(scaled, 1)
                if has(n, 2):
                    m = size(n - 2) if isinstance(n, int) else P
                    for half in range(2):
                        dve.wait_ge(rounded, 2 * n + (half - 3))
                        src = turned[p][half][:, :].rearrange("p (k t) -> p k t", k=4)[:, :, :m]
                        ks = slice(4 * half, 4 * half + 4)
                        dve.tensor_tensor(u_l[:, ks, cols(n - 2)], src,
                                          u_h[:, ks, cols(n - 2)].bitcast(F32),
                                          ALU.subtract).then_inc(remaindered, 1)
            over_blocks(dve, step, 2)

        @block.tensor
        def _(pe):
            def step(n, r):
                m, p = size(n), r % 2
                pe.wait_ge(scaled, n + 1)
                if used(n, 2):
                    pe.wait_ge(remaindered, 2 * (n - 1))
                for k in range(KT):
                    last = pe.transpose(turned[p][k // 4][:, (k % 4) * P:(k % 4) * P + m],
                                        xs[p][:m, k * P:(k + 1) * P], ident[:m, :m])
                last.then_inc(transposed, 1)
            over_blocks(pe, step, 0)


def pair_weights(nc, stack):
    new = lambda name, *kind: stack.enter_context(nc.sbuf_tensor(name, *kind))
    raw = [new(f"w_raw{h}", [P, KT // 2, P], F32) for h in range(2)]
    w_h = {n: new(f"w{n}_h", [P, KT, P], F32R) for n in ("q", "z")}
    w_l = {n: new(f"w{n}_l", [P, KT, P], F32R) for n in ("q", "z")}
    return raw, w_h, w_l


def attention(nc, w_in, sinks, rope_table, ident, u_h, u_l, y_t, weights):
    raw, w_h, w_l = weights
    with ExitStack() as stack:
        ph = Phase(nc, stack, "a")
        k_h, k_l = ph.sb("k_h", [P, T], F32R), ph.sb("k_l", [P, T], F32R)
        v_h, v_l = ph.sb("v_h", [P, NB, P], F32R), ph.sb("v_l", [P, NB, P], F32R)
        rope = ph.sb("rope", [P, 2, TW])
        q_f, q_s = ph.sb("q_f", [P, TW]), ph.sb("q_s", [P, TW])
        q_h = [ph.sb(f"q_h{r}", [P, TW], F32R) for r in range(2)]
        q_l = [ph.sb(f"q_l{r}", [P, TW], F32R) for r in range(2)]
        gate = [ph.sb(f"gate{r}", [P, TW]) for r in range(2)]
        prob = [ph.sb(f"prob{r}", [P, 2, 1 + 2 * P]) for r in range(2)]
        pt_h, pt_l = ph.sb("pt_h", [P, 512], F32R), ph.sb("pt_l", [P, 512], F32R)
        y = [ph.sb(f"y{r}", [P, P]) for r in range(2)]
        mask = ph.sb("mask", [P, 2 * P])
        neg_sink = ph.sb("neg_sink", [P, A_HEADS])
        sink = ph.sb("sink", [P, 2])
        stat = [ph.sb(f"stat{r}", [P, 6]) for r in range(2)]
        NEG, SUM, INV = (slice(2 * n, 2 * n + 2) for n in range(3))
        q_ps, z_ps = ph.ps("q_ps"), ph.ps("z_ps")
        s_ps = [ph.ps(f"s_ps{e}") for e in range(2)]
        pt_ps = [ph.ps(f"pt_ps{r}") for r in range(2)]
        o_ps = [ph.ps(f"o_ps{r}") for r in range(2)]
        raw_loaded = ph.sems("raw_loaded0", "raw_loaded1")
        y_stored = ph.sems("y_stored0", "y_stored1")
        (sinks_loaded, sinks_negated, mask_made, table_loaded) = ph.sems(
            "sinks_loaded", "sinks_negated", "mask_made", "table_loaded")
        PE_SEMS = q_projected, z_projected, scored, turned, weighed, v_turned = ph.sems(
            "q_projected", "z_projected", "scored", "turned", "weighed", "v_turned")
        ACT_SEMS = w_rounded, swapped, q_rounded, z_tanh, exped, pt_rounded, v_copied, v_rounded = ph.sems(
            "w_rounded", "swapped", "q_rounded", "z_tanh", "exped", "pt_rounded", "v_copied", "v_rounded")
        (roped, roped_cos, q_split, gated, sink_set, maxed, inverted, normalised, pt_split,
         y_made, v_split) = DVE_SEMS = ph.sems(
            "roped", "roped_cos", "q_split", "gated", "sink_set", "maxed", "inverted",
            "normalised", "pt_split", "y_made", "v_split")
        POOL_SEMS = w_split, roped_sin = ph.sems("w_split", "roped_sin")
        waits_met_pe, waits_met_dve, waits_met_sp = ph.sems("waits_met_pe", "waits_met_dve", "waits_met_sp")
        block = ph.block()

        tile_of = lambda b: b // 3
        key0 = lambda b: start(max(b - 1, 0))
        keys = lambda b: start(b) + length(b) - key0(b)
        mask_at = lambda b: (P, P - META, 0)[min(b, 2)]

        def chunks(b):
            out = [] if b == 0 else [(0, length(b - 1), b - 1)]
            return out + [(keys(b) - length(b), length(b), b)]

        def before(n_blocks, b):
            return PRE + n_blocks + (b if b == 0 else b - 1)

        def read_count(i, t):
            return PRE + 17 * i + (15, 0, 3, 6, 9, 12)[t]

        def pt_parts(b, dst):
            ps = pt_ps[b % 2]
            if b >= 2:
                return [(0, 0, dst[:, :], ps[:, :], True)]
            view = lambda x, c, n: x[:n, 2 * P * c:2 * P * c + 2 * P].rearrange(
                "p (e t) -> p e t", e=2)[:, :, :length(b)]
            return [(0, 0, view(dst, c, n), view(ps, c, n), True) for c, (_, n, _) in enumerate(chunks(b))]

        def v_parts(t, dst):
            b0, b1 = TILES[t]
            ps = pt_ps[t % 2]
            out = []
            if b0 == 0:
                out.append((dst[:META, 0, :], ps[:META, :P]))
                b0 = 1
            o = (b0 - TILES[t][0]) * P
            out.append((dst[:, b0:b1, :], ps[:, o:o + (b1 - b0) * P].rearrange("p (b d) -> p b d", d=P)))
            return out

        @block.sync
        def _(sp):
            for y_slot in y_stored:
                sp.sem_inc(y_slot, 16)
            sp.dma_start(neg_sink[:, :], sinks.partition_broadcast(P)).then_inc(sinks_loaded, 16)

            def table(run, t):
                sp.wait_ge(roped, PRE + run)
                a, z = tile_cols(t)
                sp.dma_start(rope[:, :, :z - a], rope_table[:, :, a:z]).then_inc(table_loaded, 16)

            def load_pair(unit, i, c0):
                sp.wait_ge(w_split, PRE + 2 * unit)
                sp.sem_inc(waits_met_sp, 1)
                load_pair_weights(sp, raw, w_in, (A_HD * i + c0, A_HD * i + (c0 + A_HD * A_PAIRS)), raw_loaded)

            def store(i, b):
                sp.wait_ge(y_made, PRE + 17 * i + b + 1)
                sp.dma_start(y_t[bass.ds(P * i, P), start(b):start(b) + length(b)],
                             y[b % 2][:, :length(b)]).then_inc(y_stored[b % 2], 16)

            for half_loaded in raw_loaded:
                sp.sem_inc(half_loaded, 64)
            load_pair(2, 0, 0)
            for run in range(6):
                table(run, run)
            load_pair(3, 0, A_Z0)
            table(6, 0)
            with sp.Fori(0, A_PAIRS) as i:
                for s in range(19):
                    if s < 18:
                        run = 6 * i + s // 3 + 7
                        if s % 3 == 0:
                            table(run, (s // 3 + 1) % 6)
                        if s == 1:
                            load_pair(4 + 2 * i, (i + 1) % A_PAIRS, 0)
                        if s == 14:
                            load_pair(5 + 2 * i, (i + 1) % A_PAIRS, A_Z0)
                    if 0 <= s - 2 < NB:
                        store(i, s - 2)
            sp.wait_ge(y_stored[0], 16 * (1 + 9 * A_PAIRS))
            sp.wait_ge(y_stored[1], 16 * (1 + 8 * A_PAIRS))

        @block.gpsimd
        def _(pool):
            for sem in POOL_SEMS:
                pool.sem_inc(sem, PRE)
            pool.sem_inc(w_split, 2)
            pool.memset(mask[:, :], 0.0).then_inc(mask_made, 1)
            pool.wait_ge(mask_made, 1)
            pool.affine_select(out=mask[:, :P], in_=mask[:, :P], compare_op=ALU.is_gt, fill=MASKED, base=0,
                               pattern=[[1, P]], channel_multiplier=-1).then_inc(mask_made, 1)
            pool.affine_select(out=mask[:, P:], in_=mask[:, P:], compare_op=ALU.is_ge, fill=MASKED, base=0,
                               pattern=[[-1, P]], channel_multiplier=1).then_inc(mask_made, 1)

            def split(unit, name):
                for h in range(2):
                    pool.wait_ge(w_rounded, PRE + 2 * unit + h + 1)
                    ks = slice(4 * h, 4 * h + 4)
                    pool.tensor_tensor(w_l[name][:, ks, :], raw[h][:, :, :], w_h[name][:, ks, :].bitcast(F32),
                                       ALU.subtract).then_inc(w_split, 1)

            def rotate(run, t):
                w = tile_cols(t)[1] - tile_cols(t)[0]
                pool.wait_ge(swapped, PRE + run + 1)
                pool.wait_ge(table_loaded, 16 * (run + 1))
                pool.tensor_tensor(q_s[:, :w], q_s[:, :w], rope[:, 1, :w], ALU.mult).then_inc(roped_sin, 1)

            split(1, "z")
            for t in range(6):
                rotate(t, t)
            split(2, "q")
            split(3, "z")
            rotate(6, 0)
            with pool.Fori(0, A_PAIRS) as i:
                for t in range(1, 6):
                    rotate(6 * i + t + 6, t)
                split(4 + 2 * i, "q")
                split(5 + 2 * i, "z")
                rotate(6 * i + 12, 0)

        @block.scalar
        def _(act):
            for sem in ACT_SEMS:
                act.sem_inc(sem, PRE)
            act.sem_inc(w_rounded, 2)

            def round_w(unit, name):
                for h in range(2):
                    act.wait_ge(raw_loaded[h], 32 * (unit + 1))
                    act.activation(w_h[name][:, 4 * h:4 * h + 4, :], raw[h][:, :, :], ACT.Copy
                                   ).then_inc(w_rounded, 1)

            def swap(run, t):
                a, z = tile_cols(t)
                act.wait_ge(q_projected, PRE + run + 1)
                act.wait_ge(roped, PRE + run)
                for r in range(0, P, 64):
                    for x, z0 in ((0, 32), (32, 0)):
                        ins = act.activation(q_s[r + x:r + x + 32, :z - a], q_ps[r + z0:r + z0 + 32, :z - a],
                                             ACT.Copy)
                ins.then_inc(swapped, 1)

            def round_q(run, i, t):
                a, z = tile_cols(t)
                if i is not None:
                    act.wait_ge(scored, read_count(i, t))
                act.wait_ge(roped, PRE + run + 1)
                act.activation(q_h[t % 2][:, :z - a], q_f[:, :z - a], ACT.Copy).then_inc(q_rounded, 1)

            def tanh_z(i, t):
                a, z = tile_cols(t)
                act.wait_ge(z_projected, PRE + 6 * i + t + 7)
                act.wait_ge(y_made, PRE + 17 * i + (-2, 0, 3, 6, 9, 12)[t])
                act.activation(gate[t % 2][:, :z - a], z_ps[:, :z - a], ACT.Tanh, scale=0.5).then_inc(z_tanh, 1)

            def exponentials(i, b):
                m, r, n = length(b), b % 2, keys(b) + 1
                act.wait_ge(maxed, PRE + 17 * i + b + 1)
                for e in range(2):
                    ins = act.activation(prob[r][:m, e, :n], prob[r][:m, e, :n], ACT.Exp,
                                         bias=stat[r][:m, NEG.start + e:NEG.start + e + 1], scale=-1.0,
                                         accum_out=stat[r][:m, SUM.start + e:SUM.start + e + 1])
                ins.then_inc(exped, 1)

            def round_pt(i, b):
                act.wait_ge(turned, PRE + 17 * i + b + 1)
                act.wait_ge(weighed, PRE + 17 * i + b)
                for at, n, out, src, last in pt_parts(b, pt_h):
                    ins = act.activation(out, src, ACT.Copy)
                ins.then_inc(pt_rounded, 1)

            round_w(1, "z")
            for t in range(7):
                if t < 6:
                    swap(t, t)
                if t > 0:
                    act.wait_ge(v_turned, PRE + t)
                    for out, src in v_parts(t - 1, v_h):
                        ins = act.activation(out, src, ACT.Copy)
                    ins.then_inc(v_rounded, 1)
                if t < 6:
                    a, z = tile_cols(t)
                    act.wait_ge(roped, PRE + t + 1)
                    act.activation(k_h[:, a:z], q_f[:, :z - a], ACT.Copy).then_inc(q_rounded, 1)
                    if t == 5:
                        act.wait_ge(q_projected, PRE + 6)
                        round_w(2, "q")
                    act.wait_ge(z_projected, PRE + t + 1)
                    act.activation(gate[t % 2][:, :z - a], z_ps[:, :z - a], ACT.Copy).then_inc(v_copied, 1)
            round_w(3, "z")
            swap(6, 0)
            round_q(6, None, 0)
            with act.Fori(0, A_PAIRS) as i:
                for s in range(18):
                    t, run = (s // 3 + 1) % 6, 6 * i + s // 3 + 7
                    if s > 0:
                        round_pt(i, s - 1)
                    if s < NB:
                        exponentials(i, s)
                    if s % 3 == 0:
                        tanh_z(i, s // 3)
                    if s % 3 == 1:
                        swap(run, t)
                    if s % 3 == 2:
                        round_q(run, i, t)
                    if s == 13:
                        act.wait_ge(q_projected, PRE + 6 * i + 12)
                        round_w(4 + 2 * i, "q")
                    if s == 15:
                        act.wait_ge(z_projected, PRE + 6 * i + 12)
                        round_w(5 + 2 * i, "z")

        @block.vector
        def _(dve):
            for sem in DVE_SEMS:
                dve.sem_inc(sem, PRE)
            dve.wait_ge(sinks_loaded, 16)
            dve.tensor_scalar(neg_sink[:, :], neg_sink[:, :], -1.0, None, ALU.mult).then_inc(sinks_negated, 1)
            dve.wait_ge(sinks_negated, 1)
            dve.wait_ge(mask_made, 3)

            def rotate_cos(run, t):
                w = tile_cols(t)[1] - tile_cols(t)[0]
                dve.wait_ge(swapped, PRE + run + 1)
                dve.wait_ge(table_loaded, 16 * (run + 1))
                dve.wait_ge(q_split, PRE + run)
                dve.tensor_tensor(q_f[:, :w], q_ps[:, :w], rope[:, 0, :w], ALU.mult).then_inc(roped_cos, 1)

            def rotate_sum(run, t):
                w = tile_cols(t)[1] - tile_cols(t)[0]
                dve.wait_ge(roped_cos, PRE + run + 1)
                dve.wait_ge(roped_sin, PRE + run + 1)
                dve.tensor_tensor(q_f[:, :w], q_f[:, :w], q_s[:, :w], ALU.add).then_inc(roped, 1)

            def split_q(run, out_l, out_h, w):
                dve.wait_ge(q_rounded, PRE + run + 1)
                dve.tensor_tensor(out_l, q_f[:, :w], out_h.bitcast(F32), ALU.subtract).then_inc(q_split, 1)

            def split_query(run, t):
                w = tile_cols(t)[1] - tile_cols(t)[0]
                split_q(run, q_l[t % 2][:, :w], q_h[t % 2][:, :w], w)

            def make_gate(i, t):
                w = tile_cols(t)[1] - tile_cols(t)[0]
                dve.wait_ge(z_tanh, PRE + 6 * i + t + 1)
                dve.scalar_tensor_tensor(out=gate[t % 2][:, :w], in0=gate[t % 2][:, :w], scalar=1.0,
                                         in1=z_ps[:, :w], op0=ALU.add, op1=ALU.mult).then_inc(gated, 1)

            def soften(i, b):
                m, r, n, c = length(b), b % 2, keys(b), mask_at(b)
                if b == 0:
                    dve.wait_ge(maxed, PRE + 17 * i)
                    dve.tensor_copy(sink[:, :], neg_sink[:, :].rearrange("p (e i) -> p e i", e=2)[:, :, bass.ds(i, 1)].rearrange("p e i -> p (e i)")
                                    ).then_inc(sink_set, 1)
                    dve.wait_ge(sink_set, PRE + i + 1)
                dve.wait_ge(turned, before(17 * i, b))
                dve.tensor_copy(prob[r][:m, :, 0], sink[:m, :])
                dve.wait_ge(scored, PRE + 17 * i + b + 1)
                dve.sem_inc(waits_met_dve, 1)
                for e in range(2):
                    ins = dve.tensor_tensor_reduce(
                        prob[r][:m, e, 1:n + 1], s_ps[e][:m, :n], mask[:m, c:c + n],
                        -A_HD ** -0.5, sink[:m, e:e + 1], ALU.add, ALU.min,
                        stat[r][:m, NEG.start + e:NEG.start + e + 1])
                ins.then_inc(maxed, 1)

            def normalise(i, b):
                m, r, n = length(b), b % 2, keys(b)
                st = stat[r]
                dve.wait_ge(exped, PRE + 17 * i + b + 1)
                dve.reciprocal(st[:m, INV], st[:m, SUM]).then_inc(inverted, 1)
                dve.wait_ge(inverted, PRE + 17 * i + b + 1)
                for e in range(2):
                    ins = dve.tensor_scalar(prob[r][:m, e, 1:n + 1], prob[r][:m, e, 1:n + 1],
                                            st[:m, INV.start + e:INV.start + e + 1], None, ALU.mult)
                ins.then_inc(normalised, 1)

            def split_pt(i, b):
                dve.wait_ge(pt_rounded, PRE + 17 * i + b + 1)
                for (_, _, out, src, _), (_, _, high, _, _) in zip(pt_parts(b, pt_l), pt_parts(b, pt_h)):
                    ins = dve.tensor_tensor(out, src, high.bitcast(F32), ALU.subtract)
                ins.then_inc(pt_split, 1)

            def make_y(i, b):
                m, r, t = length(b), b % 2, tile_of(b)
                dve.wait_ge(weighed, PRE + 17 * i + b + 1)
                dve.wait_ge(gated, PRE + 6 * i + t + 1)
                dve.wait_ge(y_stored[r], 16 * (1 + (9 - r) * i + b // 2))
                c = start(b) - tile_cols(t)[0]
                for e in range(2):
                    rows = slice(A_HD * e, A_HD * e + A_HD)
                    ins = dve.scalar_tensor_tensor(out=y[r][rows, :m], in0=o_ps[r][rows, m * e:m * e + m],
                                                   scalar=0.5, in1=gate[t % 2][rows, c:c + m],
                                                   op0=ALU.mult, op1=ALU.mult)
                ins.then_inc(y_made, 1)

            for t in range(7):
                if t > 0:
                    dve.wait_ge(v_rounded, PRE + t)
                    for (out, src), (high, _) in zip(v_parts(t - 1, v_l), v_parts(t - 1, v_h)):
                        ins = dve.tensor_tensor(out, src, high.bitcast(F32), ALU.subtract)
                    ins.then_inc(v_split, 1)
                rotate_cos(t, t % 6)
                rotate_sum(t, t % 6)
                if t < 6:
                    a, z = tile_cols(t)
                    split_q(t, k_l[:, a:z], k_h[:, a:z], z - a)
            split_query(6, 0)
            with dve.Fori(0, A_PAIRS) as i:
                for s in range(19):
                    t, run = (s // 3 + 1) % 6, 6 * i + s // 3 + 7
                    if 0 <= s - 2 < NB:
                        make_y(i, s - 2)
                    if s < NB:
                        soften(i, s)
                    if s % 3 == 2:
                        rotate_sum(run, t)
                    if 0 <= s - 1 < NB:
                        split_pt(i, s - 1)
                    if s % 3 == 2:
                        split_query(run, t)
                    if s < NB:
                        normalise(i, s)
                    if s % 3 == 0 and s < 18:
                        make_gate(i, s // 3)
                    if s % 3 == 1:
                        rotate_cos(run, t)

        @block.tensor
        def _(pe):
            for sem in PE_SEMS:
                pe.sem_inc(sem, PRE)

            def project(ps, name, t, ks):
                a, z = tile_cols(t)
                for k in ks:
                    last = product(pe, ps[:, :z - a], w_h[name][:, k, :], w_l[name][:, k, :],
                                   u_h[:, k, a:z], u_l[:, k, a:z], k == 0, k == KT - 1)
                return last

            def project_part(i, m, t, part):
                name, ks = "qz"[part // 3], (range(0, 3), range(3, 6), range(6, 8))[part % 3]
                if part == 0:
                    pe.wait_ge(roped_cos, PRE + m + 6)
                    if t == 0:
                        pe.wait_ge(w_split, PRE + 2 * (2 * i + 4) + 2)
                if part == 3:
                    pe.wait_ge(gated, PRE + m)
                    if t == 0:
                        pe.wait_ge(w_split, PRE + 2 * (2 * i + 5) + 2)
                last = project(q_ps if name == "q" else z_ps, name, t, ks)
                if part == 2:
                    last.then_inc(q_projected, 1)
                if part == 5:
                    last.then_inc(z_projected, 1)

            def scores(i, b):
                m, r, n, t = length(b), b % 2, keys(b), tile_of(b)
                c = start(b) - tile_cols(t)[0]
                if b == TILES[t][0]:
                    pe.wait_ge(q_split, PRE + 6 * i + t + 7)
                pe.wait_ge(maxed, PRE + 17 * i + b)
                if b == 0:
                    pe.sem_inc(waits_met_pe, 1)
                for e in range(2):
                    rows = slice(A_HD * e, A_HD * e + A_HD)
                    last = product(pe, s_ps[e][:m, :n],
                                   q_h[t % 2][rows, c:c + m], q_l[t % 2][rows, c:c + m],
                                   k_h[rows, key0(b):key0(b) + n], k_l[rows, key0(b):key0(b) + n], True, True)
                last.then_inc(scored, 1)

            def turn(i, b):
                m, r = length(b), b % 2
                pe.wait_ge(normalised, PRE + 17 * i + b + 1)
                pe.wait_ge(pt_split, before(17 * i, b))
                if b == 0:
                    pe.sem_inc(waits_met_pe, 1)
                for c, (at, n, _) in enumerate(chunks(b)):
                    for e in range(2):
                        last = pe.transpose(pt_ps[r][:n, 2 * P * c + P * e:2 * P * c + P * e + m],
                                            prob[r][:m, e, 1 + at:1 + at + n], ident[:m, :m])
                last.then_inc(turned, 1)

            def weigh(i, b):
                m, r = length(b), b % 2
                pe.wait_ge(pt_split, PRE + 17 * i + b + 1)
                pe.wait_ge(y_made, before(17 * i, b))
                parts = chunks(b)
                view = lambda x, c, n: x[:n, 2 * P * c:2 * P * c + 2 * P].rearrange(
                    "p (e t) -> p e t", e=2)[:, :, :m]
                out = o_ps[r][:, :2 * m].rearrange("p (e t) -> p e t", e=2)
                for c, (_, n, kb) in enumerate(parts):
                    first, final = c == 0, c == len(parts) - 1
                    pe.matmul(out, v_h[:n, kb, :], view(pt_h, c, n), start=first, stop=False)
                    pe.matmul(out, v_l[:n, kb, :], view(pt_h, c, n), start=False, stop=False)
                    last = pe.matmul(out, v_h[:n, kb, :], view(pt_l, c, n), start=False, stop=final)
                last.then_inc(weighed, 1)

            for t in range(7):
                if t < 6:
                    pe.wait_ge(roped_cos, PRE + t)
                    project(q_ps, "q", t, range(KT)).then_inc(q_projected, 1)
                if t > 0:
                    pe.wait_ge(v_copied, PRE + t)
                    if t >= 3:
                        pe.wait_ge(v_split, PRE + t - 2)
                    b0, b1 = TILES[t - 1]
                    for b in range(b0, b1):
                        c = start(b) - start(b0)
                        o = (b - b0) * P
                        last = pe.transpose(pt_ps[(t - 1) % 2][:length(b), o:o + P],
                                            gate[(t - 1) % 2][:, c:c + length(b)], ident[:, :])
                    last.then_inc(v_turned, 1)
                if t < 6:
                    if t == 0:
                        pe.wait_ge(w_split, PRE + 4)
                    pe.wait_ge(v_copied, PRE + t)
                    project(z_ps, "z", t, range(KT)).then_inc(z_projected, 1)
            pe.wait_ge(roped_cos, PRE + 6)
            pe.wait_ge(w_split, PRE + 6)
            project(q_ps, "q", 0, range(KT)).then_inc(q_projected, 1)
            pe.wait_ge(v_copied, PRE + 6)
            pe.wait_ge(w_split, PRE + 8)
            project(z_ps, "z", 0, range(KT)).then_inc(z_projected, 1)
            pe.wait_ge(v_split, PRE + 6)
            with pe.Fori(0, A_PAIRS) as i:
                for s in range(18):
                    m, t = 6 * i + s // 3 + 1, (s // 3 + 1) % 6
                    if s < NB:
                        scores(i, s)
                    if s > 0:
                        turn(i, s - 1)
                    project_part(i, m, t, 2 * (s % 3))
                    project_part(i, m, t, 2 * (s % 3) + 1)
                    if s > 0:
                        weigh(i, s - 1)


def project_out(nc, name, w_out, y_src, residual, norm_g, ident, h_store, u_f=None):
    first_layer = u_f is not None
    n_blocks = NB if first_layer else NB - 1
    peeled = 5 if first_layer else 4
    mm_lag = 0 if first_layer else 1
    lag = mm_lag + 1

    prepared = 3 if first_layer else 2

    def over(eng, step, lags):
        for n in range(peeled):
            step(n, n % 2)
        with eng.Fori(0, (n_blocks - peeled) // 2) as i:
            step(peeled + 2 * i, peeled % 2)
            step(peeled + 1 + 2 * i, 1 - peeled % 2)
        for n in range(n_blocks, n_blocks + lags):
            step(n, n % 2)

    def exists(n, lag=0):
        return not isinstance(n, int) or 0 <= n - lag < n_blocks

    def rows_of(n):
        return cols(n) if first_layer else bass.ds(P * n + META, P)

    def size_of(n):
        return size(n) if first_layer else P

    def used(n, ring=2):
        return not isinstance(n, int) or n >= ring

    with ExitStack() as stack:
        ph = Phase(nc, stack, name)
        w_h, w_l = ph.sb("w_h", [P, KT, D], F32R), ph.sb("w_l", [P, KT, D], F32R)
        raw = [ph.sb(f"raw{k}", [P, D]) for k in range(4)]
        gain, squares = ph.sb("gain", [P, D]), ph.sb("squares", [P, D])
        y_in = [ph.sb(f"y{p}", [P, D]) for p in range(2)]
        y_h = [ph.sb(f"y_h{p}", [P, KT, P], F32R) for p in range(2)]
        y_l = [ph.sb(f"y_l{p}", [P, KT, P], F32R) for p in range(2)]
        res = [ph.sb(f"res{p}", [P, D]) for p in range(2)]
        h = [ph.sb(f"h{p}", [P, D]) for p in range(2)]
        xs = [ph.sb(f"xs{p}", [P, D]) for p in range(2)]
        stat = [ph.sb(f"stat{p}", [P, 3]) for p in range(2)]
        eps = ph.sb("eps", [P, 1])
        acc = [[ph.ps(f"acc{p}{c}") for c in range(2)] for p in range(2)]
        turned_ps = [[ph.ps(f"turned{p}{c}") for c in range(2)] for p in range(2)]
        y_loaded = ph.sems("y_loaded0", "y_loaded1")
        res_loaded = ph.sems("res_loaded0", "res_loaded1")
        h_stored = ph.sems("h_stored0", "h_stored1")
        raw_loaded = ph.sems(*(f"raw_loaded{k}" for k in range(4)))
        (gain_loaded, eps_made, w_rounded, w_split_pool, w_split_dve, y_rounded, y_split, multiplied, h_made, summed,
         rooted, inverted, scaled, turned, copied_act, copied_dve) = ph.sems(
            "gain_loaded", "eps_made", "w_rounded", "w_split_pool", "w_split_dve", "y_rounded", "y_split",
            "multiplied", "h_made", "summed", "rooted", "inverted", "scaled", "turned", "copied_act", "copied_dve")
        POOL_KS, DVE_KS = (2, 5), (0, 1, 3, 4, 6, 7)
        block = ph.block()
        loads = lambda n, p: 8 * n + (8 if p else 16)

        @block.sync
        def _(sp):
            def load_w(k):
                if k >= 4:
                    sp.wait_ge(w_split_pool, sum(j <= k - 4 for j in POOL_KS)) if k - 4 in POOL_KS else \
                        sp.wait_ge(w_split_dve, sum(j <= k - 4 for j in DVE_KS))
                for e in range(2):
                    half = slice(P // 2 * e, P // 2 * e + P // 2)
                    at = D // 2 * e + P // 2 * k if first_layer else P * k + P // 2 * e
                    sp.dma_start(raw[k % 4][half, :], w_out[at:at + P // 2, :]).then_inc(raw_loaded[k % 4], 16)

            def load_y(n, p):
                if used(n):
                    sp.wait_ge(y_split, n - 1)
                if first_layer:
                    sp.dma_start(y_in[p][:, :].rearrange("p (k t) -> p k t", k=KT)[:, :, :size_of(n)],
                                 y_src[:, cols(n)].rearrange("(k p) t -> p k t", p=P)).then_inc(y_loaded[p], 16)
                else:
                    sp.dma_start(y_in[p][:, :], y_src[rows_of(n), :]).then_inc(y_loaded[p], 16)

            def load_res(n, p):
                if used(n):
                    sp.wait_ge(h_made, 2 * (n - 1))
                sp.dma_start(res[p][:size_of(n), :], residual(n)).then_inc(res_loaded[p], 16)

            def step(n, p):
                if exists(n) and not (isinstance(n, int) and n < 2):
                    load_y(n, p)
                if exists(n, 1) and not (isinstance(n, int) and n < 3):
                    load_res(n - 1, 1 - p)

            load_y(0, 0)
            load_w(0)
            load_y(1, 1)
            for k in range(1, KT):
                load_w(k)
            for n in range(2):
                load_res(n, n)
            sp.dma_start(gain[:, :], norm_g.partition_broadcast(P)).then_inc(gain_loaded, 16)
            over(sp, step, 1)

        @block.gpsimd
        def _(pool):
            pool.memset(eps[:, :], EPS).then_inc(eps_made, 1)
            for k in POOL_KS:
                pool.wait_ge(w_rounded, k + 1)
                pool.tensor_tensor(w_l[:, k, :], raw[k % 4][:, :], w_h[:, k, :].bitcast(F32),
                                   ALU.subtract).then_inc(w_split_pool, 1)

            def step(n, p):
                if exists(n, lag):
                    b, q = n - lag, (p + lag) % 2
                    m = size_of(b)
                    if first_layer:
                        pool.wait_ge(h_made, 2 * (b + 1))
                        pool.dma_start(h_store[rows_of(b), :], h[q][:m, :]).then_inc(h_stored[q], 16)
                    else:
                        pool.wait_ge(scaled, b + 1)
                        pool.dma_start(h_store[bass.ds(P * b, P), :], xs[q][:, :]).then_inc(h_stored[q], 16)
            over(pool, step, 2)
            for p in range(2):
                pool.wait_ge(h_stored[p], 16 * ((n_blocks + 1 - p) // 2))

        @block.scalar
        def _(act):
            def round_y(n, p):
                m = size_of(n)
                if used(n):
                    act.wait_ge(multiplied, n - 1)
                if first_layer:
                    act.wait_ge(y_loaded[p], loads(n, p))
                    act.activation(y_h[p][:, :, :m],
                                   y_in[p][:, :].rearrange("p (k t) -> p k t", k=KT)[:, :, :m],
                                   ACT.Copy).then_inc(y_rounded, 1)
                else:
                    act.wait_ge(turned, n + 1)
                    for c in range(2):
                        ins = act.activation(y_h[p][:, 4 * c:4 * c + 4, :],
                                             turned_ps[p][c][:, :].rearrange("p (k t) -> p k t", k=4), ACT.Copy)
                    ins.then_inc(y_rounded, 1)

            round_y(0, 0)
            for k in range(KT):
                if k == 1:
                    round_y(1, 1)
                act.wait_ge(raw_loaded[k % 4], 32 * (k // 4 + 1))
                act.activation(w_h[:, k, :], raw[k % 4][:, :], ACT.Copy).then_inc(w_rounded, 1)
            act.wait_ge(eps_made, 1)

            def step(n, p):
                if exists(n) and not (isinstance(n, int) and n < prepared):
                    round_y(n, p)
                if first_layer and isinstance(n, int) and n == 1:
                    round_y(2, 0)
                if exists(n, lag):
                    b, q = n - lag, (p + lag) % 2
                    m = size_of(b)
                    act.wait_ge(h_made, 2 * (b + 1))
                    if used(n, lag + 1):
                        act.wait_ge(rooted, b)
                    if used(n, lag + 2):
                        act.wait_ge(inverted, b - 1)
                    act.activation(squares[:m, :], h[q][:m, :], ACT.Square,
                                   accum_out=stat[q][:m, 0:1]).then_inc(summed, 1)
                    act.wait_ge(summed, b + 1)
                    act.activation(stat[q][:m, 1:2], stat[q][:m, 0:1], ACT.Sqrt, bias=eps[:m, :],
                                   scale=1.0 / D).then_inc(rooted, 1)
                if first_layer and exists(n, 2):
                    b = n - 2
                    m = size_of(b)
                    act.wait_ge(turned, b + 1)
                    act.activation(u_f[:, :4, cols(b)],
                                   turned_ps[p][0][:, :].rearrange("p (k t) -> p k t", k=4)[:, :, :m],
                                   ACT.Copy).then_inc(copied_act, 1)
            over(act, step, 2)

        @block.vector
        def _(dve):
            def split_y(n, p):
                m = size_of(n)
                dve.wait_ge(y_rounded, n + 1)
                if first_layer:
                    dve.tensor_tensor(y_l[p][:, :, :m],
                                      y_in[p][:, :].rearrange("p (k t) -> p k t", k=KT)[:, :, :m],
                                      y_h[p][:, :, :m].bitcast(F32), ALU.subtract).then_inc(y_split, 1)
                else:
                    for c in range(2):
                        ks = slice(4 * c, 4 * c + 4)
                        ins = dve.tensor_tensor(y_l[p][:, ks, :],
                                                turned_ps[p][c][:, :].rearrange("p (k t) -> p k t", k=4),
                                                y_h[p][:, ks, :].bitcast(F32), ALU.subtract)
                    ins.then_inc(y_split, 1)

            split_y(0, 0)
            for k in DVE_KS:
                if k == 1:
                    split_y(1, 1)
                dve.wait_ge(w_rounded, k + 1)
                dve.tensor_tensor(w_l[:, k, :], raw[k % 4][:, :], w_h[:, k, :].bitcast(F32),
                                  ALU.subtract).then_inc(w_split_dve, 1)
            dve.wait_ge(gain_loaded, 16)

            def step(n, p):
                if exists(n) and not (isinstance(n, int) and n < prepared):
                    split_y(n, p)
                if exists(n, lag):
                    b, q = n - lag, (p + lag) % 2
                    m = size_of(b)
                    dve.wait_ge(multiplied, b + 1)
                    dve.wait_ge(res_loaded[q], loads(b, q))
                    if used(n, lag + 2):
                        dve.wait_ge(summed, b - 1)
                        if first_layer:
                            dve.wait_ge(h_stored[q], loads(b - 2, q))
                    for c in range(2):
                        dve.tensor_tensor(h[q][:m, 512 * c:512 * c + 512], acc[q][c][:m, :],
                                          res[q][:m, 512 * c:512 * c + 512], ALU.add).then_inc(h_made, 1)
                    if first_layer and isinstance(n, int) and n == 1:
                        split_y(2, 0)
                    dve.wait_ge(rooted, b + 1)
                    dve.reciprocal(stat[q][:m, 2:3], stat[q][:m, 1:2]).then_inc(inverted, 1)
                    dve.wait_ge(inverted, b + 1)
                    if used(n, lag + 2):
                        if first_layer:
                            dve.wait_ge(turned, b - 1)
                        else:
                            dve.wait_ge(h_stored[q], loads(b - 2, q))
                    dve.scalar_tensor_tensor(out=xs[q][:m, :], in0=h[q][:m, :], scalar=stat[q][:m, 2:3],
                                             in1=gain[:m, :], op0=ALU.mult, op1=ALU.mult).then_inc(scaled, 1)
                if first_layer and exists(n, 2):
                    b = n - 2
                    m = size_of(b)
                    dve.wait_ge(turned, b + 1)
                    dve.tensor_copy(u_f[:, 4:, cols(b)],
                                    turned_ps[p][1][:, :].rearrange("p (k t) -> p k t", k=4)[:, :, :m]
                                    ).then_inc(copied_dve, 1)
            over(dve, step, 2)

        @block.tensor
        def _(pe):
            def turn(src, b, q, m):
                for k in range(KT):
                    last = pe.transpose(turned_ps[q][k // 4][:, (k % 4) * P:(k % 4) * P + m],
                                        src[q][:m, k * P:(k + 1) * P], ident[:m, :m])
                last.then_inc(turned, 1)

            def turn_norm(b, q):
                pe.wait_ge(scaled, b + 1)
                if used(b, 2):
                    pe.wait_ge(copied_act, b - 1)
                    pe.wait_ge(copied_dve, b - 1)
                turn(xs, b, q, size_of(b))

            def turn_y(n, p):
                pe.wait_ge(y_loaded[p], loads(n, p))
                if used(n):
                    pe.wait_ge(y_split, n - 1)
                turn(y_in, n, p, P)

            def multiply(q, m, k):
                for c in range(2):
                    last = product(pe, acc[q][c][:m, :], y_h[q][:, k, :m], y_l[q][:, k, :m],
                                   w_h[:, k, 512 * c:512 * c + 512], w_l[:, k, 512 * c:512 * c + 512],
                                   k == 0, k == KT - 1)
                return last

            if not first_layer:
                for n in range(2):
                    turn_y(n, n)
            for k in range(KT):
                names = (w_split_pool, POOL_KS) if k in POOL_KS else (w_split_dve, DVE_KS)
                pe.wait_ge(names[0], sum(j <= k for j in names[1]))
                for n in range(2):
                    if k == 0:
                        pe.wait_ge(y_split, n + 1)
                    last = multiply(n, size_of(n), k)
                    if k == KT - 1:
                        last.then_inc(multiplied, 1)

            def step(n, p):
                if not first_layer and exists(n) and not (isinstance(n, int) and n < 2):
                    turn_y(n, p)
                b, q = n - mm_lag, (p + mm_lag) % 2
                if exists(n, mm_lag) and not (isinstance(b, int) and b < 2):
                    pe.wait_ge(y_split, b + 1)
                    pe.wait_ge(h_made, 2 * (b - 1))
                    for k in range(KT):
                        last = multiply(q, size_of(b), k)
                    last.then_inc(multiplied, 1)
                if first_layer and isinstance(n, int) and n == 2:
                    turn_norm(0, 0)
                if first_layer and exists(n, 1) and not (isinstance(n, int) and n < 2):
                    turn_norm(n - 1, 1 - p)
            over(pe, step, 1)

def head_weights(nc, stack):
    new = lambda name, *kind: stack.enter_context(nc.sbuf_tensor(name, *kind))
    return (new("w_raw_qk", [P, KT, P], F32), new("w_raw_v", [P, KT, 3 * P], F32),
            new("wqk_h", [P, KT, P], F32R), new("wqk_l", [P, KT, P], F32R))


def load_qk_weights(sp, raw_qk, w_in, head, loaded):
    src = w_in.rearrange("(k p) n -> p k n", p=P)
    for j, at in enumerate((0, B_K0)):
        sp.dma_start(raw_qk[:, :, B_QK * j:B_QK * j + B_QK],
                     src[:, :, bass.ds(head * B_QK + at, B_QK)]).then_inc(loaded, 16)


def load_v_weights(sp, raw_v, w_in, head, loaded):
    src = w_in.rearrange("(k p) n -> p k n", p=P)
    for j, at in enumerate((B_V0, B_O0, B_Z0)):
        sp.dma_start(raw_v[:, :, P * j:P * j + P], src[:, :, bass.ds(head * P + at, P)]).then_inc(loaded, 16)


GATE_I, GATE_F = 0, 32


def gates(nc, u_f, w_in, b_gates, ident, u_h, u_l, head_cols, row_a, row_dec, weights):
    raw_qk, raw_v, wqk_h, wqk_l = weights
    H = B_HEADS
    PARTS = ((0, 4), (4, 6))
    PER_BANK = 5
    with ExitStack() as stack:
        ph = Phase(nc, stack, "g")
        w_raw = ph.sb("w_raw", [P, KT, 64])
        w_h, w_l = ph.sb("w_h", [P, KT, 64], F32R), ph.sb("w_l", [P, KT, 64], F32R)
        bias = ph.sb("bias", [64, 1])
        one = ph.sb("one", [H, 1])
        rows = ph.sb("rows", [P, T])
        log_i, log_f = ph.sb("log_i", [H, T]), ph.sb("log_f", [H, T])
        keep, scratch = ph.sb("keep", [H, T]), ph.sb("scratch", [H, T])
        m_prev, dec = ph.sb("m_prev", [H, NB]), ph.sb("dec", [H, NB])
        g_ps = [ph.ps(f"g_ps{r}") for r in range(2)]
        c_ps = [ph.ps(f"c_ps{r}") for r in range(4)]
        (w_cleared, w_loaded, w_rounded, w_split, cleared, u_rounded, u_split, projected, biased, turned, stored,
         filled) = ph.sems(
            "w_cleared", "w_loaded", "w_rounded", "w_split", "cleared", "u_rounded", "u_split", "projected",
            "biased", "turned", "stored", "filled")
        qk_loaded, v_loaded, qk_rounded, qk_split = ph.sems("qk_loaded", "v_loaded", "qk_rounded", "qk_split")
        (folded, exped, logged, log_f_made, b_summed, m_made, i_b_made, m_copied, m_prev_made, a_made, dec_summed,
         dec_made, rows_made) = ph.sems(
            "folded", "exped", "logged", "log_f_made", "b_summed", "m_made", "i_b_made", "m_copied",
            "m_prev_made", "a_made", "dec_summed", "dec_made", "rows_made")
        block = ph.block()

        def span(part):
            t0, t1 = PARTS[part]
            return slice(tile_cols(t0)[0], tile_cols(t1 - 1)[1]), TILES[t0][0], TILES[t1 - 1][1]

        @block.sync
        def _(sp):
            sp.wait_ge(w_cleared, 1)
            src = w_in.rearrange("(k p) n -> p k n", p=P)
            sp.dma_start(w_raw[:, :, GATE_I:GATE_I + H], src[:, :, B_G0:B_G0 + H]).then_inc(w_loaded, 16)
            sp.dma_start(w_raw[:, :, GATE_F:GATE_F + H], src[:, :, B_G0 + H:B_G0 + 2 * H]).then_inc(w_loaded, 16)
            bias_src = b_gates.rearrange("(n a) -> n a", a=1)
            sp.dma_start(bias[GATE_I:GATE_I + H, :], bias_src[:H, :]).then_inc(w_loaded, 16)
            sp.dma_start(bias[GATE_F:GATE_F + H, :], bias_src[H:, :]).then_inc(w_loaded, 16)
            load_qk_weights(sp, raw_qk, w_in, 0, qk_loaded)
            load_v_weights(sp, raw_v, w_in, 0, v_loaded)
            for part in range(2):
                c = span(part)[0]
                sp.wait_ge(a_made, part + 1)
                sp.dma_start(row_a.rearrange("(h t) -> h t", h=H)[:, c], log_i[:, c]).then_inc(stored, 16)
            sp.wait_ge(dec_made, 2)
            sp.dma_start(row_dec.rearrange("(h b) -> h b", h=H), dec[:, :]).then_inc(stored, 16)
            sp.wait_ge(stored, 48)
            sp.wait_ge(v_loaded, 48)

        @block.gpsimd
        def _(pool):
            pool.memset(w_raw[:, :, :], 0.0).then_inc(w_cleared, 1)
            pool.memset(rows[:, :], 0.0).then_inc(cleared, 1)
            pool.memset(keep[:, :], 1.0).then_inc(cleared, 1)
            pool.memset(one[:, :], 1.0)
            pool.wait_ge(cleared, 2)
            pool.memset(keep[:, 0:1], 0.0)
            pool.memset(keep[:, META:T:P], 0.0).then_inc(cleared, 1)
            pool.wait_ge(w_rounded, 1)
            pool.tensor_tensor(w_l[:, :, :], w_raw[:, :, :], w_h[:, :, :].bitcast(F32),
                               ALU.subtract).then_inc(w_split, 1)
            pool.wait_ge(qk_rounded, 1)
            pool.tensor_tensor(wqk_l[:, :, :], raw_qk[:, :, :], wqk_h[:, :, :].bitcast(F32),
                               ALU.subtract).then_inc(qk_split, 1)
            pool.wait_ge(qk_split, 1)

        @block.scalar
        def _(act):
            for t in range(6):
                a, z = tile_cols(t)
                act.activation(u_h[:, :, a:z], u_f[:, :, a:z], ACT.Copy).then_inc(u_rounded, 1)
                if t == 0:
                    act.wait_ge(w_loaded, 64)
                    act.activation(w_h[:, :, :], w_raw[:, :, :], ACT.Copy).then_inc(w_rounded, 1)
            act.wait_ge(qk_loaded, 32)
            act.activation(wqk_h[:, :, :], raw_qk[:, :, :], ACT.Copy).then_inc(qk_rounded, 1)
            act.wait_ge(cleared, 3)
            for part in range(2):
                c = span(part)[0]
                act.wait_ge(folded, part + 1)
                act.activation(scratch[:, c], scratch[:, c], ACT.Exp).then_inc(exped, 1)
                act.wait_ge(exped, part + 1)
                act.activation(scratch[:, c], scratch[:, c], ACT.Ln, bias=one[:, :]).then_inc(logged, 1)
                act.wait_ge(m_made, part + 1)
                act.wait_ge(b_summed, part + 1)
                act.activation(log_f[:, c], rows[64:64 + H, c], ACT.Copy).then_inc(m_copied, 1)
            act.wait_ge(dec_summed, 2)
            act.activation(dec[:, :], dec[:, :], ACT.Exp).then_inc(dec_made, 2)
            for c in range(4):
                n = min(PER_BANK, NB - PER_BANK * c)
                act.wait_ge(turned, c + 1)
                act.wait_ge(filled, c + 1)
                src = c_ps[c][:, :96 * n].rearrange("p (b q) -> p b q", q=96)
                bs = slice(PER_BANK * c, PER_BANK * c + n)
                act.activation(head_cols[:, 1, bs, :], src[:, :, 32:32 + H], ACT.Exp)
                act.activation(head_cols[:, 2, bs, :], src[:, :, 64:64 + H], ACT.Exp, scale=-1.0)

        @block.vector
        def _(dve):
            def add_bias(t):
                a, z = tile_cols(t)
                ps = g_ps[t % 2]
                dve.wait_ge(projected, t + 1)
                dve.tensor_scalar(log_i[:, a:z], ps[GATE_I:GATE_I + H, :z - a],
                                  bias[GATE_I:GATE_I + H, :], None, ALU.add)
                dve.tensor_scalar(log_f[:, a:z], ps[GATE_F:GATE_F + H, :z - a],
                                  bias[GATE_F:GATE_F + H, :], None, ALU.add).then_inc(biased, 1)

            def fold(part):
                c = span(part)[0]
                dve.wait_ge(biased, PARTS[part][1])
                dve.scalar_tensor_tensor(out=scratch[:, c], in0=log_f[:, c], scalar=-1.0, in1=log_f[:, c],
                                         op0=ALU.mult, op1=ALU.min).then_inc(folded, 1)

            def tables(part):
                c, b0, b1 = span(part)
                dve.wait_ge(logged, part + 1)
                dve.scalar_tensor_tensor(out=log_f[:, c], in0=log_f[:, c], scalar=0.0, in1=scratch[:, c],
                                         op0=ALU.min, op1=ALU.subtract).then_inc(log_f_made, 1)
                dve.wait_ge(log_f_made, part + 1)
                dve.wait_ge(cleared, 3)
                before = rows[64:64 + H, c.start - 1:c.start] if part else 0.0
                dve.tensor_tensor_scan(rows[64:64 + H, c], log_f[:, c], log_i[:, c], before, ALU.add,
                                       ALU.max).then_inc(m_made, 1)
                dve.tensor_tensor_scan(scratch[:, c], keep[:, c], log_f[:, c], 0.0, ALU.mult, ALU.add
                                       ).then_inc(b_summed, 1)
                dve.wait_ge(m_made, part + 1)
                if part == 0:
                    dve.memset(m_prev[:, 0:1], 0.0)
                first = max(b0, 1)
                dve.tensor_copy(m_prev[:, first:b1], rows[64:64 + H, start(first) - 1:start(b1 - 1):P]
                                ).then_inc(m_prev_made, 1)
                dve.wait_ge(b_summed, part + 1)
                dve.tensor_tensor(rows[0:H, c], log_i[:, c], scratch[:, c], ALU.subtract).then_inc(i_b_made, 1)
                dve.wait_ge(m_copied, part + 1)
                dve.wait_ge(i_b_made, part + 1)
                dve.tensor_tensor(log_i[:, c], scratch[:, c], log_f[:, c], ALU.subtract).then_inc(a_made, 1)
                dve.wait_ge(a_made, part + 1)
                dve.wait_ge(m_prev_made, part + 1)
                if part == 0:
                    dve.tensor_tensor(dec[:, 0:1], log_i[:, META - 1:META], m_prev[:, 0:1], ALU.add)
                last = start(first) + P - 1
                dve.tensor_tensor(dec[:, first:b1], log_i[:, last:c.stop:P], m_prev[:, first:b1], ALU.add
                                  ).then_inc(dec_summed, 1)
                for b in range(b0, b1):
                    own = slice(start(b), start(b) + length(b))
                    ins = dve.tensor_scalar(rows[32:32 + H, own], log_i[:, own], m_prev[:, b:b + 1], None, ALU.add)
                ins.then_inc(rows_made, 1)

            for t in range(6):
                a, z = tile_cols(t)
                dve.wait_ge(u_rounded, t + 1)
                dve.tensor_tensor(u_l[:, :, a:z], u_f[:, :, a:z], u_h[:, :, a:z].bitcast(F32),
                                  ALU.subtract).then_inc(u_split, 1)
                if t >= 1:
                    if t == 1:
                        dve.wait_ge(w_loaded, 64)
                    add_bias(t - 1)
                if t == 4:
                    fold(0)
            tables(0)
            add_bias(5)
            fold(1)
            tables(1)
            for c in range(4):
                n = min(PER_BANK, NB - PER_BANK * c)
                dve.wait_ge(turned, c + 1)
                bs = slice(PER_BANK * c, PER_BANK * c + n)
                dve.tensor_copy(head_cols[:, 0, bs, :],
                                c_ps[c][:, :96 * n].rearrange("p (b q) -> p b q", q=96)[:, :, :H]).then_inc(filled, 1)

        @block.tensor
        def _(pe):
            for t in range(6):
                a, z = tile_cols(t)
                pe.wait_ge(u_split, t + 1)
                if t == 0:
                    pe.wait_ge(w_split, 1)
                if t >= 2:
                    pe.wait_ge(biased, t - 1)
                for k in range(KT):
                    last = product(pe, g_ps[t % 2][:64, :z - a], w_h[:, k, :], w_l[:, k, :],
                                   u_h[:, k, a:z], u_l[:, k, a:z], k == 0, k == KT - 1)
                last.then_inc(projected, 1)
            for b in range(NB):
                if b in (0, span(1)[1]):
                    pe.wait_ge(rows_made, 1 if b == 0 else 2)
                    pe.wait_ge(i_b_made, 1 if b == 0 else 2)
                c = start(b)
                o = 96 * (b % PER_BANK)
                last = pe.transpose(c_ps[b // PER_BANK][:, o:o + 96], rows[:96, c:c + P], ident[:96, :96])
                if b % PER_BANK == PER_BANK - 1 or b == NB - 1:
                    last.then_inc(turned, 1)


def mlstm(nc, w_in, ident, u_h, u_l, head_cols, row_a, row_dec, y_out, weights):
    raw_qk, raw_v, wqk_h, wqk_l = weights
    VW = B_V + 2
    with ExitStack() as stack:
        ph = Phase(nc, stack, "m")
        wv_h, wv_l = ph.sb("wv_h", [P, KT, 3 * P], F32R), ph.sb("wv_l", [P, KT, 3 * P], F32R)
        row = [ph.sb(f"row{r}", [P, TW]) for r in range(2)]
        decay = ph.sb("decay", [B_QK, NB])
        col = ph.sb("col", [P, 3, NB])
        q_h = [ph.sb(f"q_h{r}", [B_QK, TW], F32R) for r in range(2)]
        q_l = [ph.sb(f"q_l{r}", [B_QK, TW], F32R) for r in range(2)]
        k_both = ph.sb("k_both", [P, TW])
        k_f = [k_both[:B_QK, :], k_both[B_QK:, :]]
        ident_of = [ident[:B_QK, :B_QK], ident[B_QK:, B_QK:]]
        k_h = [ph.sb(f"k_h{r}", [B_QK, TW], F32R) for r in range(2)]
        k_l = [ph.sb(f"k_l{r}", [B_QK, TW], F32R) for r in range(2)]
        v_h = [ph.sb(f"v_h{r}", [P, VW], F32R) for r in range(2)]
        v_l = [ph.sb(f"v_l{r}", [P, VW], F32R) for r in range(2)]
        gate = [ph.sb(f"gate{r}", [P, P]) for r in range(2)]
        weight = ph.sb("weight", [P, P])
        score = ph.sb("score", [P, P])
        s_h = [ph.sb(f"s_h{r}", [P, P], F32R) for r in range(2)]
        s_l = [ph.sb(f"s_l{r}", [P, P], F32R) for r in range(2)]
        k_w = ph.sb("k_w", [P, B_QK])
        kw_h = [ph.sb(f"kw_h{r}", [P, B_QK], F32R) for r in range(2)]
        kw_l = [ph.sb(f"kw_l{r}", [P, B_QK], F32R) for r in range(2)]
        state = ph.sb("state", [B_QK, VW])
        state_h, state_l = ph.sb("state_h", [B_QK, VW], F32R), ph.sb("state_l", [B_QK, VW], F32R)
        mix = ph.sb("mix", [P, VW])
        den = ph.sb("den", [P, 3])
        y = [ph.sb(f"y{r}", [P, P]) for r in range(2)]
        bound = ph.sb("bound", [P, P])
        qk_ps, s_ps, kn_ps, grow_ps = ph.ps("qk_ps"), ph.ps("s_ps"), ph.ps("kn_ps"), ph.ps("grow_ps")
        v_ps = [ph.ps(f"v_ps{r}") for r in range(2)]
        mix_ps = [ph.ps(f"mix_ps{r}") for r in range(2)]
        y_stored = ph.sems("y_stored0", "y_stored1")
        row_loaded = ph.sems("row_loaded0", "row_loaded1")
        qk_loaded, v_loaded, decay_loaded, set_up = ph.sems("qk_loaded", "v_loaded", "decay_loaded", "set_up")
        PE_SEMS = qk_projected, v_projected, scored, k_turned, mixed, grown = ph.sems(
            "qk_projected", "v_projected", "scored", "k_turned", "mixed", "grown")
        ACT_SEMS = (wqk_rounded, wv_rounded, q_rounded, k_rounded, k_copied, v_rounded, og_tanh, weighed,
                    s_rounded, kw_rounded, state_rounded) = ph.sems(
            "wqk_rounded", "wv_rounded", "q_rounded", "k_rounded", "k_copied", "v_rounded", "og_tanh", "weighed",
            "s_rounded", "kw_rounded", "state_rounded")
        DVE_SEMS = (wv_split_dve, col_copied, qk_split, v_split, bounded, z_gated, gated, scaled, s_split, k_weighed,
                    kw_split, grown_state, state_split, summed, den_abs, den_max, inverted, y_made) = ph.sems(
            "wv_split_dve", "col_copied", "qk_split", "v_split", "bounded", "z_gated", "gated", "scaled", "s_split",
            "k_weighed", "kw_split", "grown_state", "state_split", "summed", "den_abs", "den_max", "inverted",
            "y_made")
        POOL_SEMS = wqk_split, wv_split_pool = ph.sems("wqk_split", "wv_split_pool")
        waits_met_pe, waits_met_sp = ph.sems("waits_met_pe", "waits_met_sp")
        block = ph.block()

        def before(count, b):
            return PRE + count + (b if b == 0 else b - 1)

        def tile_used(i, t):
            return PRE + 17 * i + (15, 0, 3, 6, 9, 12)[t]

        def in_tile(b):
            c = start(b) - tile_cols(b // 3)[0]
            return slice(c, c + length(b))

        @block.sync
        def _(sp):
            for sem in y_stored:
                sp.sem_inc(sem, 16)

            def load_weights(unit, head):
                sp.wait_ge(wqk_split, PRE + unit)
                sp.sem_inc(waits_met_sp, 1)
                load_qk_weights(sp, raw_qk, w_in, head, qk_loaded)
                sp.wait_ge(wv_split_pool, PRE + 2 * unit)
                sp.wait_ge(wv_split_dve, PRE + 2 * unit)
                sp.sem_inc(waits_met_sp, 1)
                load_v_weights(sp, raw_v, w_in, head, v_loaded)

            def load_row(i, t):
                a, z = tile_cols(t)
                sp.wait_ge(bounded, PRE + 17 * i + (-2, 0, 3, 6, 9, 12)[t])
                sp.sem_inc(waits_met_sp, 1)
                sp.dma_start(row[t % 2][:, :z - a],
                             row_a[bass.ds(i * T + a, z - a)].partition_broadcast(P)).then_inc(row_loaded[t % 2], 16)

            sp.sem_inc(qk_loaded, 32)
            sp.sem_inc(v_loaded, 48)
            with sp.Fori(0, B_HEADS) as i:
                load_row(i, 0)
                sp.wait_ge(grown_state, PRE + 16 * i)
                sp.sem_inc(waits_met_sp, 1)
                sp.dma_start(decay[:, :], row_dec[bass.ds(i * NB, NB)].partition_broadcast(B_QK)
                             ).then_inc(decay_loaded, 16)
                load_row(i, 1)
                load_weights(i + 1, (i + 1) % B_HEADS)
                for s in range(20):
                    if s in (3, 6, 9, 12):
                        load_row(i, s // 3 + 1)
                    b = s - 3
                    if b >= 0:
                        sp.wait_ge(y_made, PRE + 17 * i + b + 1)
                        sp.dma_start(y_out[start(b):start(b) + length(b), bass.ds(i * P, P)],
                                     y[b % 2][:length(b), :]).then_inc(y_stored[b % 2], 16)
            sp.wait_ge(y_stored[0], 16 * (1 + 9 * B_HEADS))
            sp.wait_ge(y_stored[1], 16 * (1 + 8 * B_HEADS))

        @block.gpsimd
        def _(pool):
            for sem in POOL_SEMS:
                pool.sem_inc(sem, PRE)
            for r in range(2):
                pool.memset(v_h[r][:, :].bitcast(F32), 0.0)
                pool.memset(v_l[r][:, :].bitcast(F32), 0.0).then_inc(set_up, 1)
            pool.memset(bound[:, :], 0.0).then_inc(set_up, 1)
            pool.wait_ge(set_up, 3)
            for r in range(2):
                pool.memset(v_h[r][:, B_V:B_V + 1].bitcast(F32), 1.0)
            pool.affine_select(out=bound[:, :], in_=bound[:, :], compare_op=ALU.is_ge, fill=MASKED, base=0,
                               pattern=[[1, P]], channel_multiplier=-1).then_inc(set_up, 1)

            def split_qk(unit):
                pool.wait_ge(wqk_rounded, PRE + unit + 1)
                pool.tensor_tensor(wqk_l[:, :, :], raw_qk[:, :, :], wqk_h[:, :, :].bitcast(F32),
                                   ALU.subtract).then_inc(wqk_split, 1)

            def split_v(unit):
                for n, ks in ((2, slice(2, 4)), (4, slice(6, 8))):
                    pool.wait_ge(wv_rounded, PRE + 4 * unit + n)
                    pool.tensor_tensor(wv_l[:, ks, :], raw_v[:, ks, :], wv_h[:, ks, :].bitcast(F32),
                                       ALU.subtract).then_inc(wv_split_pool, 1)

            pool.sem_inc(wqk_split, 1)
            split_v(0)
            with pool.Fori(0, B_HEADS) as i:
                split_qk(i + 1)
                split_v(i + 1)

        @block.scalar
        def _(act):
            for sem in ACT_SEMS:
                act.sem_inc(sem, PRE)

            def round_qk_weights(unit):
                act.wait_ge(qk_loaded, 32 * (unit + 1))
                act.wait_ge(qk_projected, PRE + 6 * unit)
                act.activation(wqk_h[:, :, :], raw_qk[:, :, :], ACT.Copy).then_inc(wqk_rounded, 1)

            def round_v_weights(unit, pieces):
                act.wait_ge(v_loaded, 48 * (unit + 1))
                act.wait_ge(v_projected, PRE + 17 * unit)
                for n in pieces:
                    ks = slice(2 * n, 2 * n + 2)
                    act.activation(wv_h[:, ks, :], raw_v[:, ks, :], ACT.Copy).then_inc(wv_rounded, 1)

            def round_qk(i, t, m):
                w, r = tile_cols(t)[1] - tile_cols(t)[0], t % 2
                act.wait_ge(qk_projected, PRE + m + 1)
                if i is not None:
                    act.wait_ge(mixed, tile_used(i, t))
                act.activation(q_h[r][:, :w], qk_ps[:B_QK, :w], ACT.Copy)
                act.activation(k_f[r][:, :w], qk_ps[B_QK:, :w], ACT.Copy, scale=B_QK ** -0.5).then_inc(k_copied, 1)
                act.wait_ge(k_copied, PRE + m + 1)
                act.activation(k_h[r][:, :w], k_f[r][:, :w], ACT.Copy).then_inc(k_rounded, 1)

            act.sem_inc(wqk_rounded, 1)
            round_v_weights(0, range(4))
            act.wait_ge(set_up, 4)
            round_qk(None, 0, 0)
            with act.Fori(0, B_HEADS) as i:
                for s in range(18):
                    r, m = s % 2, length(s)
                    if s >= 2:
                        act.wait_ge(grown_state, PRE + 16 * i + s - 1)
                        act.wait_ge(mixed, PRE + 17 * i + s - 1)
                        act.activation(state_h[:, :], state[:, :], ACT.Copy).then_inc(state_rounded, 1)
                    if s < NB:
                        act.wait_ge(v_projected, PRE + 17 * i + s + 1)
                        act.wait_ge(mixed, before(17 * i, s))
                        act.wait_ge(grown, before(16 * i, s))
                        act.activation(v_h[r][:m, :B_V], v_ps[r][:m, :B_V], ACT.Copy).then_inc(v_rounded, 1)
                        act.wait_ge(y_made, before(17 * i, s))
                        o, z = v_ps[r][:m, B_V:2 * B_V], v_ps[r][:m, 2 * B_V:3 * B_V]
                        act.activation(o, o, ACT.Tanh, scale=0.5)
                        act.activation(gate[r][:m, :], z, ACT.Tanh, scale=0.5).then_inc(og_tanh, 1)
                        act.wait_ge(bounded, PRE + 17 * i + s + 1)
                        act.activation(weight[:m, :m], weight[:m, :m], ACT.Exp).then_inc(weighed, 1)
                    if s < NB:
                        act.wait_ge(scaled, PRE + 17 * i + s + 1)
                        act.activation(s_h[r][:m, :m], score[:m, :m], ACT.Copy).then_inc(s_rounded, 1)
                    if s < NB - 1:
                        act.wait_ge(k_weighed, PRE + 16 * i + s + 1)
                        act.activation(kw_h[r][:m, :], k_w[:m, :], ACT.Copy).then_inc(kw_rounded, 1)
                    if s >= 16:
                        round_v_weights(i + 1, (0, 1) if s == 16 else (2, 3))
                    if s % 3 == 2:
                        round_qk(i, (s // 3 + 1) % 6, 6 * i + s // 3 + 1)
                    if s == 14:
                        round_qk_weights(i + 1)

        @block.vector
        def _(dve):
            for sem in DVE_SEMS:
                dve.sem_inc(sem, PRE)

            def split_v_weights(unit, piece):
                ks = slice(2 * piece, 2 * piece + 2)
                dve.wait_ge(wv_rounded, PRE + 4 * unit + piece + 1)
                dve.tensor_tensor(wv_l[:, ks, :], raw_v[:, ks, :], wv_h[:, ks, :].bitcast(F32),
                                  ALU.subtract).then_inc(wv_split_dve, 1)

            def split_qk(t, m):
                w, r = tile_cols(t)[1] - tile_cols(t)[0], t % 2
                dve.wait_ge(k_rounded, PRE + m + 1)
                dve.tensor_tensor(q_l[r][:, :w], qk_ps[:B_QK, :w], q_h[r][:, :w].bitcast(F32), ALU.subtract)
                dve.scalar_tensor_tensor(out=k_l[r][:, :w], in0=qk_ps[B_QK:, :w], scalar=B_QK ** -0.5,
                                         in1=k_h[r][:, :w].bitcast(F32), op0=ALU.mult,
                                         op1=ALU.subtract).then_inc(qk_split, 1)

            def grow(i, b):
                dve.wait_ge(grown, PRE + 16 * i + b + 1)
                dve.wait_ge(state_split, PRE + 16 * i + b)
                if b == 0:
                    ins = dve.tensor_copy(state[:, :], grow_ps[:B_QK, :VW])
                else:
                    dve.wait_ge(grown_state, PRE + 16 * i + b)
                    ins = dve.scalar_tensor_tensor(out=state[:, :], in0=state[:, :], scalar=decay[:, b:b + 1],
                                                   in1=grow_ps[:B_QK, :VW], op0=ALU.mult, op1=ALU.add)
                ins.then_inc(grown_state, 1)

            def split_state(i, b):
                dve.wait_ge(state_rounded, PRE + 16 * i + b + 1)
                dve.tensor_tensor(state_l[:, :], state[:, :], state_h[:, :].bitcast(F32),
                                  ALU.subtract).then_inc(state_split, 1)

            def make_y(i, b):
                m, r = length(b), b % 2
                n = 17 * i + b
                dve.wait_ge(mixed, PRE + n + 1)
                dve.wait_ge(y_made, PRE + n)
                if b == 0:
                    ins = dve.tensor_copy(mix[:m, :B_V + 1], mix_ps[r][:m, :B_V + 1])
                else:
                    ins = dve.tensor_scalar(mix[:m, :B_V + 1], mix_ps[r][:m, 256:256 + B_V + 1],
                                            col[:m, 1, b:b + 1], None, ALU.mult)
                ins.then_inc(summed, 1)
                dve.wait_ge(summed, PRE + 2 * n + 1)
                if b == 0:
                    dve.sem_inc(summed, 1)
                else:
                    dve.tensor_tensor(mix[:m, :B_V + 1], mix[:m, :B_V + 1], mix_ps[r][:m, :B_V + 1],
                                      ALU.add).then_inc(summed, 1)
                dve.wait_ge(summed, PRE + 2 * n + 2)
                dve.scalar_tensor_tensor(out=den[:m, 0:1], in0=mix[:m, B_V:B_V + 1], scalar=-1.0,
                                         in1=mix[:m, B_V:B_V + 1], op0=ALU.mult, op1=ALU.max).then_inc(den_abs, 1)
                dve.wait_ge(den_abs, PRE + n + 1)
                dve.tensor_scalar(den[:m, 1:2], den[:m, 0:1], col[:m, 2, b:b + 1], 4.0, ALU.max,
                                  ALU.mult).then_inc(den_max, 1)
                dve.wait_ge(den_max, PRE + n + 1)
                dve.reciprocal(den[:m, 2:3], den[:m, 1:2]).then_inc(inverted, 1)
                dve.wait_ge(inverted, PRE + n + 1)
                dve.wait_ge(y_stored[r], 16 * (1 + (9 - r) * i + b // 2))
                dve.scalar_tensor_tensor(out=y[r][:m, :], in0=mix[:m, :B_V], scalar=den[:m, 2:3],
                                         in1=gate[r][:m, :], op0=ALU.mult, op1=ALU.mult).then_inc(y_made, 1)

            split_v_weights(0, 0)
            split_v_weights(0, 2)
            dve.wait_ge(set_up, 4)
            split_qk(0, 0)
            with dve.Fori(0, B_HEADS) as i:
                for s in range(19):
                    r, m, n = s % 2, length(s), 17 * i + s
                    if s < NB:
                        if s == 0:
                            dve.wait_ge(y_made, PRE + 17 * i)
                            dve.tensor_copy(col[:, :, :], head_cols[:, :, :, bass.ds(i, 1)].rearrange(
                                "p q b o -> p q (b o)")).then_inc(col_copied, 1)
                            dve.wait_ge(col_copied, PRE + i + 1)
                        if s % 3 == 0:
                            t = s // 3
                            dve.wait_ge(row_loaded[t % 2], 16 * (3 * i + t // 2 + 1))
                        dve.wait_ge(scaled, PRE + n)
                        dve.wait_ge(k_weighed, PRE + 16 * i + min(s, 16))
                        dve.scalar_tensor_tensor(out=weight[:m, :m], in0=row[(s // 3) % 2][:m, in_tile(s)],
                                                 scalar=col[:m, 0, s:s + 1], in1=bound[:m, :m],
                                                 op0=ALU.add, op1=ALU.min).then_inc(bounded, 1)
                    if s == 2:
                        dve.wait_ge(decay_loaded, 16 * (i + 1))
                    if 0 <= s - 2 < NB - 1:
                        grow(i, s - 2)
                    if s == 17:
                        split_state(i, s - 2)
                        split_v_weights(i + 1, 2)
                    if 0 <= s - 2 < NB:
                        make_y(i, s - 2)
                    if 2 <= s < 17:
                        split_state(i, s - 2)
                    if s < NB:
                        dve.wait_ge(og_tanh, PRE + n + 1)
                        dve.wait_ge(mixed, before(17 * i, s))
                        dve.wait_ge(grown, before(16 * i, s))
                        dve.tensor_tensor(v_l[r][:m, :B_V], v_ps[r][:m, :B_V], v_h[r][:m, :B_V].bitcast(F32),
                                          ALU.subtract).then_inc(v_split, 1)
                        dve.scalar_tensor_tensor(out=gate[r][:m, :], in0=gate[r][:m, :], scalar=1.0,
                                                 in1=v_ps[r][:m, 2 * P:3 * P], op0=ALU.add,
                                                 op1=ALU.mult).then_inc(z_gated, 1)
                        dve.wait_ge(z_gated, PRE + n + 1)
                        dve.scalar_tensor_tensor(out=gate[r][:m, :], in0=v_ps[r][:m, P:2 * P], scalar=1.0,
                                                 in1=gate[r][:m, :], op0=ALU.add, op1=ALU.mult).then_inc(gated, 1)
                        dve.wait_ge(weighed, PRE + n + 1)
                        dve.wait_ge(scored, PRE + n + 1)
                        dve.wait_ge(s_split, PRE + n)
                        dve.tensor_tensor(score[:m, :m], s_ps[:m, :m], weight[:m, :m], ALU.mult
                                          ).then_inc(scaled, 1)
                    if s < NB - 1:
                        dve.wait_ge(k_turned, PRE + 16 * i + s + 1)
                        dve.wait_ge(kw_split, PRE + 16 * i + s)
                        dve.tensor_scalar(k_w[:m, :], kn_ps[:m, :B_QK], weight[:m, m - 1:m], None,
                                          ALU.mult).then_inc(k_weighed, 1)
                    if s < NB:
                        dve.wait_ge(s_rounded, PRE + n + 1)
                        dve.tensor_tensor(s_l[r][:m, :m], score[:m, :m], s_h[r][:m, :m].bitcast(F32),
                                          ALU.subtract).then_inc(s_split, 1)
                    if s < NB - 1:
                        dve.wait_ge(kw_rounded, PRE + 16 * i + s + 1)
                        dve.tensor_tensor(kw_l[r][:m, :], k_w[:m, :], kw_h[r][:m, :].bitcast(F32),
                                          ALU.subtract).then_inc(kw_split, 1)
                    if s % 3 == 2:
                        split_qk((s // 3 + 1) % 6, 6 * i + s // 3 + 1)
                    if s == 16:
                        split_v_weights(i + 1, 0)

        @block.tensor
        def _(pe):
            for sem in PE_SEMS:
                pe.sem_inc(sem, PRE)

            def project_qk(m, t, ks):
                a, z = tile_cols(t)
                if ks[0] == 0:
                    pe.wait_ge(qk_split, PRE + m)
                for k in ks:
                    last = product(pe, qk_ps[:, :z - a], wqk_h[:, k, :], wqk_l[:, k, :], u_h[:, k, a:z],
                                   u_l[:, k, a:z], k == 0, k == KT - 1)
                if ks[-1] == KT - 1:
                    last.then_inc(qk_projected, 1)

            def project_v(i, b):
                m, r = length(b), b % 2
                c = slice(start(b), start(b) + m)
                pe.wait_ge(gated, before(17 * i, b))
                for k in range(KT):
                    if b == 0 and k % 2 == 0:
                        split, n = (wv_split_dve, wv_split_pool)[k // 2 % 2], k // 4 + 1
                        pe.wait_ge(split, PRE + 2 * i + n)
                    last = product(pe, v_ps[r][:m, :3 * P], u_h[:, k, c], u_l[:, k, c], wv_h[:, k, :], wv_l[:, k, :],
                                   k == 0, k == KT - 1)
                last.then_inc(v_projected, 1)

            pe.wait_ge(wqk_split, PRE + 1)
            project_qk(0, 0, range(KT))
            with pe.Fori(0, B_HEADS) as i:
                for s in range(18):
                    r, m, n = s % 2, length(s), 17 * i + s
                    if s < NB:
                        project_v(i, s)
                        if s % 3 == 0:
                            pe.wait_ge(qk_split, PRE + 6 * i + s // 3 + 1)
                        pe.wait_ge(scaled, PRE + n)
                        if s == 0:
                            pe.sem_inc(waits_met_pe, 1)
                        tr, c = (s // 3) % 2, in_tile(s)
                        product(pe, s_ps[:m, :m], k_h[tr][:, c], k_l[tr][:, c], q_h[tr][:, c], q_l[tr][:, c],
                                True, True).then_inc(scored, 1)
                    if s < NB - 1:
                        pe.wait_ge(k_weighed, PRE + 16 * i + s)
                        pe.sem_inc(waits_met_pe, 1)
                        pe.transpose(kn_ps[:m, :B_QK], k_f[tr][:, c], ident_of[tr]).then_inc(k_turned, 1)
                    if s == 16:
                        pe.wait_ge(wqk_split, PRE + i + 2)
                    ks = (range(0, 3), range(3, 6), range(6, 8)) if s < 15 else (None, range(0, 3), range(3, 8))
                    if ks[s % 3]:
                        project_qk(6 * i + s // 3 + 1, (s // 3 + 1) % 6, ks[s % 3])
                    if s > 0:
                        b, q = s - 1, 1 - r
                        m, n = length(b), n - 1
                        tr, c = (b // 3) % 2, in_tile(b)
                        pe.wait_ge(s_split, PRE + n + 1)
                        pe.wait_ge(summed, PRE + 34 * i + 2 * (b if b == 0 else b - 1))
                        if b == 0:
                            pe.sem_inc(waits_met_pe, 1)
                        last = product(pe, mix_ps[q][:m, :VW], s_h[q][:m, :m], s_l[q][:m, :m], v_h[q][:m, :],
                                       v_l[q][:m, :], True, True)
                        if b > 0:
                            pe.wait_ge(state_split, PRE + 16 * i + b)
                            last = product(pe, mix_ps[q][:m, 256:256 + VW], q_h[tr][:, c], q_l[tr][:, c],
                                           state_h[:, :], state_l[:, :], True, True)
                        last.then_inc(mixed, 1)
                        if b < NB - 1:
                            pe.wait_ge(kw_split, PRE + 16 * i + b + 1)
                            pe.wait_ge(grown_state, PRE + 16 * i + b)
                            if b == 0:
                                pe.sem_inc(waits_met_pe, 1)
                            product(pe, grow_ps[:B_QK, :VW], kw_h[q][:m, :], kw_l[q][:m, :], v_h[q][:m, :],
                                    v_l[q][:m, :], True, True).then_inc(grown, 1)


def decoder(nc, x, meta, norm_a, w_in_a, sinks_a, w_out_a, norm_b, w_in_b, b_gates_b, w_out_b, norm_f, rope_table,
            out):
    x, out = x[0], out[0]
    y_t = nc.dram_tensor("y_t", [D, T], F32).ap()
    h1 = nc.dram_tensor("h1", [T, D], F32).ap()
    y_b = nc.dram_tensor("y_b", [T, D], F32).ap()
    row_a = nc.dram_tensor("row_a", [B_HEADS * T], F32).ap()
    row_dec = nc.dram_tensor("row_dec", [B_HEADS * NB], F32).ap()
    with ExitStack() as stack:
        ident = stack.enter_context(nc.sbuf_tensor("ident", [P, P], F32))
        ident_made = stack.enter_context(nc.semaphore("ident_made"))
        with nc.Block() as block:
            @block.gpsimd
            def _(pool):
                pool.memset(ident[:, :], 0.0).then_inc(ident_made, 1)
                pool.wait_ge(ident_made, 1)
                pool.affine_select(out=ident[:, :], in_=ident[:, :], compare_op=ALU.not_equal, fill=1.0, base=0,
                                   pattern=[[-1, P]], channel_multiplier=1).then_inc(ident_made, 1)

        with ExitStack() as inner:
            u_h, u_l = (inner.enter_context(nc.sbuf_tensor(f"u0_{part}", [P, KT, T], F32R)) for part in "hl")
            weights = pair_weights(nc, inner)
            norm_in(nc, x, meta, norm_a[0], w_in_a[0], ident, u_h, u_l, weights)
            attention(nc, w_in_a[0], sinks_a[0], rope_table, ident, u_h, u_l, y_t, weights)
        with ExitStack() as inner:
            here = nc.sbuf_base
            u_l = inner.enter_context(nc.sbuf_tensor("u1_l", [P, KT, T], F32R))
            u_f = nc.alloc_sbuf_tensor_at("u1_f", [P, KT, T], F32, offset=here)
            project_out(nc, "pa", w_out_a[0], y_t,
                        lambda n: meta if isinstance(n, int) and n == 0 else x[bass.ds(P * n - P, P), :],
                        norm_b[0], ident, h1, u_f)
            u_h = inner.enter_context(nc.sbuf_tensor("u1_h", [P, KT, T], F32R))
            head_cols = inner.enter_context(nc.sbuf_tensor("head_cols", [P, 3, NB, B_HEADS], F32))
            weights = head_weights(nc, inner)
            gates(nc, u_f, w_in_b[0], b_gates_b[0], ident, u_h, u_l, head_cols, row_a, row_dec, weights)
            mlstm(nc, w_in_b[0], ident, u_h, u_l, head_cols, row_a, row_dec, y_b, weights)
        project_out(nc, "pb", w_out_b[0], y_b, lambda n: h1[bass.ds(P * n + META, P), :], norm_f, ident, out)


def rope_constants():
    import numpy as np
    half = A_HD // 2
    inv = np.float32(10000.0) ** (-np.arange(half, dtype=np.float32) / np.float32(half))
    angle = (np.arange(T, dtype=np.float32)[None, :] * inv[:, None].astype(np.float32)).astype(np.float32)
    table = np.empty((P // half, half, 2, T), np.float32)
    table[:, :, 0] = np.cos(angle)
    table[0::2, :, 1] = -np.sin(angle)
    table[1::2, :, 1] = np.sin(angle)
    return table.reshape(P, 2, T)


_INS = ["x", "meta", "norm_a", "w_in_a", "sinks_a", "w_out_a", "norm_b", "w_in_b", "b_gates_b", "w_out_b", "norm_f"]


def kernel(**inputs):
    import numpy as np
    from concourse import bacc
    from concourse.bass_utils import run_bass_kernel_spmd

    nc = bacc.Bacc("TRN2", target_bir_lowering=False, num_devices=1)
    arrays = {f"in_{name}": np.ascontiguousarray(inputs[name]) for name in _INS}
    arrays["in_rope"] = rope_constants()
    args = [nc.dram_tensor(name, a.shape, mybir.dt.from_np(a.dtype), kind="ExternalInput").ap()
            for name, a in arrays.items()]
    args.append(nc.dram_tensor("out_dram", (1, SEQ, D), F32, kind="ExternalOutput").ap())
    decoder(nc, *args)
    return run_bass_kernel_spmd(nc, [arrays], core_ids=[0]).results[0]["out_dram"]
```
